# Optimizing a Trainium2 kernel written in Bass

```python
import jax, jax.numpy as jnp
from jax import lax
import numpy as np
import math

D_MODEL = 1024
BATCH = 1
SEQ = 256
DEPTH = 2

N_MIXERS = 2
N_LAYERS_A = (DEPTH + 1) // 2
N_LAYERS_B = DEPTH // 2
FOX_HEADS = 16
FOX_HEAD_DIM = D_MODEL // FOX_HEADS
Q_BLOCK = 128
FOX_IN = 4 * D_MODEL + FOX_HEADS
RET_HEADS = 4
RET_QK_DIM = D_MODEL // RET_HEADS
RET_V_DIM = 2 * D_MODEL // RET_HEADS
RET_CHUNK = 128
RET_IN = 2 * RET_HEADS * RET_QK_DIM + 2 * RET_HEADS * RET_V_DIM
N_GROUPS = 4
EXPERTS_PER_GROUP = 8
N_EXPERTS = N_GROUPS * EXPERTS_PER_GROUP
TOP_K = 2
EXPERT_FF = D_MODEL // 2
MOE_BLOCK = 128

EPS = 1e-6
NEG_INF = -1e30
ROPE_BASE = 10000.0


F32 = jnp.float32

def rms_norm(x, g):
    xf = x.astype(F32)
    y = xf * lax.rsqrt(jnp.mean(xf * xf, axis=-1, keepdims=True) + EPS)
    return (y * g.astype(F32)).astype(x.dtype)

def forgetting_attention(h, w_in, b_f, w_out):
    B, S, _ = h.shape
    H, dh = FOX_HEADS, FOX_HEAD_DIM
    proj = h @ w_in
    q, k, v, gate = jnp.split(proj[..., :4 * D_MODEL], 4, axis=-1)
    f_logit = (proj[..., 4 * D_MODEL:] + b_f).astype(F32)
    cum = jnp.cumsum(jax.nn.log_sigmoid(f_logit), axis=1).transpose(0, 2, 1)
    heads = lambda t: t.reshape(B, S, H, dh).transpose(0, 2, 1, 3)
    q, k, v = heads(q), heads(k), heads(v)
    scale = dh ** -0.5
    k_pos = jnp.arange(S)

    def query_block(i):
        start = i * Q_BLOCK
        q_b = lax.dynamic_slice_in_dim(q, start, Q_BLOCK, axis=2)
        c_b = lax.dynamic_slice_in_dim(cum, start, Q_BLOCK, axis=2)
        s = jnp.einsum('bhqd,bhkd->bhqk', q_b, k).astype(F32) * scale
        s = s + c_b[..., :, None] - cum[..., None, :]
        q_pos = start + jnp.arange(Q_BLOCK)
        s = jnp.where(k_pos[None, :] <= q_pos[:, None], s, NEG_INF)
        p = jax.nn.softmax(s, axis=-1)
        return jnp.einsum('bhqk,bhkd->bhqd', p.astype(v.dtype), v)

    o = lax.map(query_block, jnp.arange(S // Q_BLOCK))
    o = o.transpose(1, 0, 3, 2, 4).reshape(B, S, D_MODEL)
    o = o * jax.nn.sigmoid(gate)
    return o @ w_out

def rotary(t, pos):
    d = t.shape[-1]
    inv = 1.0 / (ROPE_BASE ** jnp.linspace(0.0, 1.0, d // 2, dtype=F32))
    ang = pos.astype(F32)[:, None] * inv[None, :]
    cos, sin = jnp.cos(ang), jnp.sin(ang)
    t1, t2 = t[..., :d // 2].astype(F32), t[..., d // 2:].astype(F32)
    return jnp.concatenate([t1 * cos - t2 * sin, t1 * sin + t2 * cos], axis=-1)

def retention(h, w_in, gn_gain, w_out):
    B, S, _ = h.shape
    H, dk, dv, C = RET_HEADS, RET_QK_DIM, RET_V_DIM, RET_CHUNK
    proj = h @ w_in
    q, k, v, gate = jnp.split(proj, [H * dk, 2 * H * dk, 2 * H * dk + H * dv], axis=-1)
    heads = lambda t, d: t.reshape(B, S, H, d).transpose(0, 2, 1, 3)
    pos = jnp.arange(S)
    q = rotary(heads(q, dk), pos)
    k = rotary(heads(k, dk), pos) * (dk ** -0.5)
    v = heads(v, dv).astype(F32)

    log_g = jnp.log(1.0 - 2.0 ** (-5.0 - jnp.arange(H, dtype=F32)))
    idx = jnp.arange(C, dtype=F32)
    rel = idx[:, None] - idx[None, :]
    intra = jnp.where(rel >= 0, jnp.exp(log_g[:, None, None] * jnp.maximum(rel, 0.0)), 0.0)
    q_decay = jnp.exp(log_g[:, None] * (idx + 1.0))[None, :, :, None]
    k_decay = jnp.exp(log_g[:, None] * (C - 1.0 - idx))[None, :, :, None]
    chunk_decay = jnp.exp(log_g * C)[None, :, None, None]

    n_chunks = S // C
    to_chunks = lambda t: t.reshape(B, H, n_chunks, C, t.shape[-1]).transpose(2, 0, 1, 3, 4)

    def step(R, qkv):
        q_n, k_n, v_n = qkv
        s = jnp.einsum('bhid,bhjd->bhij', q_n, k_n) * intra
        o = jnp.einsum('bhij,bhje->bhie', s, v_n)
        o = o + jnp.einsum('bhid,bhde->bhie', q_n, R) * q_decay
        R = R * chunk_decay + jnp.einsum('bhjd,bhje->bhde', k_n * k_decay, v_n)
        return R, o

    R0 = jnp.zeros((B, H, dk, dv), F32)
    _, o = lax.scan(step, R0, (to_chunks(q), to_chunks(k), to_chunks(v)))
    o = o.transpose(1, 0, 3, 2, 4).reshape(B, S, H, dv)
    mu = jnp.mean(o, axis=-1, keepdims=True)
    var = jnp.mean(jnp.square(o - mu), axis=-1, keepdims=True)
    o = ((o - mu) * lax.rsqrt(var + EPS)).reshape(B, S, H * dv) * gn_gain.astype(F32)
    o = jax.nn.silu(gate.astype(F32)) * o
    return o.astype(h.dtype) @ w_out

def grouped_experts(xf, expert_id, gates, w_gu, w_down):
    T, D = xf.shape
    A = T * TOP_K
    flat_e = expert_id.reshape(A)
    order = jnp.argsort(flat_e)
    sorted_e = flat_e[order]
    counts = jnp.bincount(flat_e, length=N_EXPERTS)
    padded = (counts + MOE_BLOCK - 1) // MOE_BLOCK * MOE_BLOCK
    pad_end = jnp.cumsum(padded)
    pad_start = pad_end - padded
    start = jnp.cumsum(counts) - counts
    dest = pad_start[sorted_e] + jnp.arange(A) - start[sorted_e]
    n_blocks = (A + N_EXPERTS * (MOE_BLOCK - 1) + MOE_BLOCK - 1) // MOE_BLOCK
    n_rows = n_blocks * MOE_BLOCK
    tok_sorted = (order // TOP_K).astype(jnp.int32)
    row_tok = jnp.full((n_rows,), T, jnp.int32).at[dest].set(tok_sorted)
    x_pad = jnp.concatenate([xf, jnp.zeros((1, D), xf.dtype)], axis=0)
    x_rows = x_pad[row_tok].reshape(n_blocks, MOE_BLOCK, D)
    block_e = jnp.minimum(jnp.searchsorted(pad_end, jnp.arange(n_blocks) * MOE_BLOCK, side='right'),
                          N_EXPERTS - 1)

    def expert_block(args):
        xb, e = args
        a, b = jnp.split(xb @ w_gu[e], 2, axis=-1)
        return (jax.nn.silu(a) * b) @ w_down[e]

    y_rows = lax.map(expert_block, (x_rows, block_e)).reshape(n_rows, D)
    w_sorted = gates.reshape(A)[order].astype(y_rows.dtype)
    return jax.ops.segment_sum(y_rows[dest] * w_sorted[:, None], tok_sorted, num_segments=T)

def hier_moe(h, wr_g, br_g, wr_e, br_e, w_gu, w_down):
    B, S, D = h.shape
    T = B * S
    xf = h.reshape(T, D)
    p_group = jax.nn.softmax((xf @ wr_g).astype(F32) + br_g.astype(F32), axis=-1)
    pg, gi = lax.top_k(p_group, 1)
    e_logits = ((xf @ wr_e).astype(F32) + br_e.astype(F32)).reshape(T, N_GROUPS, EXPERTS_PER_GROUP)
    e_in = jnp.einsum('tge,tg->te', e_logits, jax.nn.one_hot(gi[:, 0], N_GROUPS, dtype=F32))
    pv, pi = lax.top_k(jax.nn.softmax(e_in, axis=-1), TOP_K)
    gates = pg * pv / jnp.sum(pv, axis=-1, keepdims=True)
    expert_id = gi * EXPERTS_PER_GROUP + pi
    return grouped_experts(xf, expert_id, gates, w_gu, w_down).reshape(B, S, D)

def first_inputs(seed: int = 0) -> dict:
    key = jax.random.key(seed)
    ks = jax.random.split(key, 17)
    nrm = lambda k, shape, fan_in: jax.random.normal(k, shape, F32) * (fan_in ** -0.5)
    out_scale = (2.0 * DEPTH) ** -0.5
    return {
        "x": jax.random.normal(ks[0], (BATCH, SEQ, D_MODEL), F32),
        "fox_w_in": nrm(ks[1], (N_LAYERS_A, D_MODEL, FOX_IN), D_MODEL),
        "fox_b_f": 3.0 + 0.5 * jax.random.normal(ks[2], (N_LAYERS_A, FOX_HEADS), F32),
        "fox_w_out": nrm(ks[3], (N_LAYERS_A, D_MODEL, D_MODEL), D_MODEL) * out_scale,
        "ret_w_in": nrm(ks[4], (N_LAYERS_B, D_MODEL, RET_IN), D_MODEL),
        "ret_gn_gain": 1.0 + 0.02 * jax.random.normal(ks[5], (N_LAYERS_B, RET_HEADS * RET_V_DIM), F32),
        "ret_w_out": nrm(ks[6], (N_LAYERS_B, RET_HEADS * RET_V_DIM, D_MODEL), RET_HEADS * RET_V_DIM) * out_scale,
        "norm_mix": 1.0 + 0.02 * jax.random.normal(ks[7], (DEPTH, D_MODEL), F32),
        "norm_ffn": 1.0 + 0.02 * jax.random.normal(ks[8], (DEPTH, D_MODEL), F32),
        "router_group_w": nrm(ks[9], (DEPTH, D_MODEL, N_GROUPS), D_MODEL),
        "router_group_b": 0.01 * jax.random.normal(ks[10], (DEPTH, N_GROUPS), F32),
        "router_expert_w": nrm(ks[11], (DEPTH, D_MODEL, N_EXPERTS), D_MODEL),
        "router_expert_b": 0.01 * jax.random.normal(ks[12], (DEPTH, N_EXPERTS), F32),
        "expert_w_gu": nrm(ks[13], (DEPTH, N_EXPERTS, D_MODEL, 2 * EXPERT_FF), D_MODEL),
        "expert_w_down": nrm(ks[14], (DEPTH, N_EXPERTS, EXPERT_FF, D_MODEL), EXPERT_FF) * out_scale,
        "norm_final": 1.0 + 0.02 * jax.random.normal(ks[15], (D_MODEL,), F32),
    }

def first_block(x, fox_w_in, fox_b_f, fox_w_out, ret_w_in, ret_gn_gain, ret_w_out,
              norm_mix, norm_ffn, router_group_w, router_group_b, router_expert_w,
              router_expert_b, expert_w_gu, expert_w_down, norm_final):
    h = x
    for i in range(DEPTH):
        hn = rms_norm(h, norm_mix[i])
        j = i // N_MIXERS
        if i % N_MIXERS == 0:
            h = h + forgetting_attention(hn, fox_w_in[j], fox_b_f[j], fox_w_out[j])
        else:
            h = h + retention(hn, ret_w_in[j], ret_gn_gain[j], ret_w_out[j])
        hn = rms_norm(h, norm_ffn[i])
        h = h + hier_moe(hn, router_group_w[i], router_group_b[i], router_expert_w[i],
                         router_expert_b[i], expert_w_gu[i], expert_w_down[i])
    return rms_norm(h, norm_final)


CTX_LEN = 256
GRID_W = 64

MLSTM_HEADS = 4
MLSTM_HEAD_DIM = D_MODEL // 8
MLSTM_WIDTH = MLSTM_HEADS * MLSTM_HEAD_DIM
MLSTM_CHUNK = 128
FORGET_BIAS = 4.0
SGU_GROUPS = 4
SGU_WIDTH = D_MODEL // 4
SGU_CHUNK = 128
CONV_WIDTH = D_MODEL // 4
CONV_K = 31

MIX_WIDTH = MLSTM_WIDTH + SGU_WIDTH + CONV_WIDTH
FFN_HIDDEN = int(math.ceil(8 * D_MODEL / 3 / 256)) * 256

Q_OFF = 0
K_OFF = MLSTM_WIDTH
V_OFF = 2 * MLSTM_WIDTH
O_OFF = 3 * MLSTM_WIDTH
GATE_OFF = 4 * MLSTM_WIDTH
SGU_OFF = GATE_OFF + 4 * MLSTM_HEADS
CONV_OFF = SGU_OFF + 2 * SGU_WIDTH
IN_COLS = CONV_OFF + 2 * CONV_WIDTH


def rmsnorm(t, g):
    t32 = t.astype(jnp.float32)
    y = t32 * lax.rsqrt(jnp.mean(t32 * t32, axis=-1, keepdims=True) + EPS)
    return (y * g).astype(t.dtype)

def layernorm(t, g, b):
    t32 = t.astype(jnp.float32)
    mu = jnp.mean(t32, axis=-1, keepdims=True)
    d = t32 - mu
    var = jnp.mean(d * d, axis=-1, keepdims=True)
    return (d * lax.rsqrt(var + EPS) * g + b).astype(t.dtype)

def swiglu(h, w_gu, w_down):
    gate, up = jnp.split(h @ w_gu, 2, axis=-1)
    return (jax.nn.silu(gate) * up) @ w_down

def mlstm_inputs(p):
    B, L, _ = p.shape
    def heads(t):
        return t.reshape(B, L, MLSTM_HEADS, MLSTM_HEAD_DIM).transpose(0, 2, 1, 3).astype(jnp.float32)
    q = heads(p[..., Q_OFF:K_OFF])
    k = heads(p[..., K_OFF:V_OFF]) * (MLSTM_HEAD_DIM ** -0.5)
    v = heads(p[..., V_OFF:O_OFF])
    g = p[..., GATE_OFF:SGU_OFF].astype(jnp.float32).reshape(B, L, 4, MLSTM_HEADS).transpose(2, 0, 3, 1)
    gates = (g[0], jax.nn.log_sigmoid(g[1]), g[2], jax.nn.log_sigmoid(g[3]))
    return q, k, v, gates

def zero_state(batch):
    return (jnp.zeros((batch, MLSTM_HEADS, MLSTM_HEAD_DIM, MLSTM_HEAD_DIM), jnp.float32),
            jnp.zeros((batch, MLSTM_HEADS, MLSTM_HEAD_DIM), jnp.float32),
            jnp.zeros((batch, MLSTM_HEADS), jnp.float32))

def mlstm_scan(q, k, v, logi, logf, state, with_output):
    B, H, L, d = q.shape
    nc = L // MLSTM_CHUNK
    def to_chunks(t):
        t = t.reshape((B, H, nc, MLSTM_CHUNK) + t.shape[3:])
        return jnp.moveaxis(t, 2, 0)
    xs = tuple(to_chunks(t) for t in (q, k, v, logi, logf))
    order = jnp.tril(jnp.ones((MLSTM_CHUNK, MLSTM_CHUNK), bool))

    def step(carry, inp):
        C, n, m = carry
        qc, kc, vc, ic, fc = inp
        b = jnp.cumsum(fc, axis=-1)
        b_last = b[..., -1]
        w_log = b_last[..., None] - b + ic
        m_new = jnp.maximum(b_last + m, jnp.max(w_log, axis=-1))
        decay = jnp.exp(b_last + m - m_new)
        ks = kc * jnp.exp(w_log - m_new[..., None])[..., None]
        C_new = decay[..., None, None] * C + jnp.einsum('bhsk,bhsv->bhkv', ks, vc)
        n_new = decay[..., None] * n + jnp.sum(ks, axis=2)
        if not with_output:
            return (C_new, n_new, m_new), None
        a = b + m[..., None]
        Dlog = b[..., :, None] - b[..., None, :] + ic[..., None, :]
        Dlog = jnp.where(order, Dlog, -jnp.inf)
        m_t = jnp.maximum(a, jnp.max(Dlog, axis=-1))
        w_inter = jnp.exp(a - m_t)
        s = jnp.einsum('bhtk,bhsk->bhts', qc, kc) * jnp.exp(Dlog - m_t[..., None])
        num = w_inter[..., None] * jnp.einsum('bhtk,bhkv->bhtv', qc, C) + jnp.einsum('bhts,bhsv->bhtv', s, vc)
        den = w_inter * jnp.einsum('bhtk,bhk->bht', qc, n) + jnp.sum(s, axis=-1)
        h = num / jnp.maximum(jnp.abs(den), jnp.exp(-m_t))[..., None]
        return (C_new, n_new, m_new), h

    state, hs = lax.scan(step, state, xs)
    if not with_output:
        return None, state
    h = jnp.moveaxis(hs, 0, 2).reshape(B, H, L, d)
    return h, state

def _flip(t):
    return jnp.flip(t, axis=2)

def mlstm_bidir(q, k, v, gates, init_f, init_b, with_output):
    logi_f, logf_f, logi_b, logf_b = gates
    h_f, st_f = mlstm_scan(q, k, v, logi_f, logf_f, init_f, with_output)
    h_b, st_b = mlstm_scan(_flip(q), _flip(k), _flip(v), _flip(logi_b), _flip(logf_b), init_b, with_output)
    h = h_f + _flip(h_b) if with_output else None
    return h, st_f, st_b

def mlstm_post(h, o_pre, g):
    B, H, L, d = h.shape
    h = h * lax.rsqrt(jnp.mean(h * h, axis=-1, keepdims=True) + EPS)
    h = h.transpose(0, 2, 1, 3).reshape(B, L, H * d) * g
    return (h * jax.nn.sigmoid(o_pre.astype(jnp.float32))).astype(o_pre.dtype)

def chunk_sgu(z, ln_g, ln_b, w_s, b_s):
    z = jax.nn.gelu(z)
    u, v = jnp.split(z, 2, axis=-1)
    v = layernorm(v, ln_g, ln_b)
    B, L, C = v.shape
    vg = v.reshape(B, L // SGU_CHUNK, SGU_CHUNK, SGU_GROUPS, C // SGU_GROUPS)
    mixed = jnp.einsum('gpq,bnqgc->bnpgc', w_s, vg) + b_s.T[:, :, None]
    return u * mixed.reshape(B, L, C)

def dwconv1d(y, w, b):
    kw, ch = w.shape
    out = lax.conv_general_dilated(y, w.reshape(kw, 1, ch).astype(y.dtype), window_strides=(1,),
                                   padding=[(kw // 2, kw // 2)], dimension_numbers=('NWC', 'WIO', 'NWC'),
                                   feature_group_count=ch)
    return out + b

def axial_dwconv(y, w, b):
    B, L, C = y.shape
    rows = L // GRID_W
    half = C // 2
    yr = dwconv1d(y[..., :half].reshape(B * rows, GRID_W, half), w[:, :half], b[:half]).reshape(B, L, half)
    yc = y[..., half:].reshape(B, rows, GRID_W, half).transpose(0, 2, 1, 3).reshape(B * GRID_W, rows, half)
    yc = dwconv1d(yc, w[:, half:], b[half:]).reshape(B, GRID_W, rows, half).transpose(0, 2, 1, 3).reshape(B, L, half)
    return jnp.concatenate([yr, yc], axis=-1)

def conformer_conv(z, w_dw, b_dw, ln_g, ln_b, grid):
    a, g = jnp.split(z, 2, axis=-1)
    y = a * jax.nn.sigmoid(g)
    y = axial_dwconv(y, w_dw, b_dw) if grid else dwconv1d(y, w_dw, b_dw)
    return jax.nn.silu(layernorm(y, ln_g, ln_b))

def mix_groups(p, h_mlstm, mlstm_g, sgu_ln_g, sgu_ln_b, sgu_w, sgu_b, conv_w, conv_b, conv_ln_g, conv_ln_b, grid):
    y_a = mlstm_post(h_mlstm, p[..., O_OFF:GATE_OFF], mlstm_g)
    y_b = chunk_sgu(p[..., SGU_OFF:CONV_OFF], sgu_ln_g, sgu_ln_b, sgu_w, sgu_b)
    y_c = conformer_conv(p[..., CONV_OFF:IN_COLS], conv_w, conv_b, conv_ln_g, conv_ln_b, grid)
    return jnp.concatenate([y_a, y_b, y_c], axis=-1)

def second_inputs(seed: int = 0) -> dict:
    key = jax.random.key(seed)
    ks = jax.random.split(key, 24)
    def nrm(k, shape, scale):
        return jax.random.normal(k, shape, jnp.float32) * scale
    fb = np.zeros((IN_COLS,), np.float32)
    fb[GATE_OFF + MLSTM_HEADS:GATE_OFF + 2 * MLSTM_HEADS] = FORGET_BIAS
    fb[GATE_OFF + 3 * MLSTM_HEADS:GATE_OFF + 4 * MLSTM_HEADS] = FORGET_BIAS
    return {
        'x': nrm(ks[0], (BATCH, SEQ, D_MODEL), 1.0),
        'c': nrm(ks[1], (BATCH, D_MODEL), 1.0),
        'ctx': nrm(ks[2], (BATCH, CTX_LEN, D_MODEL), 1.0),
        'c_ctx': nrm(ks[3], (D_MODEL,), 1.0),
        'w_mod': nrm(ks[4], (DEPTH, D_MODEL, 6 * D_MODEL), 0.5 * D_MODEL ** -0.5),
        'b_mod': nrm(ks[5], (DEPTH, 6 * D_MODEL), 0.02),
        'norm1_g': 1.0 + nrm(ks[6], (DEPTH, D_MODEL), 0.02),
        'w_in': nrm(ks[7], (DEPTH, D_MODEL, IN_COLS), D_MODEL ** -0.5),
        'b_in': nrm(ks[8], (DEPTH, IN_COLS), 0.02) + jnp.asarray(fb),
        'mlstm_g': 1.0 + nrm(ks[9], (DEPTH, MLSTM_WIDTH), 0.02),
        'sgu_ln_g': 1.0 + nrm(ks[10], (DEPTH, SGU_WIDTH), 0.02),
        'sgu_ln_b': nrm(ks[11], (DEPTH, SGU_WIDTH), 0.02),
        'sgu_w': nrm(ks[12], (DEPTH, SGU_GROUPS, SGU_CHUNK, SGU_CHUNK), SGU_CHUNK ** -0.5),
        'sgu_b': nrm(ks[13], (DEPTH, SGU_GROUPS, SGU_CHUNK), 0.02),
        'conv_w': nrm(ks[14], (DEPTH, CONV_K, CONV_WIDTH), CONV_K ** -0.5),
        'conv_b': nrm(ks[15], (DEPTH, CONV_WIDTH), 0.02),
        'conv_ln_g': 1.0 + nrm(ks[16], (DEPTH, CONV_WIDTH), 0.02),
        'conv_ln_b': nrm(ks[17], (DEPTH, CONV_WIDTH), 0.02),
        'w_out': nrm(ks[18], (DEPTH, MIX_WIDTH, D_MODEL), MIX_WIDTH ** -0.5),
        'norm2_g': 1.0 + nrm(ks[19], (DEPTH, D_MODEL), 0.02),
        'w_gu': nrm(ks[20], (DEPTH, D_MODEL, 2 * FFN_HIDDEN), D_MODEL ** -0.5),
        'w_down': nrm(ks[21], (DEPTH, FFN_HIDDEN, D_MODEL), FFN_HIDDEN ** -0.5),
        'final_g': 1.0 + nrm(ks[22], (D_MODEL,), 0.02),
    }

def second_block(x, c, ctx, c_ctx, w_mod, b_mod, norm1_g, w_in, b_in, mlstm_g, sgu_ln_g, sgu_ln_b, sgu_w, sgu_b,
              conv_w, conv_b, conv_ln_g, conv_ln_b, w_out, norm2_g, w_gu, w_down, final_g):
    batch = x.shape[0]
    c_act = jax.nn.silu(c)
    cc_act = jax.nn.silu(c_ctx)
    xc = ctx
    for l in range(DEPTH):
        last = l == DEPTH - 1
        mod = (c_act @ w_mod[l] + b_mod[l])[:, None, :]
        modc = cc_act @ w_mod[l] + b_mod[l]
        sh1, sc1, g1, sh2, sc2, g2 = jnp.split(mod, 6, axis=-1)
        shc1, scc1, gc1, shc2, scc2, gc2 = jnp.split(modc, 6, axis=-1)

        px = (rmsnorm(x, norm1_g[l]) * (1.0 + sc1) + sh1) @ w_in[l] + b_in[l]
        pc = (rmsnorm(xc, norm1_g[l]) * (1.0 + scc1) + shc1) @ w_in[l] + b_in[l]
        qx, kx, vx, gtx = mlstm_inputs(px)
        qc, kc, vc, gtc = mlstm_inputs(pc)
        zs = zero_state(batch)
        h_c, st_f, st_b = mlstm_bidir(qc, kc, vc, gtc, zs, zs, not last)
        h_x, _, _ = mlstm_bidir(qx, kx, vx, gtx, st_f, st_b, True)

        y_x = mix_groups(px, h_x, mlstm_g[l], sgu_ln_g[l], sgu_ln_b[l], sgu_w[l], sgu_b[l],
                         conv_w[l], conv_b[l], conv_ln_g[l], conv_ln_b[l], True)
        x = x + g1 * (y_x @ w_out[l])
        x = x + g2 * swiglu(rmsnorm(x, norm2_g[l]) * (1.0 + sc2) + sh2, w_gu[l], w_down[l])

        if not last:
            y_c = mix_groups(pc, h_c, mlstm_g[l], sgu_ln_g[l], sgu_ln_b[l], sgu_w[l], sgu_b[l],
                             conv_w[l], conv_b[l], conv_ln_g[l], conv_ln_b[l], False)
            xc = xc + gc1 * (y_c @ w_out[l])
            xc = xc + gc2 * swiglu(rmsnorm(xc, norm2_g[l]) * (1.0 + scc2) + shc2, w_gu[l], w_down[l])
    return rmsnorm(x, final_g)


def setup_inputs(seed=0):
    out = dict(first_inputs(seed))
    for name, value in second_inputs(seed + 1).items():
        if name != "x":
            out[name + "_2"] = value
    return out


def reference(
    x, fox_w_in, fox_b_f, fox_w_out, ret_w_in, ret_gn_gain, ret_w_out, norm_mix, norm_ffn,
    router_group_w, router_group_b, router_expert_w, router_expert_b, expert_w_gu,
    expert_w_down, norm_final, c_2, ctx_2, c_ctx_2, w_mod_2, b_mod_2, norm1_g_2, w_in_2, b_in_2,
    mlstm_g_2, sgu_ln_g_2, sgu_ln_b_2, sgu_w_2, sgu_b_2, conv_w_2, conv_b_2, conv_ln_g_2,
    conv_ln_b_2, w_out_2, norm2_g_2, w_gu_2, w_down_2, final_g_2,
):
    x = first_block(
        x, fox_w_in, fox_b_f, fox_w_out, ret_w_in, ret_gn_gain, ret_w_out, norm_mix, norm_ffn,
        router_group_w, router_group_b, router_expert_w, router_expert_b, expert_w_gu,
        expert_w_down, norm_final,
    )
    return second_block(
        x, c_2, ctx_2, c_ctx_2, w_mod_2, b_mod_2, norm1_g_2, w_in_2, b_in_2, mlstm_g_2,
        sgu_ln_g_2, sgu_ln_b_2, sgu_w_2, sgu_b_2, conv_w_2, conv_b_2, conv_ln_g_2, conv_ln_b_2,
        w_out_2, norm2_g_2, w_gu_2, w_down_2, final_g_2,
    )


_drawn_inputs = setup_inputs


def setup_inputs(seed=0):
    import zlib

    import numpy as np

    out = dict(_drawn_inputs(seed))
    spreads = {}
    factors = {'ret_gn_gain': 4.829,
     'norm_mix': 3.15,
     'router_group_b': 5.827,
     'router_expert_b': 5.181,
     'norm1_g_2': 5.398,
     'mlstm_g_2': 39.253,
     'sgu_ln_g_2': 8.0,
     'sgu_ln_b_2': 8.0,
     'sgu_b_2': 8.0,
     'conv_b_2': 8.0,
     'conv_ln_g_2': 50.571,
     'conv_ln_b_2': 42.326,
     'norm2_g_2': 6.537,
     'final_g_2': 8.921}
    for name, (base, spread) in spreads.items():
        noise = np.random.default_rng([zlib.crc32(name.encode()), seed]).standard_normal(out[name].shape)
        drawn = base * np.exp(spread * noise) if base else spread * noise
        out[name] = __import__('jax').numpy.asarray(drawn.astype(out[name].dtype))
    for name, factor in factors.items():
        out[name] = (out[name] * factor).astype(out[name].dtype)
    return out
```

```python
import numpy as np
import concourse.bass as bass
from concourse import mybir
from contextlib import ExitStack

F32 = mybir.dt.float32
I32 = mybir.dt.int32
ALU = mybir.AluOpType
ACT = mybir.ActivationFunctionType
AX = mybir.AxisListType
MUL, ADD, SUB, MAX, MIN = ALU.mult, ALU.add, ALU.subtract, ALU.max, ALU.min

P = 128
DM = 1024
KC = DM // P
T = 256
EPS = 1e-6
NEG = -1e30
NE = 32
NX = 7
SL = 64
FF2 = 2816

RING = 9
SLOT = 2048
ARENA = 26752

VEC = {}
_n = [0]


def _vec(name, width):
    VEC[name] = (_n[0], width)
    _n[0] += width


for _name, _w in (("norm_mix", 16), ("norm_ffn", 16), ("norm_final", 8), ("gn", 16), ("norm1", 16),
                  ("norm2", 16), ("final", 8), ("b_mod", 96), ("mlstm_g", 8), ("cln_g", 4), ("cln_b", 4),
                  ("conv_b", 4), ("conv_w", 124), ("bq", 8), ("bk", 8), ("bg", 2), ("bu", 4), ("bc", 8),
                  ("c", 8), ("cc", 8), ("bf", 1), ("cos", 256), ("sin", 256), ("dec", 1024), ("ident", 128),
                  ("mask_z", 128), ("mask_ge", 128), ("mask_le", 128), ("tri", 128), ("ones", 128), ("iota", 64), ("zero", 64),
                  ("eps", 1), ("jota", 7)):
    _vec(_name, _w)
NVEC = _n[0]
ROW = {"bv": (0, 0, 1024), "bo": (32, 0, 1024), "bs": (64, 0, 512), "br": (64, 512, 72), "sgub": (96, 0, 1024)}
NROW = 1024


class Engines:

    def __init__(self, nc, ctx):
        self.nc = nc
        self.q = {k: [] for k in "vapgs"}
        self.n = dict.fromkeys("vapgs", 0)
        self.sem = {k: ctx.enter_context(nc.semaphore(f"done_{k}")) for k in "vapgs"}
        self.seen = {}

    def put(self, k, fn, waits=(), inc=True, own=True):
        need = {}
        waits = list(waits)
        if own and self.n[k] and k in "vag":
            waits.append((self.sem[k], self.n[k]))
        for w in waits:
            if w is None:
                continue
            s, v = w
            if v > self.seen.get((k, s.name), 0):
                need[s.name] = (s, max(v, need.get(s.name, (s, 0))[1]))
        for name, (s, v) in need.items():
            self.seen[(k, name)] = v
        if inc:
            self.n[k] += 1
        self.q[k].append((list(need.values()), fn, self.sem[k] if inc else None))
        return (self.sem[k], self.n[k])

    def dma(self, k, fn, sem, value, waits=()):
        need = []
        for w in waits:
            if w is not None and w[1] > self.seen.get((k, w[0].name), 0):
                self.seen[(k, w[0].name)] = w[1]
                need.append(w)
        self.q[k].append((need, lambda e: (fn(e).then_inc(sem, 16), None)[1], None))
        return (sem, value)

    def barrier(self):
        now = [(self.sem[k], self.n[k]) for k in "vapg" if self.n[k]]
        return now

    def run(self, block):
        def body(k):
            def _(e):
                for waits, fn, sem in self.q[k]:
                    for s, v in waits:
                        e.wait_ge(s, v)
                    r = fn(e)
                    if sem is not None:
                        r.then_inc(sem, 1)
            return _
        block.sync(body("s"))
        block.gpsimd(body("g"))
        block.scalar(body("a"))
        block.vector(body("v"))
        block.tensor(body("p"))


class Turns:

    def __init__(self, items):
        self.items = items
        self.free = [[] for _ in items]
        self.at = 0

    def next(self):
        i = self.at
        self.at = (i + 1) % len(self.items)
        w, self.free[i] = self.free[i], []
        return i, self.items[i], w

    def done(self, i, *toks):
        self.free[i] = list(toks)


def build(nc, A, stop=None):
    ctx = ExitStack()
    with ctx:
        E = Engines(nc, ctx)
        put = E.put

        def sb(name, shape, dt=F32):
            return ctx.enter_context(nc.sbuf_tensor(name, shape, dt))

        def sem(name):
            return ctx.enter_context(nc.semaphore(name))

        ring = sb("ring", [P, RING, SLOT])
        xr = sb("xr", [P, KC, 2 * T])
        vec = sb("vec_sb", [P, NVEC])
        row = sb("row_sb", [P, NROW])
        ar_t = sb("arena", [P, ARENA])
        eid = sb("eid", [1, 32], I32)
        banks = [ctx.enter_context(nc.psum_tensor(f"bank{i}", [P, 512], F32)) for i in range(8)]
        ring_sem = [sem(f"ring{i}") for i in range(RING)]
        s_vec = sem("s_vec")
        s_x = sem("s_x")
        s_small = sem("s_small")
        s_out = sem("s_out")

        def mm(out, lhsT, rhs, start, stop, w=(), inc=False, tile=None, skip=False):
            return put("p", lambda e: e.matmul(out, lhsT, rhs, start=start, stop=stop, tile_position=tile,
                                               skip_group_check=skip), w, inc)

        def tr(out, in_, w=(), inc=False):
            n = in_.shape[0]
            return put("p", lambda e: e.transpose(out, in_, V("ident")[0:n, 0:n]), w, inc)

        def act(out, in_, f, w=(), bias=None, scale=1.0, accum=None):
            kw = {}
            if bias is not None:
                kw["bias"] = bias
            if accum is not None:
                kw["accum_out"] = accum
            return put("a", lambda e: e.activation(out, in_, f, scale=scale, **kw), w)

        def tt(out, a, b, op, w=(), k="v"):
            return put(k, lambda e: e.tensor_tensor(out, a, b, op), w)

        def ts(out, a, s1, s2=None, op0=MUL, op1=None, w=(), k="v"):
            if op1 is None:
                return put(k, lambda e: e.tensor_scalar(out, a, s1, None, op0), w)
            return put(k, lambda e: e.tensor_scalar(out, a, s1, s2, op0, op1), w)

        def stt(out, a, s, b, op0, op1, w=()):
            return put("v", lambda e: e.scalar_tensor_tensor(out, a, s, b, op0, op1), w)

        def cp(out, a, w=(), k="v"):
            if k == "a":
                return act(out, a, ACT.Copy, w)
            return put(k, lambda e: e.tensor_copy(out, a), w)

        def red(out, a, op, w=(), axis=AX.X):
            return put("v", lambda e: e.tensor_reduce(out, a, axis, op), w)

        def rcp(out, a, w=()):
            return put("v", lambda e: e.reciprocal(out, a), w)

        def scan(out, a, b, init, op0, op1, w=()):
            return put("v", lambda e: e.tensor_tensor_scan(out, a, b, init, op0, op1), w)

        def fill(out, value, w=(), k="v"):
            return put(k, lambda e: e.memset(out, value), w)

        def bc(ap, shape, *axes):
            for x in axes:
                ap = ap.unsqueeze(x)
            return ap.to_broadcast(shape)

        def V(name, a=0, n=None):
            o, wd = VEC[name]
            return vec[:, o + a:o + (wd if n is None else a + n)]

        def R(name, a=0, n=None):
            q, o, wd = ROW[name]
            return row[q:q + 1, o + a:o + (wd if n is None else a + n)], ones[q:q + 1, :]

        eps = V("eps")
        ones = V("ones")
        ident = V("ident")

        top = [0]
        since = [[]]

        def phase():
            top[0] = 0
            since[0] = E.barrier()
            for k in "vag":
                put(k, lambda e: e.nop(), since[0])
            put("p", lambda e: e.nop(), since[0])

        def ar(*dims):
            n = int(np.prod(dims))
            a = ar_t[:, top[0]:top[0] + n]
            top[0] += n
            assert top[0] <= ARENA, top[0]
            if len(dims) == 2:
                a = a.rearrange("p (a b) -> p a b", a=dims[0])
            if len(dims) == 3:
                a = a.rearrange("p (a b c) -> p a b c", a=dims[0], b=dims[1])
            if len(dims) == 4:
                a = a.rearrange("p (a b c d) -> p a b c d", a=dims[0], b=dims[1], c=dims[2])
            return a

        wt = {"n": 0, "free": [None] * RING, "count": [0] * RING}

        def wload(src, a, b, cond=None):
            i = wt["n"] % RING
            wt["n"] += 1
            wt["count"][i] += 1
            dst = ring[:, i, 0:a * b].rearrange("p (a b) -> p a b", a=a)
            s = src.rearrange("(a p) n -> p a n", p=P)
            tok = E.dma("s", lambda e: e.dma_start(dst, s), ring_sem[i], 16 * wt["count"][i], [wt["free"][i]])
            return i, dst, tok

        def wfree(slots, tok):
            for i, _, _ in slots:
                wt["free"][i] = tok

        pb = Turns(banks)

        def blocks(n):
            return [(o, min(512, n - o)) for o in range(0, n, 512)]

        def fetch(W, kchunks, o, nc_):
            step = 4 if nc_ > 256 else 8
            slots = [wload(W[g * P:min(g + step, kchunks) * P, o:o + nc_], min(step, kchunks - g), nc_)
                     for g in range(0, kchunks, step)]

            def at(k):
                return slots[k // step][1][:, k % step, :], slots[k // step][2]
            return slots, at

        def gemm_t(W, kchunks, N, rhs, ntok, evac, w):
            per = 512 // ntok
            for o, n in blocks(N):
                slots, at = fetch(W, kchunks, o, n)
                j = 0
                nch = n // P
                while j < nch:
                    cnt = min(per, nch - j)
                    bi, bank, bw = pb.next()
                    view = bank[:, 0:cnt * ntok].rearrange("p (a t) -> p a t", a=cnt)
                    for c in range(cnt):
                        for k in range(kchunks):
                            a, dt_ = at(k)
                            last = mm(view[:, c, :], a[:, (j + c) * P:(j + c + 1) * P], rhs(k),
                                      k == 0, k == kchunks - 1, list(w) + bw + [dt_],
                                      inc=(c == cnt - 1 and k == kchunks - 1))
                    pb.done(bi, *evac(o // P + j, cnt, view, last))
                    j += cnt
                wfree(slots, last)

        def gemm_n(W, kchunks, N, lhsT, tiles, evac, w, bias=None):
            for o, n in blocks(N):
                slots, at = fetch(W, kchunks, o, n)
                for tt_ in tiles:
                    bi, bank, bw = pb.next()
                    for k in range(kchunks):
                        a, dt_ = at(k)
                        end = k == kchunks - 1 and bias is None
                        last = mm(bank[:, 0:n], lhsT(k, tt_), a[:, 0:n], k == 0, end,
                                  list(w) + bw + [dt_], inc=end)
                    if bias is not None:
                        last = mm(bank[:, 0:n], bias[1], bias[0][:, o:o + n], False, True, inc=True)
                    pb.done(bi, *evac(tt_, o, n, bank[:, 0:n], last))
                wfree(slots, last)

        def colsum(views, ntok, w):
            bi, bank, bw = pb.next()
            for i, v in enumerate(views):
                last = mm(bank[:, 0:ntok], ones, v, i == 0, i == len(views) - 1, list(w) + bw,
                          inc=i == len(views) - 1)
            return bi, bank[:, 0:ntok], last

        def rstd_of(out, src, scale, w):
            t = act(out, src, ACT.Sqrt, w, bias=eps, scale=scale)
            return rcp(out, out, [t]), t

        def rms_t(x, ntok, out, mul, add, tmp, rs, w):
            t = act(tmp, x, ACT.Square, w)
            bi, s, tok = colsum([tmp[:, c, :] for c in range(KC)], ntok, [t])
            r, t = rstd_of(rs, s, 1.0 / DM, [tok])
            pb.done(bi, t)
            for c in range(KC):
                for lo, hi, m, a in mul:
                    t = stt(out[:, c, lo:hi], x[:, c, lo:hi], m(c), rs[:, lo:hi], MUL, MUL, [r])
                    if a is not None:
                        t = act(out[:, c, lo:hi], out[:, c, lo:hi], ACT.Identity, [t], bias=a(c))
            return [t, (E.sem["v"], E.n["v"])]

        nsm = [0]

        def small(dst, src, w=()):
            nsm[0] += 16
            return E.dma("g", lambda e: e.dma_start(dst, src), s_small, nsm[0], list(w) + since[0])

        E.dma("s", lambda e: e.dma_start(vec[:, :], A["vec"]), s_vec, 16)
        E.dma("s", lambda e: e.dma_start(row[:, :], A["row"]), s_vec, 32)
        ready = (s_vec, 32)
        for k in "vagp":
            put(k, lambda e: e.nop(), [ready])

        x = xr[:, :, T:2 * T]
        xin = ar(2, DM)
        cin = ar(2, DM)
        E.dma("s", lambda e: e.dma_start(xin, A["x"][0].rearrange("(a p) d -> p a d", p=P)), s_x, 16)
        E.dma("s", lambda e: e.dma_start(cin, A["ctx_2"][0].rearrange("(a p) d -> p a d", p=P)), s_x, 32)
        for src, dst in ((xin, x), (cin, xr[:, :, 0:T])):
            for a in range(2):
                for c in range(0, KC, 4):
                    bi, bank, bw = pb.next()
                    for j in range(4):
                        last = tr(bank[:, j * P:(j + 1) * P], src[:, a, (c + j) * P:(c + j + 1) * P],
                                  bw + [(s_x, 32)], inc=j == 3)
                    pb.done(bi, cp(dst[:, c:c + 4, a * P:(a + 1) * P],
                                   bank[:, :].rearrange("p (a t) -> p a t", a=4), [last], k="a" if c else "v"))

        def fox():
            phase()
            H, dh = 16, 64
            W = A["fox_w_in"][0]
            xt = ar(KC, T)
            tmp = ar(KC, T)
            rs = ar(T)
            qt = ar(KC, T)
            kt = ar(KC, T)
            gt = ar(KC, T)
            v = ar(2, DM)
            cum = ar(T)
            ncum = ar(T)
            wf = ar(KC, P)
            zf = fill(wf, 0.0)
            for q0 in (0, 64):
                tf = small(wf[:, :, q0:q0 + H], W[:, 4 * DM:4 * DM + H].rearrange("(a p) n -> p a n", p=P), [zf])
            g = V("norm_mix")
            xw = rms_t(x, T, xt, [(0, T, lambda c: g[:, c:c + 1], None)], None, tmp, rs, ())
            bi, bank, bw = pb.next()
            for k in range(KC):
                last = mm(bank[:, 0:T], wf[:, k, :], xt[:, k, :], k == 0, k == KC - 1, xw + bw + [tf],
                          inc=k == KC - 1)
            z = ts(ncum[:, :], bank[:, 0:T], V("bf")[:, :], op0=ADD, w=[last])
            pb.done(bi, z)
            z = stt(cum[:, :], ncum[:, :], -1.0, ncum[:, :], MUL, MAX, [z])
            z = act(cum[:, :], cum[:, :], ACT.Exp, [z], scale=-1.0)
            z = act(cum[:, :], cum[:, :], ACT.Ln, [z], bias=ones[:, 0:1])
            z = stt(ncum[:, :], ncum[:, :], 0.0, cum[:, :], MIN, SUB, [z])
            z = scan(cum[:, :], bc(ones[:, 0:1], [P, T]), ncum[:, :], 0.0, MUL, ADD, [z])
            cw = ts(ncum[:, :], cum[:, :], -1.0, w=[z])

            gemm_t(W[:, 0:DM], KC, DM, lambda k: xt[:, k, :], T,
                   lambda j, n, ps, t: [act(qt[:, j:j + n, :], ps, ACT.Copy, [t], scale=dh ** -0.5)], xw)
            gemm_t(W[:, DM:2 * DM], KC, DM, lambda k: xt[:, k, :], T,
                   lambda j, n, ps, t: [cp(kt[:, j:j + n, :], ps, [t])], xw)
            gemm_n(W[:, 2 * DM:3 * DM], KC, DM, lambda k, a: xt[:, k, a * P:(a + 1) * P], (0, 1),
                   lambda a, o, n, ps, t: [cp(v[:, a, o:o + n], ps, [t])], xw)
            gemm_t(W[:, 3 * DM:4 * DM], KC, DM, lambda k: xt[:, k, :], T,
                   lambda j, n, ps, t: [act(gt[:, j:j + n, :], ps, ACT.Sigmoid, [t])], xw)
            ot = xt
            top[0] = 0
            xt_ = ar(KC, T)
            del xt_
            st = [(tmp[:, 2 * i:2 * i + 2, :], tmp[:, 4 + 2 * i:6 + 2 * i, :]) for i in range(2)]
            bufs = Turns(st)
            mx = rs
            qkv = E.barrier()
            mask = vec[:, VEC["mask_z"][0]:VEC["mask_z"][0] + 2 * P]
            for qb in range(2):
                nh = 4 if qb == 0 else 2
                nk = P * (qb + 1)
                for h0 in [2 * nh * i + j for i in range(H // nh // 2) for j in range(2)]:
                    heads = [h0 + 2 * i for i in range(nh)]
                    bi, bank, bw = pb.next()
                    sv = bank[:, :].rearrange("p (h k) -> p h k", h=nh)
                    for i in range(nh):
                        h = heads[i]
                        q0 = 64 * (h % 2)
                        mm(sv[:, i, :], qt[q0:q0 + 64, h // 2, qb * P:(qb + 1) * P],
                           kt[q0:q0 + 64, h // 2, 0:nk], True, False, qkv + bw + [cw])
                        sel = ident[q0:q0 + H, q0 + h:q0 + h + 1]
                        mm(sv[:, i, :], sel.to_broadcast([H, P]), ncum[q0:q0 + H, 0:nk], False, False)
                        last = mm(sv[:, i, :], cum[q0:q0 + H, qb * P:(qb + 1) * P], sel.to_broadcast([H, nk]),
                                  False, True, inc=i == nh - 1)
                    ui, (sbuf_, pt), uw = bufs.next()
                    s = sbuf_.rearrange("p a t -> p (a t)").rearrange("p (h k) -> p h k", h=nh)
                    t = tt(s, sv, bc(mask[:, P - (nk - P):2 * P], [P, nh, nk], 1), ADD, [last] + uw)
                    pb.done(bi, t)
                    m = mx[:, 0:nh]
                    t = red(m, s, MAX, [t])
                    t = tt(s, s, bc(m, [P, nh, nk], 2), SUB, [t])
                    t = act(s, s, ACT.Exp, [t])
                    t = red(m, s, ADD, [t])
                    t = rcp(m, m, [t])
                    t = tt(s, s, bc(m, [P, nh, nk], 2), MUL, [t])
                    bi, bank, bw = pb.next()
                    sf = s.rearrange("p h k -> p (h k)")
                    for i in range(4):
                        last = tr(bank[:, i * P:(i + 1) * P], sf[:, i * P:(i + 1) * P], [t] + bw, inc=i == 3)
                    ptf = pt.rearrange("p a t -> p (a t)")
                    t = cp(ptf, bank[:, :], [last], k="a")
                    pb.done(bi, t)
                    bi, bank, bw = pb.next()
                    q0 = 64 * (h0 % 2)
                    for i, h in enumerate(heads):
                        for kb in range(qb + 1):
                            last = mm(bank[q0:q0 + 64, i * P:(i + 1) * P], v[:, kb, h * dh:(h + 1) * dh],
                                      ptf[:, (i * (qb + 1) + kb) * P:(i * (qb + 1) + kb + 1) * P],
                                      kb == 0, kb == qb, [t] + bw, inc=(i == nh - 1 and kb == qb),
                                      tile=(0, q0))
                    c0 = h0 // 2
                    t = tt(ot[q0:q0 + 64, c0:c0 + nh, qb * P:(qb + 1) * P],
                           bank[q0:q0 + 64, 0:nh * P].rearrange("p (a t) -> p a t", a=nh),
                           gt[q0:q0 + 64, c0:c0 + nh, qb * P:(qb + 1) * P], MUL, [last])
                    pb.done(bi, t)
                    bufs.done(ui, last)
            gemm_t(A["fox_w_out"][0], KC, DM, lambda k: ot[:, k, :], T,
                   lambda j, n, ps, tk: [tt(x[:, j:j + n, :], ps, x[:, j:j + n, :], ADD, [tk])], [t])

        def moe(L):
            phase()
            xt = ar(KC, T)
            tmp = ar(KC, T)
            rs = ar(T)
            xn = ar(2, DM)
            wr = ar(KC, 36)
            tw = small(wr, A["wr"][L])
            g = V("norm_ffn", 8 * L, 8)
            xw = rms_t(x, T, xt, [(0, T, lambda c: g[:, c:c + 1], None)], None, tmp, rs, ())
            for a in range(2):
                for c in range(0, KC, 4):
                    bi, bank, bw = pb.next()
                    for j in range(4):
                        last = tr(bank[:, j * P:(j + 1) * P], xt[:, c + j, a * P:(a + 1) * P], xw + bw, inc=j == 3)
                    xnw = cp(xn[:, a, c * P:(c + 4) * P], bank[:, :], [last], k="a")
                    pb.done(bi, xnw)
            lg = ar(2, 36)
            bi, bank, bw = pb.next()
            rb, r1_ = R("br", 36 * L, 36)
            for a in range(2):
                for k in range(KC):
                    mm(bank[:, 36 * a:36 * a + 36], xt[:, k, a * P:(a + 1) * P], wr[:, k, :], k == 0, False,
                       xw + bw + [tw])
                last = mm(bank[:, 36 * a:36 * a + 36], r1_, rb, False, True, inc=a == 1)
            t = cp(lg, bank[:, 0:72].rearrange("p (a n) -> p a n", a=2), [last])
            pb.done(bi, t)

            def softmax(out, src, n, w):
                m = ar(2)
                t = red(m, src, MAX, w)
                t = tt(out, src, bc(m, [P, 2, n], 2), SUB, [t])
                t = act(out, out, ACT.Exp, [t])
                t = red(m, out, ADD, [t])
                t = rcp(m, m, [t])
                return tt(out, out, bc(m, [P, 2, n], 2), MUL, [t])

            def first_max(oh, val, src, n, w):
                c = ar(2, n)
                m = ar(2)
                t = red(val, src, MAX, w)
                t = tt(c, src, bc(val, [P, 2, n], 2), ALU.is_equal, [t])
                t = stt(c, c, -64.0, bc(V("iota", 0, n), [P, 2, n], 1), MUL, ADD, [t])
                t = red(m, c, MIN, [t])
                return tt(oh, c, bc(m, [P, 2, n], 2), ALU.is_equal, [t])

            pg, ohg, pgv = ar(2, 4), ar(2, 4), ar(2)
            t = softmax(pg, lg[:, :, 0:4], 4, [t])
            t = first_max(ohg, pgv, pg, 4, [t])
            big = ar(2, 4, 8)
            ein, oh1, oh2, m1, m2 = ar(2, 8), ar(2, 8), ar(2, 8), ar(2), ar(2)
            for a in range(2):
                t = tt(big[:, a], lg[:, a, 4:36].rearrange("p (g e) -> p g e", g=4),
                       bc(ohg[:, a], [P, 4, 8], 2), MUL, [t])
                t = red(ein[:, a, :], big[:, a].rearrange("p g e -> p e g"), ADD, [t])
            t = softmax(ein, ein, 8, [t])
            t = first_max(oh1, m1, ein, 8, [t])
            t = stt(ein, oh1, -2.0, ein, MUL, ADD, [t])
            t = first_max(oh2, m2, ein, 8, [t])
            r = ar(2)
            t = tt(r, m1, m2, ADD, [t])
            t = rcp(r, r, [t])
            t = tt(r, r, pgv, MUL, [t])
            t = tt(m1, m1, r, MUL, [t])
            t = tt(m2, m2, r, MUL, [t])
            sel8, gat8 = ar(2, 8), ar(2, 8)
            t = tt(sel8, oh1, oh2, ADD, [t])
            t = tt(oh1, oh1, bc(m1, [P, 2, 8], 2), MUL, [t])
            t = tt(oh2, oh2, bc(m2, [P, 2, 8], 2), MUL, [t])
            t = tt(gat8, oh1, oh2, ADD, [t])
            sel, px, gx = ar(2, NE), ar(2, NE + NX), ar(2, NE + NX)
            for a in range(2):
                t = tt(sel[:, a, :].rearrange("p (g e) -> p g e", g=4), bc(ohg[:, a], [P, 4, 8], 2),
                       bc(sel8[:, a], [P, 4, 8], 1), MUL, [t])
                t = tt(gx[:, a, 0:NE].rearrange("p (g e) -> p g e", g=4), bc(ohg[:, a], [P, 4, 8], 2),
                       bc(gat8[:, a], [P, 4, 8], 1), MUL, [t])
            bi, bank, bw = pb.next()
            mm(bank[:, 0:NE], V("tri"), sel[:, 0, :], True, True, [t] + bw)
            mm(bank[:, NE:2 * NE], ones, sel[:, 0, :], True, False)
            mm(bank[:, NE:2 * NE], V("tri"), sel[:, 1, :], False, True)
            mm(bank[:, 2 * NE:3 * NE], ones, sel[:, 0, :], True, False)
            last = mm(bank[:, 2 * NE:3 * NE], ones, sel[:, 1, :], False, True, inc=True)
            pos1, cnt, nb, pre = ar(2, NE), ar(NE), ar(NE), ar(NE)
            t = stt(pos1, bank[:, 0:2 * NE].rearrange("p (a n) -> p a n", a=2), 1.0, sel, ADD, MUL, [last])
            t = cp(cnt, bank[:, 2 * NE:3 * NE], [t])
            pb.done(bi, t)
            t = ts(px[:, :, 0:NE], pos1, -1.0, op0=ADD, w=[t])
            t = ts(nb, cnt, 64.5, op0=ALU.is_gt, w=[t])
            t = stt(nb, cnt, 128.5, nb, ALU.is_gt, ADD, [t])
            t = stt(nb, cnt, 192.5, nb, ALU.is_gt, ADD, [t])
            t = scan(pre, bc(ones[:, 0:1], [P, NE]), nb, 0.0, MUL, ADD, [t])
            ohj, ohk = ar(NX, NE), ar(NX, NE)
            jota = bc(V("jota"), [P, NX, NE], 2)
            t = tt(ohk, bc(pre, [P, NX, NE], 1), jota, ALU.is_gt, [t])
            t = tt(pre, pre, nb, SUB, [t])
            t = tt(ohj, bc(pre, [P, NX, NE], 1), jota, ALU.is_le, [t])
            t = tt(ohj, ohj, ohk, MUL, [t])
            off, ids = ar(NX), ar(2, NX)
            t = tt(ohk, ohj, bc(pre, [P, NX, NE], 1), MUL, [t])
            t = red(off, ohk, ADD, [t])
            t = tt(off, V("jota"), off, SUB, [t])
            t = ts(off, off, 64.0, 65.0, MUL, ADD, [t])
            t = tt(ohk, ohj, bc(V("iota", 0, NE), [P, NX, NE], 1), MUL, [t])
            t = red(ids[:, 0, :], ohk, ADD, [t])
            t = red(ids[:, 1, :], ohj, ADD, [t])
            for a in range(2):
                t = tt(ohk, ohj, bc(pos1[:, a], [P, NX, NE], 1), MUL, [t])
                t = red(px[:, a, NE:], ohk, ADD, [t])
                t = tt(px[:, a, NE:], px[:, a, NE:], off, SUB, [t])
                t = tt(ohk, ohj, bc(gx[:, a, 0:NE], [P, NX, NE], 1), MUL, [t])
                t = red(gx[:, a, NE:], ohk, ADD, [t])
            tid = cp(eid[0:1, 0:2 * NX], ids[0:1].rearrange("p a n -> p (a n)"), [t])
            routed = tid

            xg_b = Turns([ar(KC, 4, SL) for _ in range(2)])
            dt_b = Turns([ar(4, T) for _ in range(2)])
            d_t = ar(2, 4, SL)
            dg_t = ar(2, 4, 2, SL)
            hs_b = Turns([ar(512) for _ in range(2)])
            ht_b = Turns([ar(4, SL) for _ in range(2)])
            y_b = Turns([ar(512) for _ in range(2)])
            NB = NE + NX
            acc = banks[0:4]
            accw = [fill(acc[i][:, :], 0.0, pb.free[i]) for i in range(4)]
            pq = Turns(banks[4:8])
            pq.free = [list(pb.free[i]) for i in range(4, 8)]
            group = {}
            lastd = [[], []]

            def prepare(q):
                n = min(4, NB - 4 * q)
                dw = []
                for a in range(2):
                    t = tt(d_t[:, a, 0:n, :], bc(V("iota"), [P, n, SL], 1),
                           bc(px[:, a, 4 * q:4 * q + n], [P, n, SL], 2), ALU.is_equal, [routed] + lastd[0])
                    dw.append(t)
                for a in range(2):
                    for b in range(n):
                        t = ts(dg_t[:, a, b], bc(d_t[:, a, b], [P, 2, SL], 1), gx[:, a, 4 * q + b:4 * q + b + 1],
                               w=[t] + lastd[1])
                xi, xg, xgw = xg_b.next()
                evs = []
                for c in range(0, KC, 2):
                    bi, bank, bw = pq.next()
                    for j in range(2):
                        for a in range(2):
                            last = mm(bank[:, j * T:j * T + n * SL], xn[:, a, (c + j) * P:(c + j + 1) * P],
                                      d_t[:, a, 0:n, :], a == 0, a == 1, dw + bw + [xnw], inc=(j == 1 and a == 1))
                    e = cp(xg[:, c:c + 2, 0:n, :], bank[:, :].rearrange("p (a b s) -> p a b s", a=2, b=4)[:, :, 0:n, :],
                           [last] + xgw, k="a" if c % 4 else "v")
                    evs.append(e)
                    pq.done(bi, e)
                lastd[0] = [last]
                di, dt_, dtw = dt_b.next()
                dte = []
                for b in range(0, n, 2):
                    m = min(2, n - b)
                    bi, bank, bw = pq.next()
                    for j in range(m):
                        for a in range(2):
                            last = tr(bank[:, j * T + a * P:j * T + (a + 1) * P],
                                      dg_t[:, a, b + j].rearrange("p d s -> p (d s)"), [t] + bw,
                                      inc=(j == m - 1 and a == 1))
                    e = cp(dt_[:, b:b + m, :], bank[:, 0:m * T].rearrange("p (a t) -> p a t", a=m), [last] + dtw, k="a")
                    dte.append(e)
                    pq.done(bi, e)
                lastd[1] = [last]
                group[q] = (xi, xg, evs, di, dt_, dte)

            info = {}

            def up(b):
                q = b // 4
                if b % 4 == 0:
                    prepare(q)
                if b < NE:
                    gu = [wload(A["expert_w_gu"][L, b, k * 256:(k + 1) * 256, :], 2, DM) for k in range(4)]
                    dn = [wload(A["expert_w_down"][L, b, k * 256:(k + 1) * 256, :], 2, DM) for k in range(2)]
                else:
                    j = b - NE
                    if j == 0:
                        E.put("s", lambda e: load_ids(e), [tid], inc=False)
                    gu = [wdyn(A["expert_w_gu"][L], j, k * 256) for k in range(4)]
                    dn = [wdyn(A["expert_w_down"][L], j, k * 256) for k in range(2)]
                xi, xg, evs, *_ = group[q]
                bi, bank, bw = pq.next()
                for k in range(KC):
                    for h in range(2):
                        last = mm(bank[64 * h:64 * h + 64, :], xg[:, k, b % 4, :],
                                  gu[k // 2][1][:, k % 2, 512 * h:512 * h + 512], k == 0, k == KC - 1,
                                  evs + bw + [gu[k // 2][2]], inc=(k == KC - 1 and h == 1), tile=(0, 64 * h))
                wfree(gu, last)
                xg_b.done(xi, last)
                hi, hs, hw = hs_b.next()
                t = act(hs[0:64, :], bank[0:64, :], ACT.Silu, [last] + hw)
                t = tt(hs[0:64, :], hs[0:64, :], bank[64:128, :], MUL, [t])
                pq.done(bi, t)
                info[b] = dict(dn=dn, hs=hs, hi=hi, t=t)

            def across(b):
                f = info[b]
                bi, bank, bw = pq.next()
                for k in range(4):
                    last = tr(bank[:, k * SL:(k + 1) * SL], f["hs"][0:64, k * P:(k + 1) * P], [f["t"]] + bw, inc=k == 3)
                hs_b.done(f["hi"], last)
                hi, ht, hw = ht_b.next()
                t = cp(ht, bank[:, 0:4 * SL].rearrange("p (a s) -> p a s", a=4), [last] + hw, k="a")
                pq.done(bi, t)
                f.update(ht=ht, hti=hi, t=t)

            def down(b):
                f = info[b]
                dn = f["dn"]
                bi, bank, bw = pq.next()
                for k in range(4):
                    for h in range(2):
                        last = mm(bank[64 * h:64 * h + 64, :], f["ht"][:, k, :],
                                  dn[k // 2][1][:, k % 2, 512 * h:512 * h + 512], k == 0, k == 3,
                                  [f["t"]] + bw + [dn[k // 2][2]], inc=(k == 3 and h == 1), tile=(0, 64 * h))
                wfree(dn, last)
                ht_b.done(f["hti"], last)
                yi, y, yw = y_b.next()
                t = cp(y, bank[:, :], [last] + yw)
                pq.done(bi, t)
                f.update(y=y, yi=yi, t=t)

            def back(b):
                f = info.pop(b)
                _, _, _, di, dt_, dte = group[b // 4]
                for j in range(4):
                    for h in range(2):
                        c = 4 * h + j
                        last = mm(acc[c // 2][:, (c % 2) * T:(c % 2 + 1) * T],
                                  f["y"][64 * h:64 * h + 64, j * P:(j + 1) * P],
                                  dt_[64 * h:64 * h + 64, b % 4, :], False, b == NB - 1,
                                  [f["t"]] + dte + (accw if b == 0 else []), inc=(j == 3 and h == 1),
                                  tile=(64 * h, 0), skip=True)
                y_b.done(f["yi"], last)
                dt_b.done(di, last)
                return last

            for b in range(NB + 2):
                if b < NB:
                    up(b)
                if 1 <= b <= NB:
                    across(b - 1)
                if b >= 2:
                    last = back(b - 2)
                if 1 <= b <= NB:
                    down(b - 1)
            ends = []
            for i in range(4):
                ends.append(tt(x[:, 2 * i:2 * i + 2, :], acc[i][:, :].rearrange("p (a t) -> p a t", a=2),
                               x[:, 2 * i:2 * i + 2, :], ADD, [last]))
            for i in range(4):
                pb.free[i] = [ends[i]]
                pb.free[4 + i] = pq.free[i]

        idv = {}

        def load_ids(e):
            for j in range(NX):
                idv[j] = (e.value_load(eid[0:1, j:j + 1], min_val=0, max_val=NE - 1),
                          e.value_load(eid[0:1, NX + j:NX + j + 1], min_val=0, max_val=1))
            return None

        def wdyn(src, j, k0):
            i = wt["n"] % RING
            wt["n"] += 1
            wt["count"][i] += 1
            dst = ring[:, i, :].rearrange("p (a b) -> p a b", a=2)

            def go(e):
                v, ok = idv[j]
                s = src[bass.ds(v, 1), k0:k0 + 256, :].rearrange("o (a p) n -> p (o a) n", p=P)
                return e.dma_start(dst, s, cond=ok)
            tok = E.dma("s", go, ring_sem[i], 16 * wt["count"][i], [wt["free"][i]])
            return i, dst, tok

        def ret():
            phase()
            W = A["ret_w_in"][0]
            xt = ar(KC, T)
            tmp = ar(KC, T)
            rs = ar(T)
            qt, kt = ar(4, 2, T), ar(4, 2, T)
            v = ar(2, 2048)
            gt = ar(16, T)
            g = V("norm_mix", 8, 8)
            xw = rms_t(x, T, xt, [(0, T, lambda c: g[:, c:c + 1], None)], None, tmp, rs, ())
            qf, kf = qt.rearrange("p h c t -> p (h c) t"), kt.rearrange("p h c t -> p (h c) t")
            gemm_t(W[:, 0:DM], KC, DM, lambda k: xt[:, k, :], T,
                   lambda j, n, ps, t: [cp(qf[:, j:j + n, :], ps, [t], k="a")], xw)
            gemm_t(W[:, DM:2 * DM], KC, DM, lambda k: xt[:, k, :], T,
                   lambda j, n, ps, t: [act(kf[:, j:j + n, :], ps, ACT.Copy, [t], scale=1.0 / 16)], xw)
            done = E.barrier()
            t4 = tmp.rearrange("p (a h) t -> p a h t", a=2)
            cosb, sinb = bc(V("cos"), [P, 4, T], 1), bc(V("sin"), [P, 4, T], 1)
            for m in (qt, kt):
                a, b = m[:, :, 0, :], m[:, :, 1, :]
                t = tt(t4[:, 0], a, sinb, MUL, done)
                t = tt(t4[:, 1], b, sinb, MUL, [t])
                t = tt(a, a, cosb, MUL, [t])
                t = tt(b, b, cosb, MUL, [t])
                t = tt(a, a, t4[:, 1], SUB, [t])
                rot = tt(b, b, t4[:, 0], ADD, [t])
            gemm_n(W[:, 2 * DM:4 * DM], KC, 2048, lambda k, a: xt[:, k, a * P:(a + 1) * P], (0, 1),
                   lambda a, o, n, ps, t: [cp(v[:, a, o:o + n], ps, [t])], xw)
            gemm_t(W[:, 4 * DM:6 * DM], KC, 2048, lambda k: xt[:, k, :], T,
                   lambda j, n, ps, t: [act(gt[:, j:j + n, :], ps, ACT.Silu, [t])], xw)
            done = E.barrier()
            dec = V("dec").rearrange("p (h t) -> p h t", h=4)
            st = xt.rearrange("p a t -> p (a t)")
            sts = Turns([st[:, 0:384], st[:, 512:896]])
            o_b = tmp[:, 0:4, :]
            sq = tmp[:, 4:8, :]
            gn = V("gn")
            tsq = None
            for h in range(4):
                bi, bank, bw = pb.next()
                for c in range(2):
                    mm(bank[:, 0:T], kt[:, h, c, 0:P], qt[:, h, c, :], c == 0, c == 1, done + bw + [rot])
                for c in range(2):
                    last = mm(bank[:, T:T + P], kt[:, h, c, P:T], qt[:, h, c, P:T], c == 0, c == 1, inc=c == 1)
                si, s, sw = sts.next()
                t = tt(s[:, 0:T], bank[:, 0:T], dec[:, h, :], MUL, [last] + sw)
                t = tt(s[:, T:T + P], bank[:, T:T + P], dec[:, h, 0:P], MUL, [t])
                pb.done(bi, t)
                for e in range(0, 4, 2):
                    bi, bank, bw = pb.next()
                    for j in range(2):
                        o = h * 512 + (e + j) * P
                        mm(bank[:, j * T:j * T + P], v[:, 0, o:o + P], s[:, 0:P], True, True, [t] + bw)
                        mm(bank[:, j * T + P:(j + 1) * T], v[:, 0, o:o + P], s[:, P:T], True, False)
                        last = mm(bank[:, j * T + P:(j + 1) * T], v[:, 1, o:o + P], s[:, T:T + P], False, True,
                                  inc=j == 1)
                    to = cp(o_b[:, e:e + 2, :], bank[:, :].rearrange("p (a t) -> p a t", a=2), [last, tsq], k="a")
                    pb.done(bi, to)
                sts.done(si, last)
                bi, ps, tok = colsum([o_b[:, e, :] for e in range(4)], T, [to])
                for e in range(4):
                    t = stt(o_b[:, e, :], ps, -1.0 / 512, o_b[:, e, :], MUL, ADD, [tok])
                pb.done(bi, t)
                tq = act(sq, o_b, ACT.Square, [t])
                bi, ps, tok = colsum([sq[:, e, :] for e in range(4)], T, [tq])
                r, ta = rstd_of(rs, ps, 1.0 / 512, [tok])
                pb.done(bi, ta)
                t = tt(o_b, o_b, bc(rs, [P, 4, T], 1), MUL, [r])
                for e in range(4):
                    j = 4 * h + e
                    tsq = stt(gt[:, j, :], o_b[:, e, :], gn[:, j:j + 1], gt[:, j, :], MUL, MUL, [t])
            gemm_t(A["ret_w_out"][0], 16, DM, lambda k: gt[:, k, :], T,
                   lambda j, n, ps, tk: [tt(x[:, j:j + n, :], ps, x[:, j:j + n, :], ADD, [tk])], [tsq])

        def second(L):
            phase()
            last_layer = L == 1
            lo = T if last_layer else 0
            mod = ar(48, 2)
            gm = ar(2, 8, 2)
            keep = top[0]
            cs = ar(KC, 32)
            mrow = ar(512)
            mrow2 = ar(512)
            t = fill(cs, 0.0)
            t = act(cs[:, :, 0], V("cc"), ACT.Silu, [t])
            t = act(cs[:, :, 1], V("c"), ACT.Silu, [t])
            sel2 = ar(2)
            ts_ = red(sel2, ident.rearrange("p (a b) -> p b a", a=4)[:, 0:2, :], ADD)
            mbank, mw = banks[0], pb.free[0]
            pm = Turns(banks[1:])
            pm.free = pb.free[1:]
            rows = Turns([mrow, mrow2])
            for o in range(0, 6 * DM, 512):
                slots = [wload(A["w_mod_2"][L, g * 512:(g + 1) * 512, o:o + 512], 4, 512) for g in range(2)]
                bi, bank, bw = pm.next()
                for g in range(2):
                    for c in range(4):
                        last = mm(bank[32 * c:32 * c + 32, :], cs[:, 4 * g + c, :], slots[g][1][:, c, :], g == 0, g == 1,
                                  [t, slots[g][2]] + bw, inc=(g == 1 and c == 3), tile=(0, 32 * c))
                wfree(slots, last)
                ri, rr, rw = rows.next()
                tr_ = cp(rr, bank[:, :], [last] + rw, k="a")
                pm.done(bi, tr_)
                for j in range(4):
                    c = o // P + j
                    last = mm(mbank[:, 2 * c:2 * c + 2], rr[:, j * P:(j + 1) * P], sel2, True, True,
                              [tr_, ts_] + mw, inc=j == 3)
                rows.done(ri, last)
            t = tt(mod, mbank[:, 0:96].rearrange("p (c v) -> p c v", v=2), bc(V("b_mod", 48 * L, 48), [P, 48, 2], 2),
                   ADD, [last])
            pb.free[0] = [t]
            pb.free[1:] = pm.free
            for i, (nm, sc) in enumerate((("norm1", 8), ("norm2", 32))):
                t = stt(gm[:, i], mod[:, sc:sc + 8, :], 1.0, bc(V(nm, 8 * L, 8), [P, 8, 2], 2), ADD, MUL, [t])
            modw = t
            done = E.barrier()
            for k in "vag":
                put(k, lambda e: e.nop(), done)
            top[0] = keep

            def parts(i, sh, lo_):
                out = []
                for v_, a, b in ((0, 0, T), (1, T, 2 * T)):
                    if a >= lo_:
                        out.append((a, b, lambda c, v_=v_: gm[:, i, c, v_:v_ + 1],
                                    lambda c, v_=v_: mod[:, sh + c, v_:v_ + 1]))
                return out

            def residual(g0, lo_):
                def ev(j, n, ps, tk):
                    for i in range(n):
                        for v_, a, b in ((0, 0, T), (1, T, 2 * T)):
                            if a >= lo_:
                                t = stt(xr[:, j + i, a:b], ps[:, i, a - lo_:b - lo_], mod[:, g0 + j + i, v_:v_ + 1],
                                        xr[:, j + i, a:b], MUL, ADD, [tk])
                    return [t]
                return ev

            xt = ar(KC, 2 * T)
            yt = ar(KC, 2 * T)
            rs = ar(2 * T)
            xw = rms_t(xr[:, :, :], 2 * T, xt, parts(0, 0, 0), None, yt, rs, [modw])
            mark = E.barrier()
            W = A["w_in_2"][L]
            X = lambda k: xt[:, k, :]
            XL = lambda k: xt[:, k, lo:]
            nq = 2 * T - lo
            tiles = range(lo // P, 4)
            bcv = V("bc", 4 * L, 4)
            bu = V("bu", 2 * L, 2)
            early = top[0]
            cva, cvg, ut, sv = ar(2, 2 * T), ar(2, 2 * T), ar(2, 2 * T), ar(4, 256)
            lngb, wst = ar(2, 256), ar(4, P)
            st6, mv, sr = ar(4, 6), ar(4, 2), ar(4)
            early_end = top[0]
            qt, kt = ar(4, 2 * T), ar(4, 2 * T)
            vn = ar(4, 4, 129)
            on = ar(4, 512)
            graw = ar(2 * T)
            g_in, g_f = ar(2 * T), ar(2 * T)
            bks = ar(4)
            gemm_t(W[:, 2576:2832], KC, 256, XL, nq,
                   lambda j, n, ps, tk: [ts(cva[:, j + i, lo:], ps[:, i, :], bcv[:, j + i:j + i + 1], op0=ADD, w=[tk])
                                         for i in range(n)], xw)
            gemm_t(W[:, 2832:3088], KC, 256, XL, nq,
                   lambda j, n, ps, tk: [act(cvg[:, j + i, lo:], ps[:, i, :], ACT.Sigmoid, [tk],
                                             bias=bcv[:, 2 + j + i:3 + j + i]) for i in range(n)], xw)
            after_conv_in = E.barrier()
            cw = V("conv_w", 62 * L, 62).rearrange("p (c k) -> p c k", c=2)
            cb = V("conv_b", 2 * L, 2)
            pads = yt.rearrange("p a t -> p (a t)")
            t = fill(pads[:, 0:286 * 2 + 376 + 640], 0.0, after_conv_in)
            t = tt(cva[:, :, lo:], cva[:, :, lo:], cvg[:, :, lo:], MUL, [t])
            ct = cvg
            o1 = 572
            px0 = pads[:, o1:o1 + 376].rearrange("p (r c) -> p r c", r=4)
            px1 = pads[:, o1 + 376:o1 + 376 + 640]
            t = cp(px0[:, :, 15:79], cva[:, 0, T:].rearrange("p (r c) -> p r c", r=4), [t])
            t = cp(px1[:, 192:448], cva[:, 1, T:], [t])
            if not last_layer:
                pc = pads[:, 0:572].rearrange("p (c t) -> p c t", c=2)
                t = cp(pc[:, :, 15:271], cva[:, :, 0:T], [t])
                for c in range(2):
                    o = ct[:, c, 0:T]
                    t = ts(o, pc[:, c, 0:T], cw[:, c, 0:1], cb[:, c:c + 1], MUL, ADD, [t])
                    for k in range(1, 31):
                        t = stt(o, pc[:, c, k:k + T], cw[:, c, k:k + 1], o, MUL, ADD, [t])
            o = ct[:, 0, T:].rearrange("p (r c) -> p r c", r=4)
            t = ts(o, px0[:, :, 0:64], cw[:, 0, 0:1], cb[:, 0:1], MUL, ADD, [t])
            for k in range(1, 31):
                t = stt(o, px0[:, :, k:k + 64], cw[:, 0, k:k + 1], o, MUL, ADD, [t])
            o = ct[:, 1, T:]
            t = ts(o, px1[:, 0:T], cw[:, 1, 12:13], cb[:, 1:2], MUL, ADD, [t])
            for d in range(1, 7):
                t = stt(o, px1[:, 64 * d:64 * d + T], cw[:, 1, 12 + d:13 + d], o, MUL, ADD, [t])
            conv_done = t

            gemm_t(W[:, 2064:2320], KC, 256, XL, nq,
                   lambda j, n, ps, tk: [act(ut[:, j + i, lo:], ps[:, i, :], ACT.Gelu_apprx_tanh, [tk],
                                             bias=bu[:, j + i:j + i + 1]) for i in range(n)], xw)
            gemm_n(W[:, 2320:2576], KC, 256, lambda k, a: xt[:, k, a * P:(a + 1) * P], tiles,
                   lambda a, o, n, ps, tk: [act(sv[:, a, :], ps, ACT.Gelu_apprx_tanh, [tk])],
                   xw, bias=R("bs", 256 * L, 256))
            tv = fill(vn[:, :, :, 128:129], 1.0, k="g")
            bq, bk = V("bq", 4 * L, 4), V("bk", 4 * L, 4)
            tbk = act(bks, bk, ACT.Copy, scale=128 ** -0.5)
            gemm_t(W[:, 0:512], KC, 512, XL, nq,
                   lambda j, n, ps, tk: [act(qt[:, j + i, lo:], ps[:, i, :], ACT.Identity, [tk],
                                             bias=bq[:, j + i:j + i + 1]) for i in range(n)], xw)
            gemm_t(W[:, 512:1024], KC, 512, X, 512,
                   lambda j, n, ps, tk: [act(kt[:, j, :], ps[:, 0, :], ACT.Identity, [tk, tbk],
                                             bias=bks[:, j:j + 1], scale=128 ** -0.5)], xw)
            gemm_n(W[:, 1024:1536], KC, 512, lambda k, a: xt[:, k, a * P:(a + 1) * P], range(4),
                   lambda a, o, n, ps, tk: [cp(vn[:, a, :, 0:P], ps.rearrange("p (h d) -> p h d", h=4), [tk, tv], k="a")],
                   xw, bias=R("bv", 512 * L, 512))
            gemm_n(W[:, 1536:2048], KC, 512, lambda k, a: xt[:, k, a * P:(a + 1) * P], tiles,
                   lambda a, o, n, ps, tk: [act(on[:, a, :], ps, ACT.Sigmoid, [tk])],
                   xw, bias=R("bo", 512 * L, 512))
            slot = wload(W[:, 2048:2064], KC, 16)
            bi, bank, bw = pb.next()
            for k in range(KC):
                last = mm(bank[0:16, :], slot[1][:, k, :], X(k), k == 0, k == KC - 1, xw + bw + [slot[2]], inc=k == KC - 1)
            wfree([slot], last)
            t = act(graw[0:16, :], bank[0:16, :], ACT.Identity, [last], bias=V("bg", L, 1)[0:16, :])
            pb.done(bi, t)
            for j in range(4):
                q0 = 32 * (j // 2)
                bi, bank, bw = pb.next()
                last = mm(bank[q0:q0 + 4, :], ident[0:16, 4 * j:4 * j + 4], graw[0:16, :], True, True, [t] + bw,
                          inc=True, tile=(0, q0))
                pb.done(bi, cp((g_f if j % 2 else g_in)[q0:q0 + 4, :], bank[q0:q0 + 4, :], [last], k="a"))
            done = E.barrier()
            for k in "vagp":
                put(k, lambda e: e.nop(), done)
            hold = top[0]
            top[0] = keep
            kn = ar(4, 4, P)
            hn = ar(4, 512)
            assert top[0] <= keep + KC * 2 * T
            for a in range(4):
                bi, bank, bw = pb.next()
                for h in range(4):
                    last = tr(bank[:, h * P:(h + 1) * P], kt[:, h, a * P:(a + 1) * P], done + bw, inc=h == 3)
                knw = cp(kn[:, a], bank[:, :].rearrange("p (h d) -> p h d", h=4), [last], k="a")
                pb.done(bi, knw)
            top[0] = hold

            w_ = nq
            bi, ps, tok = colsum([ct[:, c, lo:] for c in range(2)], w_, [conv_done])
            for c in range(2):
                t = stt(ct[:, c, lo:], ps, -1.0 / 256, ct[:, c, lo:], MUL, ADD, [tok])
            pb.done(bi, t)
            tq = act(cva[:, :, lo:], ct[:, :, lo:], ACT.Square, [t])
            bi, ps, tok = colsum([cva[:, c, lo:] for c in range(2)], w_, [tq])
            r, ta = rstd_of(rs[:, lo:], ps, 1.0 / 256, [tok])
            pb.done(bi, ta)
            t = tt(ct[:, :, lo:], ct[:, :, lo:], bc(rs[:, lo:], [P, 2, w_], 1), MUL, [r])
            lg_, lb_ = V("cln_g", 2 * L, 2), V("cln_b", 2 * L, 2)
            for c in range(2):
                t = act(yt[:, 6 + c, lo:], ct[:, c, lo:], ACT.Silu, [t], bias=lb_[:, c:c + 1], scale=lg_[:, c:c + 1])

            small(lngb[:, 0, :], A["sgu_ln_g_2"][L:L + 1, :].to_broadcast([P, 256]))
            small(lngb[:, 1, :], A["sgu_ln_b_2"][L:L + 1, :].to_broadcast([P, 256]))
            tl = small(wst, A["sgu_wt"][L])
            for a in tiles:
                ia = sv[:, a, :]
                oa = st6[:, a, :]
                ma = mv[:, a, :]
                t = put("v", lambda e, o=oa, i=ia: e.bn_stats(o, i), [tl])
                t = put("v", lambda e, o=ma, i=oa: e.bn_aggr(o, i), [t])
            r0, r1 = lo // P, 4
            r, _ = rstd_of(sr[:, r0:r1], mv[:, r0:r1, 1], 1.0, [t])
            for a in tiles:
                t = ts(sv[:, a, :], sv[:, a, :], mv[:, a, 0:1], sr[:, a:a + 1], SUB, MUL, [r])
            n_ = r1 - r0
            t = tt(sv[:, r0:r1, :], sv[:, r0:r1, :], bc(lngb[:, 0, :], [P, n_, 256], 1), MUL, [t])
            t = tt(sv[:, r0:r1, :], sv[:, r0:r1, :], bc(lngb[:, 1, :], [P, n_, 256], 1), ADD, [t])
            for c in range(2):
                bi, bank, bw = pb.next()
                for a in tiles:
                    for g in (2 * c, 2 * c + 1):
                        q0 = 64 * (g % 2)
                        o = bank[q0:q0 + 64, (a - r0) * P:(a - r0 + 1) * P]
                        mm(o, sv[:, a, g * 64:(g + 1) * 64], wst[:, g, :], True, False, [t] + bw, tile=(0, q0))
                        last = mm(o, R("sgub")[1][:, 0:64], R("sgub", 512 * L + g * P, P)[0], False, True,
                                  inc=(a == 3 and g % 2 == 1), tile=(96, q0))
                pb.done(bi, tt(yt[:, 4 + c, lo:], ut[:, c, lo:], bank[:, 0:w_], MUL, [last]))

            done = E.barrier()
            for k in "vagp":
                put(k, lambda e: e.nop(), done)
            hold = top[0]
            top[0] = early
            rows5 = [ar(2 * T) for _ in range(5)]
            cn = ar(2, 4, 129)
            dts = Turns([ar(4, P) for _ in range(2)])
            assert top[0] <= early_end
            top[0] = hold
            gates = {}
            zero = V("zero")
            emt = ar(32)

            for d in range(2):
                q0 = 32 * d
                fi = g_f[q0:q0 + 4, :]
                ii = g_in[q0:q0 + 4, :]
                B, U, NM, WI, MT = (r_[q0:q0 + 4, :] for r_ in rows5)
                on4 = ones[q0:q0 + 4, 0:1]
                t = stt(B, fi, -1.0, fi, MUL, MAX)
                t = act(B, B, ACT.Exp, [t], scale=-1.0)
                t = act(B, B, ACT.Ln, [t], bias=on4)
                t = stt(fi, fi, 0.0, B, MIN, SUB, [t])
                prev = zero[q0:q0 + 4, 0:1]
                for a in ((0, 1, 2, 3) if d == 0 else (1, 0, 3, 2)):
                    s0, s1 = a * P, (a + 1) * P
                    if d == 0:
                        view = slice(s0, s1)
                    else:
                        view = slice(s1 - 1, s0 - 1 if s0 else None, -1)
                    le = s1 - 1 if d == 0 else s0
                    t = scan(B[:, view], bc(on4, [4, P]), fi[:, view], 0.0, MUL, ADD, [t])
                    t = tt(U[:, s0:s1], ii[:, s0:s1], B[:, s0:s1], SUB, [t])
                    t = scan(MT[:, view], U[:, view], U[:, view], prev, MAX, MAX, [t])
                    t = ts(NM[:, s0:s1], MT[:, s0:s1], -1.0, w=[t])
                    t = ts(WI[:, s0:s1], MT[:, s0:s1], -1.0, prev, MUL, ADD, [t])
                    t = tt(MT[:, s0:s1], MT[:, s0:s1], B[:, s0:s1], ADD, [t])
                    prev = MT[:, le:le + 1]
                pm, pmb, pmw = pb.next()
                for a in range(4):
                    mtw = mm(pmb[:, 4 * a:4 * a + 4], MT[:, a * P:(a + 1) * P], ident[q0:q0 + 4, q0:q0 + 4],
                             True, True, [t] + pmw, inc=True)
                te = act(emt[:, 16 * d:16 * d + 16], pmb[:, 0:16], ACT.Exp, [mtw], scale=-1.0)
                pb.done(pm, te)
                gates[d] = (U, NM, WI, t)
            cnw = fill(cn, 0.0)
            wb, qs, st_, ks = ar(4, P), ar(4, P), ar(4, P), ar(4, P)
            rd = ar(4)
            masks = (V("mask_le"), V("mask_ge"))
            order = []
            for f, b in zip((0, 1, 2, 3), (1, 0, 3, 2)):
                order += [(0, f), (1, b)]
            rel = {"wb": [], "qs": [], "st": [], "ks": [], "cn": [cnw]}
            written = set()
            for d, a in order:
                U, NM, WI, gw = gates[d]
                q0 = 32 * d
                s0, s1 = a * P, (a + 1) * P
                le = P - 1 if d == 0 else 0
                with_out = not (last_layer and a < 2)
                final = a == (3 if d == 0 else 2)
                v4 = lambda bank: bank[:, :].rearrange("p (h t) -> p h t", h=4)
                bi, bank, bw = pb.next()
                for h in range(4):
                    sl = ident[q0:q0 + 4, q0 + h:q0 + h + 1].to_broadcast([4, P])
                    mm(v4(bank)[:, h, :], U[:, s0:s1], sl, True, False, [gw] + bw)
                    last = mm(v4(bank)[:, h, :], sl, NM[:, s0:s1], False, True, inc=h == 3)
                di, dt_, dw = dts.next()
                t = tt(dt_, v4(bank), bc(masks[d], [P, 4, P], 1), ADD, [last] + dw)
                pb.done(bi, t)
                dtw = act(dt_, dt_, ACT.Exp, [t])
                bi, bank, bw = pb.next()
                for h in range(4):
                    sl = ident[q0:q0 + 4, q0 + h:q0 + h + 1].to_broadcast([4, P])
                    last = mm(v4(bank)[:, h, :], sl, WI[:, s0:s1], True, True, bw, inc=h == 3)
                wbw = act(wb, v4(bank), ACT.Exp, [last] + rel["wb"])
                pb.done(bi, wbw)
                rel["wb"] = []
                if with_out:
                    tqs = tt(qs, qt[:, :, s0:s1], wb, MUL, [wbw] + rel["qs"])
                    bi, bank, bw = pb.next()
                    for h in range(4):
                        last = mm(v4(bank)[:, h, :], kt[:, h, s0:s1], qt[:, h, s0:s1], True, True, bw, inc=h == 3)
                    tst = tt(st_, v4(bank), dt_, MUL, [last, dtw] + rel["st"])
                    pb.done(bi, tst)
                    for hp in range(2):
                        bi, bank, bw = pb.next()
                        pv = bank[:, 0:258].rearrange("p (h n) -> p h n", h=2)
                        for i in range(2):
                            h = 2 * hp + i
                            mm(pv[:, i, :], st_[:, h, :], vn[:, a, h, :], True, False, [tst, tqs] + bw + rel["cn"])
                            last = mm(pv[:, i, :], qs[:, h, :], cn[:, d, h, :], False, True, inc=i == 1)
                        t = cp(rd[:, 2:4], pv[:, :, 128], [last, te])
                        em = emt[:, 16 * d + 4 * a + 2 * hp:16 * d + 4 * a + 2 * hp + 2]
                        t = stt(rd[:, 0:2], rd[:, 2:4], -1.0, em, MUL, MAX, [t])
                        t = tt(rd[:, 0:2], rd[:, 0:2], rd[:, 2:4], MAX, [t])
                        t = rcp(rd[:, 0:2], rd[:, 0:2], [t])
                        for i in range(2):
                            h = 2 * hp + i
                            o = hn[:, a, h * P:(h + 1) * P]
                            if a in written:
                                t = stt(o, pv[:, i, 0:P], rd[:, i:i + 1], o, MUL, ADD, [t])
                            else:
                                t = ts(o, pv[:, i, 0:P], rd[:, i:i + 1], w=[t])
                        pb.done(bi, t)
                    written.add(a)
                    rel["qs"] = rel["st"] = [last]
                    read = last
                else:
                    read = None
                if not final:
                    t = tt(ks, kn[:, a], bc(dt_[:, :, le], [P, 4, P], 2), MUL, [dtw, knw] + rel["ks"])
                    tcn = []
                    for hp in range(2):
                        bi, bank, bw = pb.next()
                        pv = bank[:, 0:258].rearrange("p (h n) -> p h n", h=2)
                        for i in range(2):
                            h = 2 * hp + i
                            last = mm(pv[:, i, :], ks[:, h, :], vn[:, a, h, :], True, True, [t] + bw, inc=i == 1)
                        for i in range(2):
                            h = 2 * hp + i
                            tc_ = stt(cn[:, d, h, :], cn[:, d, h, :], wb[:, h, le:le + 1], pv[:, i, :], MUL, ADD,
                                      [last, wbw, read])
                        pb.done(bi, tc_)
                    rel["ks"] = [last]
                    rel["cn"] = [tc_]
                    rel["wb"] = [tc_]
                else:
                    rel["wb"] = [tqs]
                dts.done(di, (E.sem["v"], E.n["v"]))
            mg = V("mlstm_g", 4 * L, 4)
            ss = ar(4)
            prevr = []
            for a in tiles:
                sq4 = st_
                h4 = hn[:, a, :].rearrange("p (h d) -> p h d", h=4)
                t = act(sq4, h4, ACT.Square, E.barrier() if a == r0 else [])
                t = red(ss, sq4, ADD, [t])
                r, _ = rstd_of(ss, ss, 1.0 / P, [t])
                t = tt(h4, h4, bc(ss, [P, 4, P], 2), MUL, [r])
                t = tt(hn[:, a, :], hn[:, a, :], on[:, a, :], MUL, [t])
                bi, bank, bw = pb.next()
                for h in range(4):
                    last = tr(bank[:, h * P:(h + 1) * P], hn[:, a, h * P:(h + 1) * P], [t] + bw, inc=h == 3)
                t = tt(yt[:, 0:4, a * P:(a + 1) * P], bank[:, :].rearrange("p (h t) -> p h t", h=4),
                       bc(mg, [P, 4, P], 2), MUL, [last])
                pb.done(bi, t)
            done = E.barrier()
            gemm_t(A["w_out_2"][L], KC, DM, lambda k: yt[:, k, lo:], nq, residual(16, lo), done)

            done = E.barrier()
            for k in "vagp":
                put(k, lambda e: e.nop(), done)
            top[0] = keep
            xt = ar(KC, 2 * T)[:, :, lo:]
            rs = ar(2 * T)
            ht = ar(22, nq)
            sg = Turns([ar(512) for _ in range(3)])
            tmpv = ht.rearrange("p a t -> p (a t)")[:, 0:KC * nq].rearrange("p (a t) -> p a t", a=KC)
            ps_ = [(a - lo, b - lo, m, s) for a, b, m, s in parts(1, 24, lo)]
            xw = rms_t(xr[:, :, lo:], nq, xt, ps_, None, tmpv, rs[:, 0:nq], [])
            for o, n in blocks(FF2):
                sa, fa = fetch(A["w_gu_2"][L], KC, o, n)
                sb_, fb = fetch(A["w_gu_2"][L], KC, FF2 + o, n)
                for j in range(n // P):
                    bs = []
                    for f in (fa, fb):
                        bi, bank, bw = pb.next()
                        for k in range(KC):
                            w0, dt_ = f(k)
                            last = mm(bank[:, 0:nq], w0[:, j * P:(j + 1) * P], xt[:, k, :], k == 0, k == KC - 1,
                                      xw + bw + [dt_], inc=k == KC - 1)
                        bs.append((bi, bank, last))
                    si, s, sw = sg.next()
                    t = act(s[:, 0:nq], bs[0][1][:, 0:nq], ACT.Silu, [bs[0][2]] + sw)
                    pb.done(bs[0][0], t)
                    t = tt(ht[:, o // P + j, :], s[:, 0:nq], bs[1][1][:, 0:nq], MUL, [t, bs[1][2]])
                    pb.done(bs[1][0], t)
                    sg.done(si, t)
                wfree(sa, last)
                wfree(sb_, last)
            gemm_t(A["w_down_2"][L], 22, DM, lambda k: ht[:, k, :], nq, residual(40, lo), [t])

        def final_():
            phase()
            xt = ar(KC, T)
            tmp = ar(KC, T)
            rs = ar(T)
            res = ar(2, DM)
            g = V("final")
            xw = rms_t(x, T, xt, [(0, T, lambda c: g[:, c:c + 1], None)], None, tmp, rs, ())
            put_out(xt, res, xw)

        def put_out(xt, res, xw):
            for a in range(2):
                for c in range(0, KC, 4):
                    bi, bank, bw = pb.next()
                    for j in range(4):
                        last = tr(bank[:, j * P:(j + 1) * P], xt[:, c + j, a * P:(a + 1) * P], list(xw) + bw, inc=j == 3)
                    t = cp(res[:, a, c * P:(c + 4) * P], bank[:, :], [last], k="v")
                    pb.done(bi, t)
            E.dma("s", lambda e: e.dma_start(A["out"][0].rearrange("(a p) d -> p a d", p=P), res), s_out, 16, [t])
            E.q["s"].append(([(s_out, 16)], lambda e: None, None))

        def norm_x():
            phase()
            tmp = ar(KC, T)
            rs = ar(T)
            g = V("norm_final")
            rms_t(x, T, x, [(0, T, lambda c: g[:, c:c + 1], None)], None, tmp, rs, ())

        steps = [("fox", fox), ("moe0", lambda: moe(0)), ("ret", ret), ("moe1", lambda: moe(1)),
                 ("norm", norm_x), ("sec0", lambda: second(0)), ("sec1", lambda: second(1))]
        for name, f in steps:
            f()
            if stop == name:
                break
        if stop is None:
            final_()
        else:
            phase()
            put_out(x, ar(2, DM), E.barrier())
        tail = [(ring_sem[i], 16 * wt["count"][i]) for i in range(RING) if wt["count"][i]]
        tail += [(s_small, nsm[0]), (s_x, 32)]
        E.q["s"].append((tail, lambda e: None, None))
        block = ctx.enter_context(nc.Block())
        E.run(block)


def consts():
    f = np.float32
    p = np.arange(P)
    inv = (f(1.0) / (f(10000.0) ** np.linspace(0.0, 1.0, 128, dtype=f))).astype(f)
    ang = (np.arange(T, dtype=f)[:, None] * inv[None, :]).astype(f)
    lg = np.log(1.0 - 2.0 ** (-5.0 - np.arange(4, dtype=np.float64)))
    rel = np.arange(T)[None, :] - p[:, None]
    dec = np.where(rel[:, None, :] >= 0, np.exp(lg[None, :, None] * np.maximum(rel, 0)[:, None, :]), 0.0)
    d = {
        "cos": np.cos(ang).T, "sin": np.sin(ang).T, "dec": dec.reshape(P, 1024), "ident": np.eye(P),
        "mask_z": np.zeros((P, P)), "mask_ge": np.where(p[None, :] > p[:, None], NEG, 0.0), "mask_le": np.where(p[None, :] < p[:, None], NEG, 0.0),
        "tri": (p[:, None] < p[None, :]), "ones": np.ones((P, P)), "iota": np.tile(np.arange(64), (P, 1)),
        "zero": np.zeros((P, 64)), "eps": np.full((P, 1), EPS), "jota": np.tile(np.arange(NX), (P, 1)),
    }
    return {k: np.asarray(v, f) for k, v in d.items()}


def layout(a):
    f = np.float32
    v = np.zeros((P, NVEC), f)

    def cols(name, x):
        o, w = VEC[name]
        v[:, o:o + w] = x.reshape(w, P).T

    cols("norm_mix", a["norm_mix"])
    cols("norm_ffn", a["norm_ffn"])
    cols("norm_final", a["norm_final"])
    cols("gn", a["ret_gn_gain"])
    cols("norm1", a["norm1_g_2"])
    cols("norm2", a["norm2_g_2"])
    cols("final", a["final_g_2"])
    cols("b_mod", a["b_mod_2"])
    cols("mlstm_g", a["mlstm_g_2"])
    cols("cln_g", a["conv_ln_g_2"])
    cols("cln_b", a["conv_ln_b_2"])
    cols("conv_b", a["conv_b_2"])
    cols("c", a["c_2"])
    cols("cc", a["c_ctx_2"])
    b = a["b_in_2"]
    cols("bq", b[:, 0:512])
    cols("bk", b[:, 512:1024])
    cols("bu", b[:, 2064:2320])
    cols("bc", b[:, 2576:3088])
    o, w = VEC["conv_w"]
    v[:, o:o + w] = a["conv_w_2"].reshape(2, 31, 2, P).transpose(3, 0, 2, 1).reshape(P, 124)
    o, _ = VEC["bg"]
    v[0:16, o:o + 2] = b[:, 2048:2064].T
    o, _ = VEC["bf"]
    v[0:16, o] = v[64:80, o] = a["fox_b_f"][0]
    for k, x in consts().items():
        o, w = VEC[k]
        v[:, o:o + w] = x
    r = np.zeros((P, NROW), f)

    def put(name, x):
        q, o, w = ROW[name]
        r[q, o:o + w] = x.reshape(-1)

    put("br", np.concatenate([a["router_group_b"], a["router_expert_b"]], 1))
    put("bv", b[:, 1024:1536])
    put("bo", b[:, 1536:2048])
    put("bs", b[:, 2320:2576])
    put("sgub", a["sgu_b_2"])
    wr = np.concatenate([a["router_group_w"], a["router_expert_w"]], 2)
    out = {k: a[k] for k in BIG}
    out["vec"], out["row"] = v, r
    out["wr"] = np.ascontiguousarray(wr.reshape(2, KC, P, 36).transpose(0, 2, 1, 3))
    out["sgu_wt"] = np.ascontiguousarray(a["sgu_w_2"].transpose(0, 3, 1, 2))
    return out


BIG = ["x", "ctx_2", "fox_w_in", "fox_w_out", "ret_w_in", "ret_w_out", "expert_w_gu", "expert_w_down",
       "w_mod_2", "w_in_2", "w_out_2", "w_gu_2", "w_down_2", "sgu_ln_g_2", "sgu_ln_b_2"]


def kernel(**inputs):
    import numpy as _np
    import concourse.bacc as _bacc
    from concourse import mybir as _mybir
    from concourse.bass_utils import run_bass_kernel_spmd as _run

    arrays = {k: _np.ascontiguousarray(v) for k, v in layout({k: _np.asarray(v) for k, v in inputs.items()}).items()}
    nc = _bacc.Bacc("TRN2", target_bir_lowering=False, num_devices=1)
    aps = {k: nc.dram_tensor(f"in_{k}", v.shape, _mybir.dt.from_np(v.dtype), kind="ExternalInput").ap()
           for k, v in arrays.items()}
    aps["out"] = nc.dram_tensor("out_0", (1, T, DM), _mybir.dt.float32, kind="ExternalOutput").ap()
    build(nc, aps)
    r = _run(nc, [{f"in_{k}": v for k, v in arrays.items()}], core_ids=[0])
    return r.results[0]["out_0"]
```

```python
import numpy as np
import concourse.bass as bass
from concourse import mybir
from contextlib import ExitStack

F32 = mybir.dt.float32
I32 = mybir.dt.int32
F32R = mybir.dt.float32r
ALU = mybir.AluOpType
ACT = mybir.ActivationFunctionType
AX = mybir.AxisListType
MUL, ADD, SUB, MAX, MIN = ALU.mult, ALU.add, ALU.subtract, ALU.max, ALU.min

P = 128
DM = 1024
KC = DM // P
T = 256
EPS = 1e-6
NEG = -1e30
NE = 32
NX = 15
SL = 32
GB = 8
FF2 = 2816

NSLOT = 12
F_LONG = 19512
SLOT = 2048
SPACE = 44772

VEC = {}
_n = [0]


def _vec(name, width):
    VEC[name] = (_n[0], width)
    _n[0] += width


for _name, _w in (("norm_mix", 16), ("norm_ffn", 16), ("norm_final", 8), ("gn", 16), ("norm1", 16),
                  ("norm2", 16), ("final", 8), ("b_mod", 96), ("mlstm_g", 8), ("cln_g", 4), ("cln_b", 4),
                  ("conv_b", 4), ("conv_w", 124), ("bq", 8), ("bk", 8), ("bg", 2), ("bu", 4), ("bc", 8),
                  ("c", 8), ("cc", 8), ("bf", 1), ("cos", 256), ("sin", 256), ("dec", 1024), ("ident", 128),
                  ("mask_z", 128), ("mask_ge", 128), ("mask_le", 128), ("tri", 128), ("ones", 128), ("iota", 64), ("zero", 64),
                  ("eps", 1), ("jota", NX)):
    _vec(_name, _w)
NVEC = _n[0]
ROW = {"bv": (0, 0, 1024), "bo": (32, 0, 1024), "bs": (64, 0, 512), "br": (64, 512, 72), "sgub": (96, 0, 1024)}
NROW = 1024


class Engines:

    def __init__(self, nc, ctx):
        self.nc = nc
        self.q = {k: [] for k in "vapgs"}
        self.n = dict.fromkeys("vapgs", 0)
        self.sem = {k: ctx.enter_context(nc.semaphore(f"done_{k}")) for k in "vapgs"}
        self.seen = {}

    def put(self, k, fn, waits=(), inc=True, own=True):
        need = {}
        waits = list(waits)
        if own and self.n[k] and k in "vag":
            waits.append((self.sem[k], self.n[k]))
        for w in waits:
            if w is None:
                continue
            s, v = w
            if v > self.seen.get((k, s.name), 0):
                need[s.name] = (s, max(v, need.get(s.name, (s, 0))[1]))
        for name, (s, v) in need.items():
            self.seen[(k, name)] = v
        if inc:
            self.n[k] += 1
        self.q[k].append((list(need.values()), fn, self.sem[k] if inc else None))
        return (self.sem[k], self.n[k])

    def dma(self, k, fn, sem, value, waits=()):
        need = []
        for w in waits:
            if w is not None and w[1] > self.seen.get((k, w[0].name), 0):
                self.seen[(k, w[0].name)] = w[1]
                need.append(w)
        self.q[k].append((need, lambda e: (fn(e).then_inc(sem, 16), None)[1], None))
        return (sem, value)

    def branch(self, cell, ready):
        self.saved = dict(self.seen)
        self.at = dict(self.n)
        for k in "vaps":
            self.q[k].append(("if", cell, ready))

    def join(self, extra):
        for k in "vaps":
            adds = [(self.sem[k], self.at[k], self.n[k] - self.at[k])] if self.n[k] > self.at[k] else []
            self.q[k].append(("end", adds + (extra if k == "s" else [])))
        self.seen = self.saved

    def barrier(self):
        now = [(self.sem[k], self.n[k]) for k in "vapg" if self.n[k]]
        return now

    def run(self, block):
        def emit(e, items):
            while items:
                head = items.pop(0)
                if head[0] == "if":
                    e.wait_ge(*head[2])
                    v = e.value_load(head[1], min_val=0, max_val=NX)
                    with e.If(v > 0):
                        adds = emit(e, items)
                    with e.Else():
                        for s, at, n in adds:
                            if at:
                                e.wait_ge(s, at)
                            e.sem_inc(s, n)
                    continue
                if head[0] == "end":
                    return head[1]
                waits, fn, sem = head
                for s, v in waits:
                    e.wait_ge(s, v)
                r = fn(e)
                if sem is not None:
                    r.then_inc(sem, 1)

        def body(k):
            def _(e):
                emit(e, self.q[k])
            return _
        block.sync(body("s"))
        block.gpsimd(body("g"))
        block.scalar(body("a"))
        block.vector(body("v"))
        block.tensor(body("p"))


class Turns:

    def __init__(self, items):
        self.items = items
        self.free = [[] for _ in items]
        self.at = 0

    def next(self):
        i = self.at
        self.at = (i + 1) % len(self.items)
        w, self.free[i] = self.free[i], []
        return i, self.items[i], w

    def done(self, i, *toks):
        self.free[i] = list(toks)


def build(nc, A, stop=None):
    ctx = ExitStack()
    with ctx:
        E = Engines(nc, ctx)
        put = E.put

        def sb(name, shape, dt=F32):
            return ctx.enter_context(nc.sbuf_tensor(name, shape, dt))

        def sem(name):
            return ctx.enter_context(nc.semaphore(name))

        xr = sb("xr", [P, KC, 2 * T])
        vec = sb("vec_sb", [P, NVEC])
        row = sb("row_sb", [P, NROW])
        mods = sb("mods", [P, 128])
        eid = sb("eid", [1, 2 * NX + 2], I32)
        banks = [ctx.enter_context(nc.psum_tensor(f"bank{i}", [P, 512], F32)) for i in range(8)]
        ring_sem = [sem(f"ring{i}") for i in range(NSLOT)]
        x_sem = [sem(f"xring{i}") for i in range(3)]
        s_vec = sem("s_vec")
        s_x = sem("s_x")
        s_small = sem("s_small")
        s_out = sem("s_out")

        def mm(out, lhsT, rhs, start, stop, w=(), inc=False, tile=None, skip=False):
            return put("p", lambda e: e.matmul(out, lhsT, rhs, start=start, stop=stop, tile_position=tile,
                                               skip_group_check=skip), w, inc)

        def tr(out, in_, w=(), inc=False):
            n = in_.shape[0]
            return put("p", lambda e: e.transpose(out, in_, V("ident")[0:n, 0:n]), w, inc)

        def act(out, in_, f, w=(), bias=None, scale=1.0, accum=None):
            kw = {}
            if bias is not None:
                kw["bias"] = bias
            if accum is not None:
                kw["accum_out"] = accum
            return put("a", lambda e: e.activation(out, in_, f, scale=scale, **kw), w)

        def tt(out, a, b, op, w=(), k="v"):
            return put(k, lambda e: e.tensor_tensor(out, a, b, op), w)

        def ts(out, a, s1, s2=None, op0=MUL, op1=None, w=(), k="v"):
            if op1 is None:
                return put(k, lambda e: e.tensor_scalar(out, a, s1, None, op0), w)
            return put(k, lambda e: e.tensor_scalar(out, a, s1, s2, op0, op1), w)

        def stt(out, a, s, b, op0, op1, w=()):
            return put("v", lambda e: e.scalar_tensor_tensor(out, a, s, b, op0, op1), w)

        def cp(out, a, w=(), k="v"):
            if k == "a":
                return act(out, a, ACT.Copy, w)
            return put(k, lambda e: e.tensor_copy(out, a), w)

        def red(out, a, op, w=(), axis=AX.X):
            return put("v", lambda e: e.tensor_reduce(out, a, axis, op), w)

        def rcp(out, a, w=()):
            return put("v", lambda e: e.reciprocal(out, a), w)

        def scan(out, a, b, init, op0, op1, w=()):
            return put("v", lambda e: e.tensor_tensor_scan(out, a, b, init, op0, op1), w)

        def fill(out, value, w=(), k="v"):
            return put(k, lambda e: e.memset(out, value), w)

        def bc(ap, shape, *axes):
            for x in axes:
                ap = ap.unsqueeze(x)
            return ap.to_broadcast(shape)

        def V(name, a=0, n=None):
            o, wd = VEC[name]
            return vec[:, o + a:o + (wd if n is None else a + n)]

        def R(name, a=0, n=None):
            q, o, wd = ROW[name]
            return row[q:q + 1, o + a:o + (wd if n is None else a + n)], ones[q:q + 1, :]

        eps = V("eps")
        ones = V("ones")
        ident = V("ident")

        rooms = []
        names = [0]
        ring = [None]
        wt = {"n": 0, "use": 0, "free": [[] for _ in range(NSLOT)], "count": [0] * NSLOT}

        def shut(n=0):
            while len(rooms) > n:
                rooms.pop()[0].close()

        def room(kind, size=None):
            taken = sum(r[3] for r in rooms)
            size = SPACE - taken if size is None else size
            assert taken + size <= SPACE, (taken, size)
            st = ExitStack()
            names[0] += 1
            t = st.enter_context(nc.sbuf_tensor(f"{kind}{names[0]}", [P, size], F32))
            rooms.append([st, t, kind, size, 0])
            return len(rooms)

        def all_wait(toks):
            for k in "vagp":
                put(k, lambda e: e.nop(), toks)

        def phase(slots):
            shut()
            now = E.barrier()
            all_wait(now)
            for i in range(wt["use"], slots):
                wt["free"][i] = now
            wt["use"] = slots
            if wt["n"] >= slots:
                wt["n"] = 0
            room("ring", slots * SLOT)
            ring[0] = rooms[0][1]

        def ar(*dims, kind="f", at=None):
            r = [r for r in rooms if r[2] == kind][-1]
            n = int(np.prod(dims))
            o = r[4] if at is None else at
            a = r[1][:, o:o + n]
            assert o + n <= r[3], (o, n, r[3])
            if at is None:
                r[4] += n
            if len(dims) == 2:
                a = a.rearrange("p (a b) -> p a b", a=dims[0])
            if len(dims) == 3:
                a = a.rearrange("p (a b c) -> p a b c", a=dims[0], b=dims[1])
            if len(dims) == 4:
                a = a.rearrange("p (a b c d) -> p a b c d", a=dims[0], b=dims[1], c=dims[2])
            return a

        def ra(*dims):
            return ar(*dims, kind="r")

        def back_to(o):
            r = [r for r in rooms if r[2] == "f"][-1]
            was, r[4] = r[4], o
            return was

        def slot_at(i, a, b):
            o = i * SLOT
            return ring[0][:, o:o + a * b].rearrange("p (a b) -> p a b", a=a)

        def wload(src, a, b):
            i = wt["n"]
            wt["n"] = (i + 1) % wt["use"]
            wt["count"][i] += 1
            dst = slot_at(i, a, b)
            s = src.rearrange("(a p) n -> p a n", p=P)
            tok = E.dma("s", lambda e: e.dma_start(dst, s), ring_sem[i], 16 * wt["count"][i], wt["free"][i])
            wt["free"][i] = []
            return i, dst, tok

        def wfree(slots, tok):
            for i, _, _ in slots:
                wt["free"][i] = [tok]

        pb = Turns(banks)

        def blocks(n):
            return [(o, min(512, n - o)) for o in range(0, n, 512)]

        def split(x, high, low, w, k="a"):
            t1 = cp(high.bitcast(F32R), x, w, k=k)
            return [t1, tt(low.bitcast(F32R), x, high, SUB, [t1])]

        def mm3(out, a, b, start, stop, w=(), inc=False, tile=None):
            (ah, al), (bh, bl) = a, b
            for i, (p, q) in enumerate(((ah, bh), (ah, bl), (al, bh))):
                last = mm(out, p.bitcast(F32R), q.bitcast(F32R), start and i == 0, stop and i == 2, w,
                          inc and i == 2, tile)
            return last

        hb = [None]

        def pairs(n):
            hb[0] = Turns([(ra(SLOT // 2), ra(SLOT // 2)) for _ in range(n)])

        def job(W, kchunks, N, x, outs, evac, w, moving, bias=None, wide=512, after=None):
            return dict(W=W, K=kchunks, N=N, x=x, outs=outs, evac=evac, w=w, moving=moving, bias=bias, wide=wide,
                        after=after)

        def gemm(jobs):
            items = []
            for jb in jobs:
                step = 4 if jb["wide"] > 256 else 8
                for o in range(0, jb["N"], jb["wide"]):
                    n = min(jb["wide"], jb["N"] - o)
                    for g in range(0, jb["K"], step):
                        kn = min(step, jb["K"] - g)
                        half = min(step // 2, kn)
                        for i in range(0, kn, half):
                            items.append((jb, o, n, g, kn, i, min(half, kn - i)))
            ready_ = []
            now = [None]

            def prep(jb, o, n, g, kn, i, m):
                if i == 0:
                    now[0] = wload(jb["W"][g * P:(g + kn) * P, o:o + n], kn, n)
                sl = now[0]
                hi_, hl, hw = hb[0].next()
                high, low = (z[:, 0:m * n].rearrange("p (a b) -> p a b", a=m) for z in hl)
                toks = split(sl[1][:, i:i + m, :], high, low, [sl[2]] + hw)
                if i + m == kn:
                    wfree([sl], toks[1])
                ready_.append((hi_, high, low, toks))

            ahead = len(hb[0].items) - 1
            nxt = 0
            for i, (jb, o, n, g, kn, i0, m) in enumerate(items):
                while nxt < len(items) and nxt <= i + ahead:
                    prep(*items[nxt])
                    nxt += 1
                hi_, high, low, sw = ready_.pop(0)
                k0 = g + i0
                if k0 == 0:
                    cn_ = min(P, n)
                    outs = list(range(n // cn_)) if jb["moving"] else jb["outs"]
                    acc_ = [pb.next() for _ in outs]
                end = k0 + m == jb["K"]
                toks = []
                for u, (bi, bank, bw) in zip(outs, acc_):
                    for k in range(m):
                        w = list(jb["w"](k0 + k) if callable(jb["w"]) else jb["w"]) + bw + sw
                        stop_ = end and k == m - 1 and jb["bias"] is None
                        inc = (k == m - 1)
                        if jb["moving"]:
                            c = slice(u * cn_, (u + 1) * cn_)
                            out = bank[0:cn_, 0:jb["outs"]]
                            last = mm3(out, (high[:, k, c], low[:, k, c]), jb["x"](k0 + k), k0 + k == 0, stop_, w, inc)
                        else:
                            out = bank[:, 0:n]
                            last = mm3(out, jb["x"](k0 + k, u), (high[:, k, :], low[:, k, :]), k0 + k == 0, stop_, w,
                                       inc)
                    if end and jb["bias"] is not None:
                        last = mm(out, jb["bias"][1], jb["bias"][0][:, o:o + n], False, True, inc=True)
                    toks.append((u, bi, out, last))
                hb[0].done(hi_, last)
                if end:
                    for u, bi, out, tok in toks:
                        if jb["moving"]:
                            pb.done(bi, *jb["evac"](o // P + u, 1, out.unsqueeze(1), tok))
                        else:
                            pb.done(bi, *jb["evac"](u, o, n, out, tok))
                    if o + n >= jb["N"] and jb["after"] is not None:
                        jb["after"]()

        def gemm_t(W, kchunks, N, x, ntok, evac, w, **kw):
            return job(W, kchunks, N, x, ntok, evac, w, True, **kw)

        def gemm_n(W, kchunks, N, x, tiles, evac, w, **kw):
            return job(W, kchunks, N, x, list(tiles), evac, w, False, **kw)

        def colsum(views, ntok, w):
            bi, bank, bw = pb.next()
            for i, v in enumerate(views):
                last = mm(bank[:, 0:ntok], ones, v, i == 0, i == len(views) - 1, list(w) + bw,
                          inc=i == len(views) - 1)
            return bi, bank[:, 0:ntok], last

        def rstd_of(out, src, scale, w):
            t = act(out, src, ACT.Sqrt, w, bias=eps, scale=scale)
            return rcp(out, out, [t]), t

        def rstd_t(x, ntok, sq, rs, w):
            bi, bank, bw = pb.next()
            for c in range(KC):
                if c % 2:
                    t = tt(sq[:, c, :], x[:, c, :], x[:, c, :], MUL, w)
                else:
                    t = act(sq[:, c, :], x[:, c, :], ACT.Square, w)
                last = mm(bank[:, 0:ntok], ones, sq[:, c, :], c == 0, c == KC - 1, [t] + bw, inc=c == KC - 1)
            r, t = rstd_of(rs, bank[:, 0:ntok], 1.0 / DM, [last])
            pb.done(bi, t)
            return r

        def rms_t(x, ntok, out, m, tmp, rs, w):
            t = rstd_t(x, ntok, tmp, rs, w)
            toks = []
            for c in range(KC):
                t = stt(out[:, c, :], x[:, c, :], m(c), rs, MUL, MUL, [t])
                toks.append([t])
            return toks

        def rms_split(x, ntok, high, low, parts_, sq, tmp, rs, w):
            r = rstd_t(x, ntok, sq, rs, w)
            toks = []
            for c in range(KC):
                for lo, hi, m, a in parts_:
                    o = tmp[:, c, lo:hi]
                    t = stt(o, x[:, c, lo:hi], m(c), rs[:, lo:hi], MUL, MUL, [r])
                    h, l = high[:, c, lo:hi], low[:, c, lo:hi]
                    if a is None:
                        t1 = act(h.bitcast(F32R), o, ACT.Copy, [t])
                        t2 = tt(l.bitcast(F32R), o, h, SUB, [t1])
                    else:
                        t1 = act(h.bitcast(F32R), o, ACT.Identity, [t], bias=a(c))
                        t2 = stt(l.bitcast(F32R), o, a(c), h, ADD, SUB, [t1])
                toks.append([t1, t2])
            return toks

        nsm = [0]

        def small(dst, src, w=()):
            nsm[0] += 16
            return E.dma("g", lambda e: e.dma_start(dst, src), s_small, nsm[0], list(w))

        E.dma("s", lambda e: e.dma_start(vec[:, :], A["vec"]), s_vec, 16)
        E.dma("s", lambda e: e.dma_start(row[:, :], A["row"]), s_vec, 32)
        ready = (s_vec, 32)
        for k in "vagp":
            put(k, lambda e: e.nop(), [ready])

        x = xr[:, :, T:2 * T]
        phase(6)
        room("f")
        xin = ar(2, DM)
        cin = ar(2, DM)
        E.dma("s", lambda e: e.dma_start(xin, A["x"][0].rearrange("(a p) d -> p a d", p=P)), s_x, 16)
        E.dma("s", lambda e: e.dma_start(cin, A["ctx_2"][0].rearrange("(a p) d -> p a d", p=P)), s_x, 32)
        for src, dst in ((xin, x), (cin, xr[:, :, 0:T])):
            for a in range(2):
                for c in range(0, KC, 4):
                    bi, bank, bw = pb.next()
                    for j in range(4):
                        last = tr(bank[:, j * P:(j + 1) * P], src[:, a, (c + j) * P:(c + j + 1) * P],
                                  bw + [(s_x, 32)], inc=j == 3)
                    pb.done(bi, cp(dst[:, c:c + 4, a * P:(a + 1) * P],
                                   bank[:, :].rearrange("p (a t) -> p a t", a=4), [last], k="a" if c else "v"))

        def fox():
            phase(6)
            room("r", 2 * KC * T + 2 * KC * P + 10 * SLOT // 2)
            xh, xl, wfh, wfl = ra(KC, T), ra(KC, T), ra(KC, P), ra(KC, P)
            pairs(5)
            room("f")
            H, dh = 16, 64
            W = A["fox_w_in"][0]
            xt = ar(KC, T)
            tmp = ar(KC, T)
            rs = ar(T)
            qt = ar(KC, T)
            kt = ar(KC, T)
            gt = ar(KC, T)
            v = ar(2, DM)
            cum = ar(T)
            ncum = ar(T)
            wf = ar(KC, P)
            zf = fill(wf, 0.0)
            for q0 in (0, 64):
                tf = small(wf[:, :, q0:q0 + H], W[:, 4 * DM:4 * DM + H].rearrange("(a p) n -> p a n", p=P), [zf])
            g = V("norm_mix")
            fw = split(wf, wfh, wfl, [tf])
            xtok = rms_split(x, T, xh, xl, [(0, T, lambda c: g[:, c:c + 1], None)], tmp, xt, rs, ())
            xw = lambda k: xtok[k]
            X = lambda k: (xh[:, k, :], xl[:, k, :])
            bi, bank, bw = pb.next()
            for k in range(KC):
                last = mm3(bank[:, 0:T], (wfh[:, k, :], wfl[:, k, :]), X(k), k == 0, k == KC - 1, xw(k) + bw + fw,
                           inc=k == KC - 1)
            z = ts(ncum[:, :], bank[:, 0:T], V("bf")[:, :], op0=ADD, w=[last])
            pb.done(bi, z)
            z = stt(cum[:, :], ncum[:, :], -1.0, ncum[:, :], MUL, MAX, [z])
            z = act(cum[:, :], cum[:, :], ACT.Exp, [z], scale=-1.0)
            z = act(cum[:, :], cum[:, :], ACT.Ln, [z], bias=ones[:, 0:1])
            z = stt(ncum[:, :], ncum[:, :], 0.0, cum[:, :], MIN, SUB, [z])
            z = scan(cum[:, :], bc(ones[:, 0:1], [P, T]), ncum[:, :], 0.0, MUL, ADD, [z])
            cw = ts(ncum[:, :], cum[:, :], -1.0, w=[z])

            gemm([gemm_t(W[:, 0:DM], KC, DM, X, T,
                         lambda j, n, ps, t: [act(qt[:, j:j + n, :], ps, ACT.Copy, [t], scale=dh ** -0.5)], xw),
                  gemm_t(W[:, DM:2 * DM], KC, DM, X, T,
                         lambda j, n, ps, t: [cp(kt[:, j:j + n, :], ps, [t], k="a")], xw),
                  gemm_n(W[:, 2 * DM:3 * DM], KC, DM,
                         lambda k, a: (xh[:, k, a * P:(a + 1) * P], xl[:, k, a * P:(a + 1) * P]), (0, 1),
                         lambda a, o, n, ps, t: [cp(v[:, a, o:o + n], ps, [t], k="a")], xw),
                  gemm_t(W[:, 3 * DM:4 * DM], KC, DM, X, T,
                         lambda j, n, ps, t: [act(gt[:, j:j + n, :], ps, ACT.Sigmoid, [t])], xw)])
            ot = xt
            st = [(tmp[:, 2 * i:2 * i + 2, :], tmp[:, 4 + 2 * i:6 + 2 * i, :]) for i in range(2)]
            bufs = Turns(st)
            mx = rs
            qkv = E.barrier()
            mask = vec[:, VEC["mask_z"][0]:VEC["mask_z"][0] + 2 * P]
            for qb in range(2):
                nh = 4 if qb == 0 else 2
                nk = P * (qb + 1)
                for h0 in [2 * nh * i + j for i in range(H // nh // 2) for j in range(2)]:
                    heads = [h0 + 2 * i for i in range(nh)]
                    bi, bank, bw = pb.next()
                    sv = bank[:, :].rearrange("p (h k) -> p h k", h=nh)
                    for i in range(nh):
                        h = heads[i]
                        q0 = 64 * (h % 2)
                        mm(sv[:, i, :], qt[q0:q0 + 64, h // 2, qb * P:(qb + 1) * P],
                           kt[q0:q0 + 64, h // 2, 0:nk], True, False, qkv + bw + [cw])
                        sel = ident[q0:q0 + H, q0 + h:q0 + h + 1]
                        mm(sv[:, i, :], sel.to_broadcast([H, P]), ncum[q0:q0 + H, 0:nk], False, False)
                        last = mm(sv[:, i, :], cum[q0:q0 + H, qb * P:(qb + 1) * P], sel.to_broadcast([H, nk]),
                                  False, True, inc=i == nh - 1)
                    ui, (sbuf_, pt), uw = bufs.next()
                    s = sbuf_.rearrange("p a t -> p (a t)").rearrange("p (h k) -> p h k", h=nh)
                    t = tt(s, sv, bc(mask[:, P - (nk - P):2 * P], [P, nh, nk], 1), ADD, [last] + uw)
                    pb.done(bi, t)
                    m = mx[:, 0:nh]
                    t = red(m, s, MAX, [t])
                    t = tt(s, s, bc(m, [P, nh, nk], 2), SUB, [t])
                    t = act(s, s, ACT.Exp, [t])
                    t = red(m, s, ADD, [t])
                    t = rcp(m, m, [t])
                    t = tt(s, s, bc(m, [P, nh, nk], 2), MUL, [t])
                    bi, bank, bw = pb.next()
                    sf = s.rearrange("p h k -> p (h k)")
                    for i in range(4):
                        last = tr(bank[:, i * P:(i + 1) * P], sf[:, i * P:(i + 1) * P], [t] + bw, inc=i == 3)
                    ptf = pt.rearrange("p a t -> p (a t)")
                    t = cp(ptf, bank[:, :], [last], k="a")
                    pb.done(bi, t)
                    bi, bank, bw = pb.next()
                    q0 = 64 * (h0 % 2)
                    for i, h in enumerate(heads):
                        for kb in range(qb + 1):
                            last = mm(bank[q0:q0 + 64, i * P:(i + 1) * P], v[:, kb, h * dh:(h + 1) * dh],
                                      ptf[:, (i * (qb + 1) + kb) * P:(i * (qb + 1) + kb + 1) * P],
                                      kb == 0, kb == qb, [t] + bw, inc=(i == nh - 1 and kb == qb),
                                      tile=(0, q0))
                    c0 = h0 // 2
                    t = tt(ot[q0:q0 + 64, c0:c0 + nh, qb * P:(qb + 1) * P],
                           bank[q0:q0 + 64, 0:nh * P].rearrange("p (a t) -> p a t", a=nh),
                           gt[q0:q0 + 64, c0:c0 + nh, qb * P:(qb + 1) * P], MUL, [last])
                    pb.done(bi, t)
                    bufs.done(ui, last)
            otok = [split(ot[:, k, :], xh[:, k, :], xl[:, k, :], [t]) for k in range(KC)]
            gemm([gemm_t(A["fox_w_out"][0], KC, DM, X, T,
                         lambda j, n, ps, tk: [tt(x[:, j:j + n, :], ps, x[:, j:j + n, :], ADD, [tk])], lambda k: otok[k])])

        def moe(L):
            phase(12)
            room("f")
            xt = ar(KC, T)
            tmp = ar(KC, T)
            rs = ar(T)
            xn = ar(2, DM)
            wr = ar(KC, 36)
            tw = small(wr, A["wr"][L])
            g = V("norm_ffn", 8 * L, 8)
            xw = rms_t(x, T, xt, lambda c: g[:, c:c + 1], tmp, rs, ())[-1]
            for a in range(2):
                for c in range(0, KC, 4):
                    bi, bank, bw = pb.next()
                    for j in range(4):
                        last = tr(bank[:, j * P:(j + 1) * P], xt[:, c + j, a * P:(a + 1) * P], xw + bw, inc=j == 3)
                    xnw = cp(xn[:, a, c * P:(c + 4) * P], bank[:, :], [last], k="a")
                    pb.done(bi, xnw)
            lg = ar(2, 36)
            bi, bank, bw = pb.next()
            rb, r1_ = R("br", 36 * L, 36)
            for a in range(2):
                for k in range(KC):
                    mm(bank[:, 36 * a:36 * a + 36], xt[:, k, a * P:(a + 1) * P], wr[:, k, :], k == 0, False,
                       xw + bw + [tw])
                last = mm(bank[:, 36 * a:36 * a + 36], r1_, rb, False, True, inc=a == 1)
            t = cp(lg, bank[:, 0:72].rearrange("p (a n) -> p a n", a=2), [last])
            pb.done(bi, t)

            def softmax(out, src, n, w):
                m = ar(2)
                t = red(m, src, MAX, w)
                t = tt(out, src, bc(m, [P, 2, n], 2), SUB, [t])
                t = act(out, out, ACT.Exp, [t])
                t = red(m, out, ADD, [t])
                t = rcp(m, m, [t])
                return tt(out, out, bc(m, [P, 2, n], 2), MUL, [t])

            def first_max(oh, val, src, n, w):
                c = ar(2, n)
                m = ar(2)
                t = red(val, src, MAX, w)
                t = tt(c, src, bc(val, [P, 2, n], 2), ALU.is_equal, [t])
                t = stt(c, c, -64.0, bc(V("iota", 0, n), [P, 2, n], 1), MUL, ADD, [t])
                t = red(m, c, MIN, [t])
                return tt(oh, c, bc(m, [P, 2, n], 2), ALU.is_equal, [t])

            pg, ohg, pgv = ar(2, 4), ar(2, 4), ar(2)
            t = softmax(pg, lg[:, :, 0:4], 4, [t])
            t = first_max(ohg, pgv, pg, 4, [t])
            big = ar(2, 4, 8)
            ein, oh1, oh2, m1, m2 = ar(2, 8), ar(2, 8), ar(2, 8), ar(2), ar(2)
            for a in range(2):
                t = tt(big[:, a], lg[:, a, 4:36].rearrange("p (g e) -> p g e", g=4),
                       bc(ohg[:, a], [P, 4, 8], 2), MUL, [t])
                t = red(ein[:, a, :], big[:, a].rearrange("p g e -> p e g"), ADD, [t])
            t = softmax(ein, ein, 8, [t])
            t = first_max(oh1, m1, ein, 8, [t])
            t = stt(ein, oh1, -2.0, ein, MUL, ADD, [t])
            t = first_max(oh2, m2, ein, 8, [t])
            r = ar(2)
            t = tt(r, m1, m2, ADD, [t])
            t = rcp(r, r, [t])
            t = tt(r, r, pgv, MUL, [t])
            t = tt(m1, m1, r, MUL, [t])
            t = tt(m2, m2, r, MUL, [t])
            sel8, gat8 = ar(2, 8), ar(2, 8)
            t = tt(sel8, oh1, oh2, ADD, [t])
            t = tt(oh1, oh1, bc(m1, [P, 2, 8], 2), MUL, [t])
            t = tt(oh2, oh2, bc(m2, [P, 2, 8], 2), MUL, [t])
            t = tt(gat8, oh1, oh2, ADD, [t])
            sel, px, gx = ar(2, NE), ar(2, NE + NX), ar(2, NE + NX)
            for a in range(2):
                t = tt(sel[:, a, :].rearrange("p (g e) -> p g e", g=4), bc(ohg[:, a], [P, 4, 8], 2),
                       bc(sel8[:, a], [P, 4, 8], 1), MUL, [t])
                t = tt(gx[:, a, 0:NE].rearrange("p (g e) -> p g e", g=4), bc(ohg[:, a], [P, 4, 8], 2),
                       bc(gat8[:, a], [P, 4, 8], 1), MUL, [t])
            bi, bank, bw = pb.next()
            mm(bank[:, 0:NE], V("tri"), sel[:, 0, :], True, True, [t] + bw)
            mm(bank[:, NE:2 * NE], ones, sel[:, 0, :], True, False)
            mm(bank[:, NE:2 * NE], V("tri"), sel[:, 1, :], False, True)
            mm(bank[:, 2 * NE:3 * NE], ones, sel[:, 0, :], True, False)
            last = mm(bank[:, 2 * NE:3 * NE], ones, sel[:, 1, :], False, True, inc=True)
            pos1, cnt, nb, pre = ar(2, NE), ar(NE), ar(NE), ar(NE)
            t = stt(pos1, bank[:, 0:2 * NE].rearrange("p (a n) -> p a n", a=2), 1.0, sel, ADD, MUL, [last])
            t = cp(cnt, bank[:, 2 * NE:3 * NE], [t])
            pb.done(bi, t)
            t = ts(px[:, :, 0:NE], pos1, -1.0, op0=ADD, w=[t])
            routed = t

            nx_ = dict(ohj=ar(NX, NE), ohk=ar(NX, NE), off=ar(NX), ids=ar(2, NX + 1))

            def further():
                t = routed
                t = ts(nb, cnt, SL + 0.5, op0=ALU.is_gt, w=[t])
                for i in range(2, T // SL):
                    t = stt(nb, cnt, i * SL + 0.5, nb, ALU.is_gt, ADD, [t])
                t = scan(pre, bc(ones[:, 0:1], [P, NE]), nb, 0.0, MUL, ADD, [t])
                ohj, ohk, off, ids = nx_["ohj"], nx_["ohk"], nx_["off"], nx_["ids"]
                jota = bc(V("jota"), [P, NX, NE], 2)
                t = tt(ohk, bc(pre, [P, NX, NE], 1), jota, ALU.is_gt, [t])
                t = tt(pre, pre, nb, SUB, [t])
                t = tt(ohj, bc(pre, [P, NX, NE], 1), jota, ALU.is_le, [t])
                t = tt(ohj, ohj, ohk, MUL, [t])
                t = tt(ohk, ohj, bc(pre, [P, NX, NE], 1), MUL, [t])
                t = red(off, ohk, ADD, [t])
                t = tt(off, V("jota"), off, SUB, [t])
                t = ts(off, off, float(SL), SL + 1.0, MUL, ADD, [t])
                t = tt(ohk, ohj, bc(V("iota", 0, NE), [P, NX, NE], 1), MUL, [t])
                t = red(ids[:, 0, 0:NX], ohk, ADD, [t])
                t = red(ids[:, 1, 0:NX], ohj, ADD, [t])
                t = red(ids[:, 0, NX:], nb, ADD, [t])
                t = red(ids[:, 1, NX:], nb, ADD, [t])
                for a in range(2):
                    t = tt(ohk, ohj, bc(pos1[:, a], [P, NX, NE], 1), MUL, [t])
                    t = red(px[:, a, NE:], ohk, ADD, [t])
                    t = tt(px[:, a, NE:], px[:, a, NE:], off, SUB, [t])
                    t = tt(ohk, ohj, bc(gx[:, a, 0:NE], [P, NX, NE], 1), MUL, [t])
                    t = red(gx[:, a, NE:], ohk, ADD, [t])
                tid = cp(eid[0:1, 0:2 * NX + 2], ids[0:1].rearrange("p a n -> p (a n)"), [t])
                return tid

            hold = back_to(0)
            xg_b = Turns([ar(KC, GB, SL) for _ in range(2)])
            back_to(hold)
            dt_b = Turns([ar(GB, T) for _ in range(2)])
            d_t = ar(2, GB, SL)
            dg_t = ar(2, GB, 4, SL)
            hs_b = Turns([ar(256) for _ in range(2)])
            ht_b = Turns([ar(2, 2, SL) for _ in range(2)])
            y_b = Turns([ar(256) for _ in range(2)])
            NB = NE + NX
            acc = banks[0:4]
            accw = [fill(acc[i][:, :], 0.0, pb.free[i]) for i in range(4)]
            pq = Turns(banks[4:8])
            pq.free = [list(pb.free[i]) for i in range(4, 8)]
            group = {}
            used = {"d": [], "g": []}

            def prepare(q):
                n = min(GB, NB - GB * q)
                dw, gw = [], []
                for a in range(2):
                    t = tt(d_t[:, a, 0:n, :], bc(V("iota", 0, SL), [P, n, SL], 1),
                           bc(px[:, a, GB * q:GB * q + n], [P, n, SL], 2), ALU.is_equal, [routed] + used["d"])
                    dw.append(t)
                for a in range(2):
                    gw.append(tt(dg_t[:, a, 0:n], bc(d_t[:, a, 0:n], [P, n, 4, SL], 2),
                                 bc(gx[:, a, GB * q:GB * q + n], [P, n, 4, SL], 2, 3), MUL, dw + used["g"]))
                xi, xg, xgw = xg_b.next()
                evs = []
                for c in range(0, KC, 2):
                    bi, bank, bw = pq.next()
                    for j in range(2):
                        for a in range(2):
                            last = mm(bank[:, j * T:j * T + n * SL], xn[:, a, (c + j) * P:(c + j + 1) * P],
                                      d_t[:, a, 0:n, :], a == 0, a == 1, dw + bw + [xnw], inc=(j == 1 and a == 1))
                    e = cp(xg[:, c:c + 2, 0:n, :],
                           bank[:, :].rearrange("p (a b s) -> p a b s", a=2, b=GB)[:, :, 0:n, :],
                           [last] + xgw, k="a" if c % 4 else "v")
                    evs.append(e)
                    pq.done(bi, e)
                used["d"] = [last]
                di, dt_, dtw = dt_b.next()
                dte = []
                for b in range(0, n, 2):
                    m = min(2, n - b)
                    bi, bank, bw = pq.next()
                    for j in range(m):
                        for a in range(2):
                            last = tr(bank[:, j * T + a * P:j * T + (a + 1) * P],
                                      dg_t[:, a, b + j].rearrange("p d s -> p (d s)"), gw + bw,
                                      inc=(j == m - 1 and a == 1))
                    e = cp(dt_[:, b:b + m, :], bank[:, 0:m * T].rearrange("p (a t) -> p a t", a=m), [last] + dtw,
                           k="v" if b % 4 else "a")
                    dte.append(e)
                    pq.done(bi, e)
                used["g"] = [last]
                group[q] = (xi, xg, evs, di, dt_, dte)

            info = {}

            def up(b):
                if b < NE:
                    gu = [wload(A["expert_w_gu"][L, b, k * 256:(k + 1) * 256, :], 2, DM) for k in range(4)]
                    dn = [wload(A["expert_w_down"][L, b, k * 256:(k + 1) * 256, :], 2, DM) for k in range(2)]
                xi, xg, evs, *_ = group[b // GB]
                bi, bank, bw = pq.next()
                for k in range(KC):
                    if b >= NE and k % 2 == 0:
                        sl = xload(A["expert_w_gu"][L], b - NE, k * P)
                    elif k % 2 == 0:
                        sl = gu[k // 2]
                    for h in range(4):
                        last = mm(bank[32 * h:32 * h + 32, 0:256], xg[:, k, b % GB, :],
                                  sl[1][:, k % 2, 256 * h:256 * h + 256], k == 0, k == KC - 1,
                                  evs + bw + [sl[2]], inc=(k % 2 == 1 and h == 3), tile=(0, 32 * h))
                    if k % 2 == 1:
                        (wfree if b < NE else xfree)([sl], last)
                xg_b.done(xi, last)
                hi, hs, hw = hs_b.next()
                t = act(hs[0:64, :], bank[0:64, 0:256], ACT.Silu, [last] + hw)
                t = tt(hs[0:64, :], hs[0:64, :], bank[64:128, 0:256], MUL, [t])
                pq.done(bi, t)
                info[b] = dict(dn=dn if b < NE else None, hs=hs, hi=hi, t=t)

            def across(b):
                f = info[b]
                bi, bank, bw = pq.next()
                for k in range(2):
                    last = tr(bank[:, k * 64:(k + 1) * 64], f["hs"][0:64, k * P:(k + 1) * P], [f["t"]] + bw, inc=k == 1)
                hs_b.done(f["hi"], last)
                hi, ht, hw = ht_b.next()
                t = cp(ht, bank[:, 0:128].rearrange("p (k h s) -> p k h s", k=2, h=2), [last] + hw, k="a")
                pq.done(bi, t)
                f.update(ht=ht, hti=hi, t=t)

            def down(b):
                f = info[b]
                bi, bank, bw = pq.next()
                for k in range(4):
                    if b >= NE and k % 2 == 0:
                        sl = xload(A["expert_w_down"][L], b - NE, k * P)
                    elif k % 2 == 0:
                        sl = f["dn"][k // 2]
                    for h in range(4):
                        last = mm(bank[32 * h:32 * h + 32, 0:256], f["ht"][:, k % 2, k // 2, :],
                                  sl[1][:, k % 2, 256 * h:256 * h + 256], k == 0, k == 3,
                                  [f["t"]] + bw + [sl[2]], inc=(k % 2 == 1 and h == 3), tile=(0, 32 * h))
                    if k % 2 == 1:
                        (wfree if b < NE else xfree)([sl], last)
                ht_b.done(f["hti"], last)
                yi, y, yw = y_b.next()
                t = cp(y, bank[:, 0:256], [last] + yw)
                pq.done(bi, t)
                f.update(y=y, yi=yi, t=t)

            def back(b):
                f = info.pop(b)
                _, _, _, di, dt_, dte = group[b // GB]
                for j in range(2):
                    for h in range(4):
                        last = mm(acc[h][:, j * T:(j + 1) * T], f["y"][32 * h:32 * h + 32, j * P:(j + 1) * P],
                                  dt_[32 * h:32 * h + 32, b % GB, :], False, True,
                                  [f["t"]] + dte + accw, inc=(j == 1 and h == 3), tile=(32 * h, 0), skip=True)
                y_b.done(f["yi"], last)
                dt_b.done(di, last)
                return last

            prepare(0)
            for b in range(NE + 2):
                if b < NE:
                    up(b)
                if b == 1:
                    tid = further()
                if b % GB == 5 and b // GB + 1 < NE // GB:
                    prepare(b // GB + 1)
                if 1 <= b <= NE:
                    across(b - 1)
                if b >= 2:
                    last = back(b - 2)
                if 1 <= b <= NE:
                    down(b - 1)
            before = last
            xr_ = {"n": 0, "slots": [(wt["n"] - 3 + i) % wt["use"] for i in range(3)]}
            xat = list(xcount)

            def xload(src, j, k0):
                c = xr_["n"] % 3
                i = xr_["slots"][c]
                xr_["n"] += 1
                xcount[c] += 1
                dst = slot_at(i, 2, DM)

                def go(e):
                    v, ok = idv[j]
                    s = src[bass.ds(v, 1), k0:k0 + 256, :].rearrange("o (a p) n -> p (o a) n", p=P)
                    return e.dma_start(dst, s, cond=ok)
                tok = E.dma("s", go, x_sem[c], 16 * xcount[c], wt["free"][i])
                wt["free"][i] = []
                return i, dst, tok

            xfree = wfree
            E.branch(eid[0:1, NX:NX + 1], tid)
            E.put("s", load_ids, inc=False)
            for b in range(NE, NB):
                if b % GB == 0:
                    prepare(b // GB)
                up(b)
                across(b)
                down(b)
                last = back(b)
            E.join([(x_sem[c], 16 * xat[c], 16 * (xcount[c] - xat[c])) for c in range(3)])
            ends = []
            for i in range(4):
                ends.append(tt(x[:, 2 * i:2 * i + 2, :], acc[i][:, :].rearrange("p (a t) -> p a t", a=2),
                               x[:, 2 * i:2 * i + 2, :], ADD, [before, last]))
            for i in range(4):
                pb.free[i] = [ends[i]]
                pb.free[4 + i] = pq.free[i]

        xcount = [0, 0, 0]
        idv = {}

        def load_ids(e):
            for j in range(NX):
                idv[j] = (e.value_load(eid[0:1, j:j + 1], min_val=0, max_val=NE - 1),
                          e.value_load(eid[0:1, NX + 1 + j:NX + 2 + j], min_val=0, max_val=1))
            return None

        def ret():
            phase(6)
            room("r", 2 * 16 * T + 4 * SLOT)
            gth, gtl = ra(16, T), ra(16, T)
            xh, xl = gth[:, 0:KC, :], gtl[:, 0:KC, :]
            pairs(4)
            room("f")
            W = A["ret_w_in"][0]
            tmp = ar(KC, T)
            rs = ar(T)
            qt, kt = ar(4, 2, T), ar(4, 2, T)
            v = ar(2, 2048)
            gt = ar(16, T)
            X = lambda k: (xh[:, k, :], xl[:, k, :])
            g = V("norm_mix", 8, 8)
            xtok = rms_split(x, T, xh, xl, [(0, T, lambda c: g[:, c:c + 1], None)], tmp,
                             gt[:, 0:KC, :], rs, ())
            xw = lambda k: xtok[k]
            qf, kf = qt.rearrange("p h c t -> p (h c) t"), kt.rearrange("p h c t -> p (h c) t")
            t4 = tmp.rearrange("p (a h) t -> p a h t", a=2)
            cosb, sinb = bc(V("cos"), [P, 4, T], 1), bc(V("sin"), [P, 4, T], 1)

            def rotate(m):
                done = [(E.sem["a"], E.n["a"])]
                a, b = m[:, :, 0, :], m[:, :, 1, :]
                t = tt(t4[:, 0], a, sinb, MUL, done)
                t = tt(t4[:, 1], b, sinb, MUL, [t])
                t = tt(a, a, cosb, MUL, [t])
                t = tt(b, b, cosb, MUL, [t])
                t = tt(a, a, t4[:, 1], SUB, [t])
                tt(b, b, t4[:, 0], ADD, [t])

            gemm([gemm_t(W[:, 0:DM], KC, DM, X, T,
                         lambda j, n, ps, t: [cp(qf[:, j:j + n, :], ps, [t], k="a")], xw, after=lambda: rotate(qt)),
                  gemm_t(W[:, DM:2 * DM], KC, DM, X, T,
                         lambda j, n, ps, t: [act(kf[:, j:j + n, :], ps, ACT.Copy, [t], scale=1.0 / 16)], xw,
                         after=lambda: rotate(kt)),
                  gemm_n(W[:, 2 * DM:4 * DM], KC, 2048,
                         lambda k, a: (xh[:, k, a * P:(a + 1) * P], xl[:, k, a * P:(a + 1) * P]), (0, 1),
                         lambda a, o, n, ps, t: [cp(v[:, a, o:o + n], ps, [t], k="a")], xw),
                  gemm_t(W[:, 4 * DM:6 * DM], KC, 2048, X, T,
                         lambda j, n, ps, t: [act(gt[:, j:j + n, :], ps, ACT.Silu, [t])], xw)])
            done = E.barrier()
            rot = None
            dec = V("dec").rearrange("p (h t) -> p h t", h=4)
            sts = Turns([ar(384) for _ in range(2)])
            o_b = tmp[:, 0:4, :]
            sq = tmp[:, 4:8, :]
            gn = V("gn")
            tsq = None
            for h in range(4):
                bi, bank, bw = pb.next()
                for c in range(2):
                    mm(bank[:, 0:T], kt[:, h, c, 0:P], qt[:, h, c, :], c == 0, c == 1, done + bw + [rot])
                for c in range(2):
                    last = mm(bank[:, T:T + P], kt[:, h, c, P:T], qt[:, h, c, P:T], c == 0, c == 1, inc=c == 1)
                si, s, sw = sts.next()
                t = tt(s[:, 0:T], bank[:, 0:T], dec[:, h, :], MUL, [last] + sw)
                t = tt(s[:, T:T + P], bank[:, T:T + P], dec[:, h, 0:P], MUL, [t])
                pb.done(bi, t)
                for e in range(0, 4, 2):
                    bi, bank, bw = pb.next()
                    for j in range(2):
                        o = h * 512 + (e + j) * P
                        mm(bank[:, j * T:j * T + P], v[:, 0, o:o + P], s[:, 0:P], True, True, [t] + bw)
                        mm(bank[:, j * T + P:(j + 1) * T], v[:, 0, o:o + P], s[:, P:T], True, False)
                        last = mm(bank[:, j * T + P:(j + 1) * T], v[:, 1, o:o + P], s[:, T:T + P], False, True,
                                  inc=j == 1)
                    to = cp(o_b[:, e:e + 2, :], bank[:, :].rearrange("p (a t) -> p a t", a=2), [last, tsq], k="a")
                    pb.done(bi, to)
                sts.done(si, last)
                bi, ps, tok = colsum([o_b[:, e, :] for e in range(4)], T, [to])
                for e in range(4):
                    t = stt(o_b[:, e, :], ps, -1.0 / 512, o_b[:, e, :], MUL, ADD, [tok])
                pb.done(bi, t)
                tq = act(sq, o_b, ACT.Square, [t])
                bi, ps, tok = colsum([sq[:, e, :] for e in range(4)], T, [tq])
                r, ta = rstd_of(rs, ps, 1.0 / 512, [tok])
                pb.done(bi, ta)
                t = tt(o_b, o_b, bc(rs, [P, 4, T], 1), MUL, [r])
                for e in range(4):
                    j = 4 * h + e
                    tsq = stt(gt[:, j, :], o_b[:, e, :], gn[:, j:j + 1], gt[:, j, :], MUL, MUL, [t])
                hs = slice(4 * h, 4 * h + 4)
                split(gt[:, hs, :], gth[:, hs, :], gtl[:, hs, :], [tsq])
            gemm([gemm_t(A["ret_w_out"][0], 16, DM, lambda k: (gth[:, k, :], gtl[:, k, :]), T,
                         lambda j, n, ps, tk: [tt(x[:, j:j + n, :], ps, x[:, j:j + n, :], ADD, [tk])],
                         [(E.sem["v"], E.n["v"])])])

        def second(L):
            phase(10)
            room("f")
            last_layer = L == 1
            lo = T if last_layer else 0
            mod = mods[:, 0:96].rearrange("p (c v) -> p c v", v=2)
            gm = mods[:, 96:128].rearrange("p (i c v) -> p i c v", i=2, c=8)
            cs = ar(KC, 32)
            mrow = ar(512)
            mrow2 = ar(512)
            t = fill(cs, 0.0)
            t = act(cs[:, :, 0], V("cc"), ACT.Silu, [t])
            t = act(cs[:, :, 1], V("c"), ACT.Silu, [t])
            sel2 = ar(2)
            ts_ = red(sel2, ident.rearrange("p (a b) -> p b a", a=4)[:, 0:2, :], ADD)
            mbank, mw = banks[0], pb.free[0]
            pm = Turns(banks[1:])
            pm.free = pb.free[1:]
            rows = Turns([mrow, mrow2])
            for o in range(0, 6 * DM, 512):
                slots = [wload(A["w_mod_2"][L, g * 512:(g + 1) * 512, o:o + 512], 4, 512) for g in range(2)]
                bi, bank, bw = pm.next()
                for g in range(2):
                    for c in range(4):
                        last = mm(bank[32 * c:32 * c + 32, :], cs[:, 4 * g + c, :], slots[g][1][:, c, :], g == 0, g == 1,
                                  [t, slots[g][2]] + bw, inc=(g == 1 and c == 3), tile=(0, 32 * c))
                wfree(slots, last)
                ri, rr, rw = rows.next()
                tr_ = cp(rr, bank[:, :], [last] + rw, k="a")
                pm.done(bi, tr_)
                for j in range(4):
                    c = o // P + j
                    last = mm(mbank[:, 2 * c:2 * c + 2], rr[:, j * P:(j + 1) * P], sel2, True, True,
                              [tr_, ts_] + mw, inc=j == 3)
                rows.done(ri, last)
            t = tt(mod, mbank[:, 0:96].rearrange("p (c v) -> p c v", v=2), bc(V("b_mod", 48 * L, 48), [P, 48, 2], 2),
                   ADD, [last])
            pb.free[0] = [t]
            pb.free[1:] = pm.free
            for i, (nm, sc) in enumerate((("norm1", 8), ("norm2", 32))):
                t = stt(gm[:, i], mod[:, sc:sc + 8, :], 1.0, bc(V(nm, 8 * L, 8), [P, 8, 2], 2), ADD, MUL, [t])
            modw = t
            phase(4)
            room("r", 2 * KC * 2 * T)
            xh, xl = ra(KC, 2 * T), ra(KC, 2 * T)

            def parts(i, sh, lo_):
                out = []
                for v_, a, b in ((0, 0, T), (1, T, 2 * T)):
                    if a >= lo_:
                        out.append((a, b, lambda c, v_=v_: gm[:, i, c, v_:v_ + 1],
                                    lambda c, v_=v_: mod[:, sh + c, v_:v_ + 1]))
                return out

            def residual(g0, lo_):
                def ev(j, n, ps, tk):
                    for i in range(n):
                        for v_, a, b in ((0, 0, T), (1, T, 2 * T)):
                            if a >= lo_:
                                t = stt(xr[:, j + i, a:b], ps[:, i, a - lo_:b - lo_], mod[:, g0 + j + i, v_:v_ + 1],
                                        xr[:, j + i, a:b], MUL, ADD, [tk])
                    return [t]
                return ev

            room("f", F_LONG)
            yt = ar(KC, 2 * T)
            rs = ar(2 * T)
            sq_, tm_ = yt, ar(KC, 2 * T, at=KC * 2 * T + 2 * T)
            xtok = rms_split(xr[:, :, :], 2 * T, xh, xl, parts(0, 0, 0), sq_, tm_, rs, [modw])
            xw = lambda k: xtok[k]
            W = A["w_in_2"][L]
            X = lambda k: (xh[:, k, :], xl[:, k, :])
            XL = lambda k: (xh[:, k, lo:], xl[:, k, lo:])
            XN = lambda k, a: (xh[:, k, a * P:(a + 1) * P], xl[:, k, a * P:(a + 1) * P])
            nq = 2 * T - lo
            tiles = range(lo // P, 4)
            bcv = V("bc", 4 * L, 4)
            bu = V("bu", 2 * L, 2)
            early = KC * 2 * T + 2 * T
            cva, cvg, ut, sv = ar(2, 2 * T), ar(2, 2 * T), ar(2, 2 * T), ar(4, 256)
            lngb, wst = ar(2, 256), ar(4, P)
            st6, mv, sr = ar(4, 6), ar(4, 2), ar(4)
            qt, kt = ar(4, 2 * T), ar(4, 2 * T)
            vn = ar(4, 4, 129)
            on = ar(4, 512)
            graw = ar(2 * T)
            g_in, g_f = ar(2 * T), ar(2 * T)
            bks = ar(4)
            n_rooms = room("r")
            pairs(4)
            jobs = [
                gemm_t(W[:, 2576:2832], KC, 256, XL, nq,
                       lambda j, n, ps, tk: [act(cva[:, j + i, lo:], ps[:, i, :], ACT.Identity, [tk],
                                                 bias=bcv[:, j + i:j + i + 1]) for i in range(n)], xw, wide=256),
                gemm_t(W[:, 2832:3088], KC, 256, XL, nq,
                       lambda j, n, ps, tk: [act(cvg[:, j + i, lo:], ps[:, i, :], ACT.Sigmoid, [tk],
                                                 bias=bcv[:, 2 + j + i:3 + j + i]) for i in range(n)], xw, wide=256,
                       after=lambda: convolve())]
            conv_out = {}

            def convolve():
                after_conv_in = [(E.sem["a"], E.n["a"])]
                cw = V("conv_w", 62 * L, 62).rearrange("p (c k) -> p c k", c=2)
                cb = V("conv_b", 2 * L, 2)
                pads = yt.rearrange("p a t -> p (a t)")
                t = fill(pads[:, 0:286 * 2 + 376 + 640], 0.0, after_conv_in)
                t = tt(cva[:, :, lo:], cva[:, :, lo:], cvg[:, :, lo:], MUL, [t])
                ct = cvg
                o1 = 572
                px0 = pads[:, o1:o1 + 376].rearrange("p (r c) -> p r c", r=4)
                px1 = pads[:, o1 + 376:o1 + 376 + 640]
                t = cp(px0[:, :, 15:79], cva[:, 0, T:].rearrange("p (r c) -> p r c", r=4), [t])
                t = cp(px1[:, 192:448], cva[:, 1, T:], [t])
                if not last_layer:
                    pc = pads[:, 0:572].rearrange("p (c t) -> p c t", c=2)
                    t = cp(pc[:, :, 15:271], cva[:, :, 0:T], [t])
                    for c in range(2):
                        o = ct[:, c, 0:T]
                        t = ts(o, pc[:, c, 0:T], cw[:, c, 0:1], cb[:, c:c + 1], MUL, ADD, [t])
                        for k in range(1, 31):
                            t = stt(o, pc[:, c, k:k + T], cw[:, c, k:k + 1], o, MUL, ADD, [t])
                o = ct[:, 0, T:].rearrange("p (r c) -> p r c", r=4)
                t = ts(o, px0[:, :, 0:64], cw[:, 0, 0:1], cb[:, 0:1], MUL, ADD, [t])
                for k in range(1, 31):
                    t = stt(o, px0[:, :, k:k + 64], cw[:, 0, k:k + 1], o, MUL, ADD, [t])
                o = ct[:, 1, T:]
                t = ts(o, px1[:, 0:T], cw[:, 1, 12:13], cb[:, 1:2], MUL, ADD, [t])
                for d in range(1, 7):
                    t = stt(o, px1[:, 64 * d:64 * d + T], cw[:, 1, 12 + d:13 + d], o, MUL, ADD, [t])
                conv_out["t"] = t

            tv = fill(vn[:, :, :, 128:129], 1.0, k="g")
            bq, bk = V("bq", 4 * L, 4), V("bk", 4 * L, 4)
            tbk = act(bks, bk, ACT.Copy, scale=128 ** -0.5)
            jobs += [
                gemm_t(W[:, 2064:2320], KC, 256, XL, nq,
                       lambda j, n, ps, tk: [act(ut[:, j + i, lo:], ps[:, i, :], ACT.Gelu_apprx_tanh, [tk],
                                                 bias=bu[:, j + i:j + i + 1]) for i in range(n)], xw, wide=256),
                gemm_n(W[:, 2320:2576], KC, 256, XN, tiles,
                       lambda a, o, n, ps, tk: [act(sv[:, a, :], ps, ACT.Gelu_apprx_tanh, [tk])],
                       xw, bias=R("bs", 256 * L, 256), wide=256),
                gemm_t(W[:, 0:512], KC, 512, XL, nq,
                       lambda j, n, ps, tk: [act(qt[:, j + i, lo:], ps[:, i, :], ACT.Identity, [tk],
                                                 bias=bq[:, j + i:j + i + 1]) for i in range(n)], xw),
                gemm_t(W[:, 512:1024], KC, 512, X, 512,
                       lambda j, n, ps, tk: [act(kt[:, j, :], ps[:, 0, :], ACT.Identity, [tk, tbk],
                                                 bias=bks[:, j:j + 1], scale=128 ** -0.5)], xw),
                gemm_n(W[:, 1024:1536], KC, 512, XN, range(4),
                       lambda a, o, n, ps, tk: [cp(vn[:, a, :, 0:P], ps.rearrange("p (h d) -> p h d", h=4), [tk, tv],
                                                   k="a")],
                       xw, bias=R("bv", 512 * L, 512)),
                gemm_n(W[:, 1536:2048], KC, 512, XN, tiles,
                       lambda a, o, n, ps, tk: [act(on[:, a, :], ps, ACT.Sigmoid, [tk])],
                       xw, bias=R("bo", 512 * L, 512)),
                gemm_t(W[:, 2048:2064], KC, 16, X, 512,
                       lambda j, n, ps, tk: [act(graw[0:16, :], ps[:, 0, :], ACT.Identity, [tk],
                                                 bias=V("bg", L, 1)[0:16, :])], xw, wide=256)]
            gemm(jobs)
            ct = cvg
            t = (E.sem["a"], E.n["a"])
            for j in range(4):
                q0 = 32 * (j // 2)
                bi, bank, bw = pb.next()
                last = mm(bank[q0:q0 + 4, :], ident[0:16, 4 * j:4 * j + 4], graw[0:16, :], True, True, [t] + bw,
                          inc=True, tile=(0, q0))
                pb.done(bi, cp((g_f if j % 2 else g_in)[q0:q0 + 4, :], bank[q0:q0 + 4, :], [last], k="a"))
            done = E.barrier()
            all_wait(done)
            shut(n_rooms - 1)
            hold = back_to(early)
            rows5 = [ar(2 * T) for _ in range(5)]
            cn = ar(2, 4, 129)
            dts = Turns([ar(4, P) for _ in range(2)])
            back_to(hold)
            room("f")
            kn = ar(4, 4, P)
            hn = ar(4, 512)
            for a in range(4):
                bi, bank, bw = pb.next()
                for h in range(4):
                    last = tr(bank[:, h * P:(h + 1) * P], kt[:, h, a * P:(a + 1) * P], done + bw, inc=h == 3)
                knw = cp(kn[:, a], bank[:, :].rearrange("p (h d) -> p h d", h=4), [last], k="a")
                pb.done(bi, knw)

            w_ = nq
            bi, ps, tok = colsum([ct[:, c, lo:] for c in range(2)], w_, [conv_out["t"]])
            for c in range(2):
                t = stt(ct[:, c, lo:], ps, -1.0 / 256, ct[:, c, lo:], MUL, ADD, [tok])
            pb.done(bi, t)
            tq = act(cva[:, :, lo:], ct[:, :, lo:], ACT.Square, [t])
            bi, ps, tok = colsum([cva[:, c, lo:] for c in range(2)], w_, [tq])
            r, ta = rstd_of(rs[:, lo:], ps, 1.0 / 256, [tok])
            pb.done(bi, ta)
            t = tt(ct[:, :, lo:], ct[:, :, lo:], bc(rs[:, lo:], [P, 2, w_], 1), MUL, [r])
            lg_, lb_ = V("cln_g", 2 * L, 2), V("cln_b", 2 * L, 2)
            for c in range(2):
                t = act(yt[:, 6 + c, lo:], ct[:, c, lo:], ACT.Silu, [t], bias=lb_[:, c:c + 1], scale=lg_[:, c:c + 1])

            small(lngb[:, 0, :], A["sgu_ln_g_2"][L:L + 1, :].to_broadcast([P, 256]))
            small(lngb[:, 1, :], A["sgu_ln_b_2"][L:L + 1, :].to_broadcast([P, 256]))
            tl = small(wst, A["sgu_wt"][L])
            for a in tiles:
                ia = sv[:, a, :]
                oa = st6[:, a, :]
                ma = mv[:, a, :]
                t = put("v", lambda e, o=oa, i=ia: e.bn_stats(o, i), [tl])
                t = put("v", lambda e, o=ma, i=oa: e.bn_aggr(o, i), [t])
            r0, r1 = lo // P, 4
            r, _ = rstd_of(sr[:, r0:r1], mv[:, r0:r1, 1], 1.0, [t])
            for a in tiles:
                t = ts(sv[:, a, :], sv[:, a, :], mv[:, a, 0:1], sr[:, a:a + 1], SUB, MUL, [r])
            n_ = r1 - r0
            t = tt(sv[:, r0:r1, :], sv[:, r0:r1, :], bc(lngb[:, 0, :], [P, n_, 256], 1), MUL, [t])
            t = tt(sv[:, r0:r1, :], sv[:, r0:r1, :], bc(lngb[:, 1, :], [P, n_, 256], 1), ADD, [t])
            for c in range(2):
                bi, bank, bw = pb.next()
                for a in tiles:
                    for g in (2 * c, 2 * c + 1):
                        q0 = 64 * (g % 2)
                        o = bank[q0:q0 + 64, (a - r0) * P:(a - r0 + 1) * P]
                        mm(o, sv[:, a, g * 64:(g + 1) * 64], wst[:, g, :], True, False, [t] + bw, tile=(0, q0))
                        last = mm(o, R("sgub")[1][:, 0:64], R("sgub", 512 * L + g * P, P)[0], False, True,
                                  inc=(a == 3 and g % 2 == 1), tile=(96, q0))
                pb.done(bi, tt(yt[:, 4 + c, lo:], ut[:, c, lo:], bank[:, 0:w_], MUL, [last]))

            all_wait(E.barrier())
            gates = {}
            zero = V("zero")
            emt = ar(32)

            for d in range(2):
                q0 = 32 * d
                fi = g_f[q0:q0 + 4, :]
                ii = g_in[q0:q0 + 4, :]
                B, U, NM, WI, MT = (r_[q0:q0 + 4, :] for r_ in rows5)
                on4 = ones[q0:q0 + 4, 0:1]
                t = stt(B, fi, -1.0, fi, MUL, MAX)
                t = act(B, B, ACT.Exp, [t], scale=-1.0)
                t = act(B, B, ACT.Ln, [t], bias=on4)
                t = stt(fi, fi, 0.0, B, MIN, SUB, [t])
                prev = zero[q0:q0 + 4, 0:1]
                for a in ((0, 1, 2, 3) if d == 0 else (1, 0, 3, 2)):
                    s0, s1 = a * P, (a + 1) * P
                    if d == 0:
                        view = slice(s0, s1)
                    else:
                        view = slice(s1 - 1, s0 - 1 if s0 else None, -1)
                    le = s1 - 1 if d == 0 else s0
                    t = scan(B[:, view], bc(on4, [4, P]), fi[:, view], 0.0, MUL, ADD, [t])
                    t = tt(U[:, s0:s1], ii[:, s0:s1], B[:, s0:s1], SUB, [t])
                    t = scan(MT[:, view], U[:, view], U[:, view], prev, MAX, MAX, [t])
                    t = ts(NM[:, s0:s1], MT[:, s0:s1], -1.0, w=[t])
                    t = ts(WI[:, s0:s1], MT[:, s0:s1], -1.0, prev, MUL, ADD, [t])
                    t = tt(MT[:, s0:s1], MT[:, s0:s1], B[:, s0:s1], ADD, [t])
                    prev = MT[:, le:le + 1]
                pm, pmb, pmw = pb.next()
                for a in range(4):
                    mtw = mm(pmb[:, 4 * a:4 * a + 4], MT[:, a * P:(a + 1) * P], ident[q0:q0 + 4, q0:q0 + 4],
                             True, True, [t] + pmw, inc=True)
                te = act(emt[:, 16 * d:16 * d + 16], pmb[:, 0:16], ACT.Exp, [mtw], scale=-1.0)
                pb.done(pm, te)
                gates[d] = (U, NM, WI, t)
            cnw = fill(cn, 0.0)
            wb, qs, st_, ks = ar(4, P), ar(4, P), ar(4, P), ar(4, P)
            rd = ar(4)
            masks = (V("mask_le"), V("mask_ge"))
            order = []
            for f, b in zip((0, 1, 2, 3), (1, 0, 3, 2)):
                order += [(0, f), (1, b)]
            rel = {"wb": [], "qs": [], "st": [], "ks": [], "cn": [cnw]}
            written = set()
            for d, a in order:
                U, NM, WI, gw = gates[d]
                q0 = 32 * d
                s0, s1 = a * P, (a + 1) * P
                le = P - 1 if d == 0 else 0
                with_out = not (last_layer and a < 2)
                final = a == (3 if d == 0 else 2)
                v4 = lambda bank: bank[:, :].rearrange("p (h t) -> p h t", h=4)
                bi, bank, bw = pb.next()
                for h in range(4):
                    sl = ident[q0:q0 + 4, q0 + h:q0 + h + 1].to_broadcast([4, P])
                    mm(v4(bank)[:, h, :], U[:, s0:s1], sl, True, False, [gw] + bw)
                    last = mm(v4(bank)[:, h, :], sl, NM[:, s0:s1], False, True, inc=h == 3)
                di, dt_, dw = dts.next()
                t = tt(dt_, v4(bank), bc(masks[d], [P, 4, P], 1), ADD, [last] + dw)
                pb.done(bi, t)
                dtw = act(dt_, dt_, ACT.Exp, [t])
                bi, bank, bw = pb.next()
                for h in range(4):
                    sl = ident[q0:q0 + 4, q0 + h:q0 + h + 1].to_broadcast([4, P])
                    last = mm(v4(bank)[:, h, :], sl, WI[:, s0:s1], True, True, bw, inc=h == 3)
                wbw = act(wb, v4(bank), ACT.Exp, [last] + rel["wb"])
                pb.done(bi, wbw)
                rel["wb"] = []
                if with_out:
                    tqs = tt(qs, qt[:, :, s0:s1], wb, MUL, [wbw] + rel["qs"])
                    bi, bank, bw = pb.next()
                    for h in range(4):
                        last = mm(v4(bank)[:, h, :], kt[:, h, s0:s1], qt[:, h, s0:s1], True, True, bw, inc=h == 3)
                    tst = tt(st_, v4(bank), dt_, MUL, [last, dtw] + rel["st"])
                    pb.done(bi, tst)
                    for hp in range(2):
                        bi, bank, bw = pb.next()
                        pv = bank[:, 0:258].rearrange("p (h n) -> p h n", h=2)
                        for i in range(2):
                            h = 2 * hp + i
                            mm(pv[:, i, :], st_[:, h, :], vn[:, a, h, :], True, False, [tst, tqs] + bw + rel["cn"])
                            last = mm(pv[:, i, :], qs[:, h, :], cn[:, d, h, :], False, True, inc=i == 1)
                        t = cp(rd[:, 2:4], pv[:, :, 128], [last, te])
                        em = emt[:, 16 * d + 4 * a + 2 * hp:16 * d + 4 * a + 2 * hp + 2]
                        t = stt(rd[:, 0:2], rd[:, 2:4], -1.0, em, MUL, MAX, [t])
                        t = tt(rd[:, 0:2], rd[:, 0:2], rd[:, 2:4], MAX, [t])
                        t = rcp(rd[:, 0:2], rd[:, 0:2], [t])
                        for i in range(2):
                            h = 2 * hp + i
                            o = hn[:, a, h * P:(h + 1) * P]
                            if a in written:
                                t = stt(o, pv[:, i, 0:P], rd[:, i:i + 1], o, MUL, ADD, [t])
                            else:
                                t = ts(o, pv[:, i, 0:P], rd[:, i:i + 1], w=[t])
                        pb.done(bi, t)
                    written.add(a)
                    rel["qs"] = rel["st"] = [last]
                    read = last
                else:
                    read = None
                if not final:
                    t = tt(ks, kn[:, a], bc(dt_[:, :, le], [P, 4, P], 2), MUL, [dtw, knw] + rel["ks"])
                    tcn = []
                    for hp in range(2):
                        bi, bank, bw = pb.next()
                        pv = bank[:, 0:258].rearrange("p (h n) -> p h n", h=2)
                        for i in range(2):
                            h = 2 * hp + i
                            last = mm(pv[:, i, :], ks[:, h, :], vn[:, a, h, :], True, True, [t] + bw, inc=i == 1)
                        for i in range(2):
                            h = 2 * hp + i
                            tc_ = stt(cn[:, d, h, :], cn[:, d, h, :], wb[:, h, le:le + 1], pv[:, i, :], MUL, ADD,
                                      [last, wbw, read])
                        pb.done(bi, tc_)
                    rel["ks"] = [last]
                    rel["cn"] = [tc_]
                    rel["wb"] = [tc_]
                else:
                    rel["wb"] = [tqs]
                dts.done(di, (E.sem["v"], E.n["v"]))
            mg = V("mlstm_g", 4 * L, 4)
            ss = ar(4)
            prevr = []
            for a in tiles:
                sq4 = st_
                h4 = hn[:, a, :].rearrange("p (h d) -> p h d", h=4)
                t = act(sq4, h4, ACT.Square, E.barrier() if a == r0 else [])
                t = red(ss, sq4, ADD, [t])
                r, _ = rstd_of(ss, ss, 1.0 / P, [t])
                t = tt(h4, h4, bc(ss, [P, 4, P], 2), MUL, [r])
                t = tt(hn[:, a, :], hn[:, a, :], on[:, a, :], MUL, [t])
                bi, bank, bw = pb.next()
                for h in range(4):
                    last = tr(bank[:, h * P:(h + 1) * P], hn[:, a, h * P:(h + 1) * P], [t] + bw, inc=h == 3)
                t = tt(yt[:, 0:4, a * P:(a + 1) * P], bank[:, :].rearrange("p (h t) -> p h t", h=4),
                       bc(mg, [P, 4, P], 2), MUL, [last])
                pb.done(bi, t)
            all_wait(E.barrier())
            shut(n_rooms - 1)
            room("r")
            pairs(4)
            ytok = [split(yt[:, k, lo:], xh[:, k, lo:], xl[:, k, lo:], []) for k in range(KC)]
            gemm([gemm_t(A["w_out_2"][L], KC, DM, XL, nq, residual(16, lo), lambda k: ytok[k])])

            phase(5 if last_layer else 3)
            room("r", 2 * KC * nq + 3 * SLOT)
            xh, xl = ra(KC, nq), ra(KC, nq)
            pairs(3)
            room("f", 3 * nq)
            rs = ar(nq)
            sg = Turns([ar(nq) for _ in range(2)])
            n_rooms = room("f")
            sq_, tm_ = ar(KC, nq), ar(KC, nq)
            ps_ = [(a - lo, b - lo, m, s) for a, b, m, s in parts(1, 24, lo)]
            xtok = rms_split(xr[:, :, lo:], nq, xh, xl, ps_, sq_, tm_, rs, [])
            shut(n_rooms - 1)
            room("r")
            hh, hl = ra(22, nq), ra(22, nq)
            xw = lambda k: xtok[k]
            XF = lambda k: (xh[:, k, :], xl[:, k, :])
            jobs = []
            pend = {}

            def ev_gate(j, n, ps, tk):
                si, s, sw = sg.next()
                t = act(s, ps[:, 0, :], ACT.Silu, [tk] + sw)
                pend[j] = (si, s, t)
                return [t]

            def ev_up(j, n, ps, tk):
                si, s, t = pend.pop(j)
                t = tt(s, s, ps[:, 0, :], MUL, [t, tk])
                done = split(s, hh[:, j, :], hl[:, j, :], [t])
                sg.done(si, *done)
                return [t]

            for o in range(0, FF2, 256):
                jobs += [gemm_t(A["w_gu_2"][L][:, o:o + 256], KC, 256, XF, nq,
                                lambda j, n, ps, tk, o=o: ev_gate(o // P + j, n, ps, tk), xw, wide=256),
                         gemm_t(A["w_gu_2"][L][:, FF2 + o:FF2 + o + 256], KC, 256, XF, nq,
                                lambda j, n, ps, tk, o=o: ev_up(o // P + j, n, ps, tk), xw, wide=256)]
            gemm(jobs)
            gemm([gemm_t(A["w_down_2"][L], 22, DM, lambda k: (hh[:, k, :], hl[:, k, :]), nq, residual(40, lo),
                         [(E.sem["v"], E.n["v"])])])

        def final_():
            phase(9)
            room("f")
            xt = ar(KC, T)
            tmp = ar(KC, T)
            rs = ar(T)
            res = ar(2, DM)
            g = V("final")
            xw = rms_t(x, T, xt, lambda c: g[:, c:c + 1], tmp, rs, ())[-1]
            put_out(xt, res, xw)

        def put_out(xt, res, xw):
            for a in range(2):
                for c in range(0, KC, 4):
                    bi, bank, bw = pb.next()
                    for j in range(4):
                        last = tr(bank[:, j * P:(j + 1) * P], xt[:, c + j, a * P:(a + 1) * P], list(xw) + bw, inc=j == 3)
                    t = cp(res[:, a, c * P:(c + 4) * P], bank[:, :], [last], k="v")
                    pb.done(bi, t)
            E.dma("s", lambda e: e.dma_start(A["out"][0].rearrange("(a p) d -> p a d", p=P), res), s_out, 16, [t])
            E.q["s"].append(([(s_out, 16)], lambda e: None, None))

        def norm_x():
            phase(9)
            room("f")
            tmp = ar(KC, T)
            rs = ar(T)
            g = V("norm_final")
            rms_t(x, T, x, lambda c: g[:, c:c + 1], tmp, rs, ())

        steps = [("fox", fox), ("moe0", lambda: moe(0)), ("ret", ret), ("moe1", lambda: moe(1)),
                 ("norm", norm_x), ("sec0", lambda: second(0)), ("sec1", lambda: second(1))]
        for name, f in steps:
            f()
            if stop == name:
                break
        if stop is None:
            final_()
        else:
            phase(9)
            room("f")
            put_out(x, ar(2, DM), E.barrier())
        tail = [(ring_sem[i], 16 * wt["count"][i]) for i in range(NSLOT) if wt["count"][i]]
        tail += [(s_small, nsm[0]), (s_x, 32)]
        E.q["s"].append((tail, lambda e: None, None))
        shut()
        block = ctx.enter_context(nc.Block())
        E.run(block)


def consts():
    f = np.float32
    p = np.arange(P)
    inv = (f(1.0) / (f(10000.0) ** np.linspace(0.0, 1.0, 128, dtype=f))).astype(f)
    ang = (np.arange(T, dtype=f)[:, None] * inv[None, :]).astype(f)
    lg = np.log(1.0 - 2.0 ** (-5.0 - np.arange(4, dtype=np.float64)))
    rel = np.arange(T)[None, :] - p[:, None]
    dec = np.where(rel[:, None, :] >= 0, np.exp(lg[None, :, None] * np.maximum(rel, 0)[:, None, :]), 0.0)
    d = {
        "cos": np.cos(ang).T, "sin": np.sin(ang).T, "dec": dec.reshape(P, 1024), "ident": np.eye(P),
        "mask_z": np.zeros((P, P)), "mask_ge": np.where(p[None, :] > p[:, None], NEG, 0.0), "mask_le": np.where(p[None, :] < p[:, None], NEG, 0.0),
        "tri": (p[:, None] < p[None, :]), "ones": np.ones((P, P)), "iota": np.tile(np.arange(64), (P, 1)),
        "zero": np.zeros((P, 64)), "eps": np.full((P, 1), EPS), "jota": np.tile(np.arange(NX), (P, 1)),
    }
    return {k: np.asarray(v, f) for k, v in d.items()}


def layout(a):
    f = np.float32
    v = np.zeros((P, NVEC), f)

    def cols(name, x):
        o, w = VEC[name]
        v[:, o:o + w] = x.reshape(w, P).T

    cols("norm_mix", a["norm_mix"])
    cols("norm_ffn", a["norm_ffn"])
    cols("norm_final", a["norm_final"])
    cols("gn", a["ret_gn_gain"])
    cols("norm1", a["norm1_g_2"])
    cols("norm2", a["norm2_g_2"])
    cols("final", a["final_g_2"])
    cols("b_mod", a["b_mod_2"])
    cols("mlstm_g", a["mlstm_g_2"])
    cols("cln_g", a["conv_ln_g_2"])
    cols("cln_b", a["conv_ln_b_2"])
    cols("conv_b", a["conv_b_2"])
    cols("c", a["c_2"])
    cols("cc", a["c_ctx_2"])
    b = a["b_in_2"]
    cols("bq", b[:, 0:512])
    cols("bk", b[:, 512:1024])
    cols("bu", b[:, 2064:2320])
    cols("bc", b[:, 2576:3088])
    o, w = VEC["conv_w"]
    v[:, o:o + w] = a["conv_w_2"].reshape(2, 31, 2, P).transpose(3, 0, 2, 1).reshape(P, 124)
    o, _ = VEC["bg"]
    v[0:16, o:o + 2] = b[:, 2048:2064].T
    o, _ = VEC["bf"]
    v[0:16, o] = v[64:80, o] = a["fox_b_f"][0]
    for k, x in consts().items():
        o, w = VEC[k]
        v[:, o:o + w] = x
    r = np.zeros((P, NROW), f)

    def put(name, x):
        q, o, w = ROW[name]
        r[q, o:o + w] = x.reshape(-1)

    put("br", np.concatenate([a["router_group_b"], a["router_expert_b"]], 1))
    put("bv", b[:, 1024:1536])
    put("bo", b[:, 1536:2048])
    put("bs", b[:, 2320:2576])
    put("sgub", a["sgu_b_2"])
    wr = np.concatenate([a["router_group_w"], a["router_expert_w"]], 2)
    out = {k: a[k] for k in BIG}
    out["vec"], out["row"] = v, r
    out["wr"] = np.ascontiguousarray(wr.reshape(2, KC, P, 36).transpose(0, 2, 1, 3))
    out["sgu_wt"] = np.ascontiguousarray(a["sgu_w_2"].transpose(0, 3, 1, 2))
    return out


BIG = ["x", "ctx_2", "fox_w_in", "fox_w_out", "ret_w_in", "ret_w_out", "expert_w_gu", "expert_w_down",
       "w_mod_2", "w_in_2", "w_out_2", "w_gu_2", "w_down_2", "sgu_ln_g_2", "sgu_ln_b_2"]


def kernel(**inputs):
    import numpy as _np
    import concourse.bacc as _bacc
    from concourse import mybir as _mybir
    from concourse.bass_utils import run_bass_kernel_spmd as _run

    arrays = {k: _np.ascontiguousarray(v) for k, v in layout({k: _np.asarray(v) for k, v in inputs.items()}).items()}
    nc = _bacc.Bacc("TRN2", target_bir_lowering=False, num_devices=1)
    aps = {k: nc.dram_tensor(f"in_{k}", v.shape, _mybir.dt.from_np(v.dtype), kind="ExternalInput").ap()
           for k, v in arrays.items()}
    aps["out"] = nc.dram_tensor("out_0", (1, T, DM), _mybir.dt.float32, kind="ExternalOutput").ap()
    build(nc, aps)
    r = _run(nc, [{f"in_{k}": v for k, v in arrays.items()}], core_ids=[0])
    return r.results[0]["out_0"]
```

```python
import numpy as np
import concourse.bass as bass
from concourse import mybir
from contextlib import ExitStack

F32 = mybir.dt.float32
I32 = mybir.dt.int32
F32R = mybir.dt.float32r
ALU = mybir.AluOpType
ACT = mybir.ActivationFunctionType
AX = mybir.AxisListType
MUL, ADD, SUB, MAX, MIN = ALU.mult, ALU.add, ALU.subtract, ALU.max, ALU.min

P = 128
DM = 1024
KC = DM // P
T = 256
EPS = 1e-6
NEG = -1e30
NE = 32
NX = 15
SL = 32
GB = 8
FF2 = 2816

NSLOT = 12
RATE = 6
F_LONG = 22072
SLOT = 2048
SPACE = 44644

VEC = {}
_n = [0]


def _vec(name, width):
    VEC[name] = (_n[0], width)
    _n[0] += width


for _name, _w in (("norm_mix", 16), ("norm_ffn", 16), ("norm_final", 8), ("gn", 16), ("norm1", 16),
                  ("norm2", 16), ("final", 8), ("b_mod", 96), ("mlstm_g", 8), ("cln_g", 4), ("cln_b", 4),
                  ("conv_b", 4), ("conv_w", 124), ("bq", 8), ("bk", 8), ("bg", 2), ("bu", 4), ("bc", 8),
                  ("c", 8), ("cc", 8), ("bf", 1), ("cos", 256), ("sin", 256), ("dec", 1024), ("ident", 128),
                  ("mask_z", 128), ("mask_ge", 128), ("mask_le", 128), ("tri", 128), ("ones", 128), ("iota", 64), ("zero", 64),
                  ("eps", 1), ("jota", NX)):
    _vec(_name, _w)
NVEC = _n[0]
ROW = {"bv": (0, 0, 1024), "bo": (32, 0, 1024), "bs": (64, 0, 512), "br": (64, 512, 72), "sgub": (96, 0, 1024)}
NROW = 1024


class Engines:

    def __init__(self, nc, ctx):
        self.nc = nc
        self.q = {k: [] for k in "vapgs"}
        self.n = dict.fromkeys("vapgs", 0)
        self.sem = {k: ctx.enter_context(nc.semaphore(f"done_{k}")) for k in "vapgs"}
        self.seen = {}

    def put(self, k, fn, waits=(), inc=True, own=True):
        need = {}
        waits = list(waits)
        if own and self.n[k] and k in "vag":
            waits.append((self.sem[k], self.n[k]))
        for w in waits:
            if w is None:
                continue
            s, v = w
            if v > self.seen.get((k, s.name), 0):
                need[s.name] = (s, max(v, need.get(s.name, (s, 0))[1]))
        for name, (s, v) in need.items():
            self.seen[(k, name)] = v
        if inc:
            self.n[k] += 1
        self.q[k].append((list(need.values()), fn, self.sem[k] if inc else None))
        return (self.sem[k], self.n[k])

    def dma(self, k, fn, sem, value, waits=()):
        need = []
        for w in waits:
            if w is not None and w[1] > self.seen.get((k, w[0].name), 0):
                self.seen[(k, w[0].name)] = w[1]
                need.append(w)
        self.q[k].append((need, lambda e: (fn(e).then_inc(sem, 16), None)[1], None))
        return (sem, value)

    def branch(self, cell, ready):
        self.saved = dict(self.seen)
        self.at = dict(self.n)
        for k in "vaps":
            self.q[k].append(("if", cell, ready))

    def join(self, extra):
        for k in "vaps":
            adds = [(self.sem[k], self.at[k], self.n[k] - self.at[k])] if self.n[k] > self.at[k] else []
            self.q[k].append(("end", adds + (extra if k == "s" else [])))
        self.seen = self.saved

    def barrier(self):
        now = [(self.sem[k], self.n[k]) for k in "vapg" if self.n[k]]
        return now

    def run(self, block):
        def emit(e, items):
            while items:
                head = items.pop(0)
                if head[0] == "if":
                    e.wait_ge(*head[2])
                    v = e.value_load(head[1], min_val=0, max_val=NX)
                    with e.If(v > 0):
                        adds = emit(e, items)
                    with e.Else():
                        for s, at, n in adds:
                            if at:
                                e.wait_ge(s, at)
                            e.sem_inc(s, n)
                    continue
                if head[0] == "end":
                    return head[1]
                waits, fn, sem = head
                for s, v in waits:
                    e.wait_ge(s, v)
                r = fn(e)
                if sem is not None:
                    r.then_inc(sem, 1)

        def body(k):
            def _(e):
                emit(e, self.q[k])
            return _
        block.sync(body("s"))
        block.gpsimd(body("g"))
        block.scalar(body("a"))
        block.vector(body("v"))
        block.tensor(body("p"))


class Turns:

    def __init__(self, items):
        self.items = items
        self.free = [[] for _ in items]
        self.at = 0
        self.held = set()

    def next(self):
        while self.at in self.held:
            self.at = (self.at + 1) % len(self.items)
        i = self.at
        self.at = (i + 1) % len(self.items)
        w, self.free[i] = self.free[i], []
        return i, self.items[i], w

    def done(self, i, *toks):
        self.held.discard(i)
        self.free[i] = list(toks)


def build(nc, A, stop=None):
    ctx = ExitStack()
    with ctx:
        E = Engines(nc, ctx)
        put = E.put

        def sb(name, shape, dt=F32):
            return ctx.enter_context(nc.sbuf_tensor(name, shape, dt))

        def sem(name):
            return ctx.enter_context(nc.semaphore(name))

        xr = sb("xr", [P, KC, 2 * T])
        vec = sb("vec_sb", [P, NVEC])
        row = sb("row_sb", [P, NROW])
        mods = sb("mods", [P, 256])
        eid = sb("eid", [1, 2 * NX + 2], I32)
        banks = [ctx.enter_context(nc.psum_tensor(f"bank{i}", [P, 512], F32)) for i in range(8)]
        ring_sem = [sem(f"ring{i}") for i in range(NSLOT)]
        x_sem = [sem(f"xring{i}") for i in range(3)]
        s_vec = sem("s_vec")
        s_x = sem("s_x")
        s_small = sem("s_small")
        s_out = sem("s_out")

        def mm(out, lhsT, rhs, start, stop, w=(), inc=False, tile=None, skip=False):
            return put("p", lambda e: e.matmul(out, lhsT, rhs, start=start, stop=stop, tile_position=tile,
                                               skip_group_check=skip), w, inc)

        def tr(out, in_, w=(), inc=False):
            n = in_.shape[0]
            return put("p", lambda e: e.transpose(out, in_, V("ident")[0:n, 0:n]), w, inc)

        def act(out, in_, f, w=(), bias=None, scale=1.0, accum=None):
            kw = {}
            if bias is not None:
                kw["bias"] = bias
            if accum is not None:
                kw["accum_out"] = accum
            return put("a", lambda e: e.activation(out, in_, f, scale=scale, **kw), w)

        def tt(out, a, b, op, w=(), k="v"):
            return put(k, lambda e: e.tensor_tensor(out, a, b, op), w)

        def ts(out, a, s1, s2=None, op0=MUL, op1=None, w=(), k="v"):
            if op1 is None:
                return put(k, lambda e: e.tensor_scalar(out, a, s1, None, op0), w)
            return put(k, lambda e: e.tensor_scalar(out, a, s1, s2, op0, op1), w)

        def stt(out, a, s, b, op0, op1, w=()):
            return put("v", lambda e: e.scalar_tensor_tensor(out, a, s, b, op0, op1), w)

        def cp(out, a, w=(), k="v"):
            if k == "a":
                return act(out, a, ACT.Copy, w)
            return put(k, lambda e: e.tensor_copy(out, a), w)

        def red(out, a, op, w=(), axis=AX.X):
            return put("v", lambda e: e.tensor_reduce(out, a, axis, op), w)

        def rcp(out, a, w=()):
            return put("v", lambda e: e.reciprocal(out, a), w)

        def scan(out, a, b, init, op0, op1, w=()):
            return put("v", lambda e: e.tensor_tensor_scan(out, a, b, init, op0, op1), w)

        def fill(out, value, w=(), k="v"):
            return put(k, lambda e: e.memset(out, value), w)

        def bc(ap, shape, *axes):
            for x in axes:
                ap = ap.unsqueeze(x)
            return ap.to_broadcast(shape)

        def V(name, a=0, n=None):
            o, wd = VEC[name]
            return vec[:, o + a:o + (wd if n is None else a + n)]

        def R(name, a=0, n=None):
            q, o, wd = ROW[name]
            return row[q:q + 1, o + a:o + (wd if n is None else a + n)], ones[q:q + 1, :]

        eps = V("eps")
        ones = V("ones")
        ident = V("ident")

        rooms = []
        names = [0]
        ring = [None]
        wt = {"order": [], "use": 0, "free": [[] for _ in range(NSLOT)], "count": [0] * NSLOT}

        def shut(n=0):
            while len(rooms) > n:
                rooms.pop()[0].close()

        def room(kind, size=None):
            taken = sum(r[3] for r in rooms)
            size = SPACE - taken if size is None else size
            assert taken + size <= SPACE, (taken, size)
            st = ExitStack()
            names[0] += 1
            t = st.enter_context(nc.sbuf_tensor(f"{kind}{names[0]}", [P, size], F32))
            rooms.append([st, t, kind, size, 0])
            return len(rooms)

        def all_wait(toks):
            for k in "vagp":
                put(k, lambda e: e.nop(), toks)

        def phase(slots):
            shut()
            now = E.barrier()
            all_wait(now)
            for i in range(wt["use"], slots):
                wt["free"][i] = now
            wt["use"] = slots
            wt["order"] = [i for i in wt["order"] if i < slots]
            wt["order"] += [i for i in range(slots) if i not in wt["order"]]
            room("ring", slots * SLOT)
            ring[0] = rooms[0][1]

        def ar(*dims, kind="f", at=None):
            r = [r for r in rooms if r[2] == kind][-1]
            n = int(np.prod(dims))
            o = r[4] if at is None else at
            a = r[1][:, o:o + n]
            assert o + n <= r[3], (o, n, r[3])
            if at is None:
                r[4] += n
            if len(dims) == 2:
                a = a.rearrange("p (a b) -> p a b", a=dims[0])
            if len(dims) == 3:
                a = a.rearrange("p (a b c) -> p a b c", a=dims[0], b=dims[1])
            if len(dims) == 4:
                a = a.rearrange("p (a b c d) -> p a b c d", a=dims[0], b=dims[1], c=dims[2])
            return a

        def ra(*dims):
            return ar(*dims, kind="r")

        def back_to(o):
            r = [r for r in rooms if r[2] == "f"][-1]
            was, r[4] = r[4], o
            return was

        def slot_at(i, a, b):
            o = i * SLOT
            return ring[0][:, o:o + a * b].rearrange("p (a b) -> p a b", a=a)

        def wload(src, a, b):
            i = wt["order"].pop(0)
            wt["order"].append(i)
            wt["count"][i] += 1
            dst = slot_at(i, a, b)
            s = src.rearrange("(a p) n -> p a n", p=P)
            tok = E.dma("s", lambda e: e.dma_start(dst, s), ring_sem[i], 16 * wt["count"][i], wt["free"][i])
            wt["free"][i] = []
            return i, dst, tok

        def wfree(slots, tok):
            for i, _, _ in slots:
                wt["free"][i] = [tok]

        pb = Turns(banks)

        def blocks(n):
            return [(o, min(512, n - o)) for o in range(0, n, 512)]

        def split(x, high, low, w, k="a"):
            t1 = cp(high.bitcast(F32R), x, w, k=k)
            return [t1, tt(low.bitcast(F32R), x, high, SUB, [t1])]

        def mm3(out, a, b, start, stop, w=(), inc=False, tile=None):
            (ah, al), (bh, bl) = a, b
            for i, (p, q) in enumerate(((ah, bh), (ah, bl), (al, bh))):
                last = mm(out, p.bitcast(F32R), q.bitcast(F32R), start and i == 0, stop and i == 2, w,
                          inc and i == 2, tile)
            return last

        hb = [None]
        side = [[]]

        def drain():
            while side[0]:
                f = side[0].pop(0)
                if f is not None:
                    f()

        def pairs(n):
            hb[0] = Turns([(ra(SLOT // 2), ra(SLOT // 2)) for _ in range(n)])

        def job(W, kchunks, N, x, outs, evac, w, moving, bias=None, wide=512, after=None,
                block=None):
            return dict(W=W, K=kchunks, N=N, x=x, outs=outs, evac=evac, w=w, moving=moving, bias=bias, wide=wide,
                        after=after, block=block)

        def gemm(jobs, norm=None):
            items = []
            for jb in jobs:
                step = 4 if jb["wide"] > 256 else 8
                for o in range(0, jb["N"], jb["wide"]):
                    n = min(jb["wide"], jb["N"] - o)
                    for g in range(0, jb["K"], step):
                        kn = min(step, jb["K"] - g)
                        half = min(step // 2, kn)
                        for i in range(0, kn, half):
                            items.append((jb, o, n, g, kn, i, min(half, kn - i)))
            ready_ = []
            now = [None]

            def prep(jb, o, n, g, kn, i, m):
                if i == 0:
                    now[0] = wload(jb["W"][g * P:(g + kn) * P, o:o + n], kn, n)
                sl = now[0]
                hi_, hl, hw = hb[0].next()
                high, low = (z[:, 0:m * n].rearrange("p (a b) -> p a b", a=m) for z in hl)
                toks = split(sl[1][:, i:i + m, :], high, low, [sl[2]] + hw)
                if i + m == kn:
                    wfree([sl], toks[1])
                ready_.append((hi_, high, low, toks))

            ahead = len(hb[0].items) - 1
            nxt = [0]
            side_ = side[0]

            def up_to(n):
                while nxt[0] < min(n, len(items)):
                    prep(*items[nxt[0]])
                    nxt[0] += 1

            if norm is not None:
                norm(lambda: up_to(2))
            for i, (jb, o, n, g, kn, i0, m) in enumerate(items):
                up_to(i + ahead + 1)
                hi_, high, low, sw = ready_.pop(0)
                k0 = g + i0
                if k0 == 0:
                    cn_ = min(P, n)
                    outs = list(range(n // cn_)) if jb["moving"] else jb["outs"]
                    acc_ = [pb.next() for _ in outs]
                    pb.held.update(a[0] for a in acc_)
                end = k0 + m == jb["K"]
                toks = []
                for u, (bi, bank, bw) in zip(outs, acc_):
                    for k in range(m):
                        w = list(jb["w"](k0 + k) if callable(jb["w"]) else jb["w"]) + bw + sw
                        stop_ = end and k == m - 1 and jb["bias"] is None
                        inc = (k == m - 1)
                        if jb["moving"]:
                            c = slice(u * cn_, (u + 1) * cn_)
                            out = bank[0:cn_, 0:jb["outs"]]
                            last = mm3(out, (high[:, k, c], low[:, k, c]), jb["x"](k0 + k), k0 + k == 0, stop_, w, inc)
                        else:
                            out = bank[:, 0:n]
                            last = mm3(out, jb["x"](k0 + k, u), (high[:, k, :], low[:, k, :]), k0 + k == 0, stop_, w,
                                       inc)
                    if end and jb["bias"] is not None:
                        last = mm(out, jb["bias"][1], jb["bias"][0][:, o:o + n], False, True, inc=True)
                    toks.append((u, bi, out, last))
                hb[0].done(hi_, last)
                for _ in range(max(RATE, -(-len(side_) // max(1, len(items) - 4 - i))) if side_ else 0):
                    f = side_.pop(0) if side_ else None
                    if f is None:
                        break
                    f()
                if end:
                    for u, bi, out, tok in toks:
                        if jb["moving"]:
                            pb.done(bi, *jb["evac"](o // P + u, 1, out.unsqueeze(1), tok))
                        else:
                            pb.done(bi, *jb["evac"](u, o, n, out, tok))
                    if jb["block"] is not None:
                        jb["block"](o)
                    if o + n >= jb["N"] and jb["after"] is not None:
                        jb["after"]()

        def gemm_t(W, kchunks, N, x, ntok, evac, w, **kw):
            return job(W, kchunks, N, x, ntok, evac, w, True, **kw)

        def gemm_n(W, kchunks, N, x, tiles, evac, w, **kw):
            return job(W, kchunks, N, x, list(tiles), evac, w, False, **kw)

        def colsum(views, ntok, w):
            bi, bank, bw = pb.next()
            for i, v in enumerate(views):
                last = mm(bank[:, 0:ntok], ones, v, i == 0, i == len(views) - 1, list(w) + bw,
                          inc=i == len(views) - 1)
            return bi, bank[:, 0:ntok], last

        def rstd_of(out, src, scale, w):
            t = act(out, src, ACT.Sqrt, w, bias=eps, scale=scale)
            return rcp(out, out, [t]), t

        early_sum = {}

        def sum_early(x, ntok, scratch):
            turns = Turns(scratch)

            def go(o):
                if o:
                    return
                written = (E.sem["v"], E.n["v"])
                got = {}

                def one(c):
                    if c == 0:
                        early_sum["bank"] = pb.next()
                        pb.held.add(early_sum["bank"][0])
                    i, s, w = turns.next()
                    got[c] = (i, s, act(s, x[:, c, :], ACT.Square, [written] + w))

                def two(c):
                    i, s, t = got[c]
                    turns.done(i, mm(early_sum["bank"][1][:, 0:ntok], ones, s, c == 0, False,
                                     [t] + early_sum["bank"][2], inc=True))
                    early_sum["n"] = c + 1

                for c in range(4):
                    side[0].extend([lambda c=c: one(c), None, lambda c=c: two(c)])
            return go

        def rstd_t(x, ntok, sq, rs, w, mid=None):
            if "bank" in early_sum:
                drain()
            c0 = early_sum.pop("n", 0)
            bi, bank, bw = early_sum.pop("bank") if c0 else pb.next()
            for c in range(c0, KC):
                if c % 2:
                    t = tt(sq[:, c, :], x[:, c, :], x[:, c, :], MUL, w)
                else:
                    t = act(sq[:, c, :], x[:, c, :], ACT.Square, w)
                last = mm(bank[:, 0:ntok], ones, sq[:, c, :], c == 0, c == KC - 1, [t] + bw, inc=c == KC - 1)
            if mid is not None:
                mid()
            r, t = rstd_of(rs, bank[:, 0:ntok], 1.0 / DM, [last])
            pb.done(bi, t)
            return r

        def rms_t(x, ntok, out, m, tmp, rs, w):
            t = rstd_t(x, ntok, tmp, rs, w)
            toks = []
            for c in range(KC):
                t = stt(out[:, c, :], x[:, c, :], m(c), rs, MUL, MUL, [t])
                toks.append([t])
            return toks

        def rms_split(x, ntok, high, low, parts_, sq, tmp, rs, w, mid=None):
            r = rstd_t(x, ntok, sq, rs, w, mid)
            got = {}
            pieces = [(c, *q) for c in range(KC) for q in parts_]

            def first(c, lo, hi, m, a):
                o, h = tmp[:, c, lo:hi], high[:, c, lo:hi]
                t = stt(o, x[:, c, lo:hi], m(c), rs[:, lo:hi], MUL, MUL, [r])
                if a is None:
                    got[c, lo] = act(h.bitcast(F32R), o, ACT.Copy, [t])
                else:
                    got[c, lo] = act(h.bitcast(F32R), o, ACT.Identity, [t], bias=a(c))

            def second_(c, lo, hi, m, a):
                o, h, l = tmp[:, c, lo:hi], high[:, c, lo:hi], low[:, c, lo:hi].bitcast(F32R)
                t1 = got[c, lo]
                got[c, lo] = [t1, tt(l, o, h, SUB, [t1]) if a is None else stt(l, o, a(c), h, ADD, SUB, [t1])]

            for i in range(len(pieces) + 2):
                if i < len(pieces):
                    first(*pieces[i])
                if i >= 2:
                    second_(*pieces[i - 2])
            return [[t for lo, *_ in parts_ for t in got[c, lo]] for c in range(KC)]

        nsm = [0]

        def small(dst, src, w=()):
            nsm[0] += 16
            return E.dma("g", lambda e: e.dma_start(dst, src), s_small, nsm[0], list(w))

        E.dma("s", lambda e: e.dma_start(vec[:, :], A["vec"]), s_vec, 16)
        E.dma("s", lambda e: e.dma_start(row[:, :], A["row"]), s_vec, 32)
        ready = (s_vec, 32)
        for k in "vagp":
            put(k, lambda e: e.nop(), [ready])

        x = xr[:, :, T:2 * T]
        phase(6)
        room("f")
        xin = ar(2, DM)
        cin = ar(2, DM)
        E.dma("s", lambda e: e.dma_start(xin, A["x"][0].rearrange("(a p) d -> p a d", p=P)), s_x, 16)
        E.dma("s", lambda e: e.dma_start(cin, A["ctx_2"][0].rearrange("(a p) d -> p a d", p=P)), s_x, 32)
        for src, dst in ((xin, x), (cin, xr[:, :, 0:T])):
            for a in range(2):
                for c in range(0, KC, 4):
                    bi, bank, bw = pb.next()
                    for j in range(4):
                        last = tr(bank[:, j * P:(j + 1) * P], src[:, a, (c + j) * P:(c + j + 1) * P],
                                  bw + [(s_x, 32)], inc=j == 3)
                    pb.done(bi, cp(dst[:, c:c + 4, a * P:(a + 1) * P],
                                   bank[:, :].rearrange("p (a t) -> p a t", a=4), [last], k="a" if c else "v"))

        def modulation(L):
            cs = ar(KC, 32)
            rows = Turns([ar(512), ar(512)])
            sel2 = ar(2)
            mod = mods[:, 128 * L:128 * L + 96].rearrange("p (c v) -> p c v", v=2)
            t0 = fill(cs, 0.0)
            t0 = act(cs[:, :, 0], V("cc"), ACT.Silu, [t0])
            t0 = act(cs[:, :, 1], V("c"), ACT.Silu, [t0])
            ts_ = red(sel2, ident.rearrange("p (a b) -> p b a", a=4)[:, 0:2, :], ADD)

            def load(i, info):
                o = 512 * i
                info[i] = [wload(A["w_mod_2"][L, g * 512:(g + 1) * 512, o:o + 512], 4, 512) for g in range(2)]

            def product(i, info):
                slots = info[i]
                bi, bank, bw = pb.next()
                for g in range(2):
                    for c in range(4):
                        last = mm(bank[32 * c:32 * c + 32, :], cs[:, 4 * g + c, :], slots[g][1][:, c, :], g == 0, g == 1,
                                  [t0, slots[g][2]] + bw, inc=(c == 3), tile=(0, 32 * c))
                    wfree([slots[g]], last)
                ri, rr, rw = rows.next()
                tr_ = cp(rr, bank[:, :], [last] + rw, k="a")
                pb.done(bi, tr_)
                info[i] = (ri, rr, tr_)

            def turn(i, info):
                ri, rr, tr_ = info.pop(i)
                bi, bank, bw = pb.next()
                for j in range(4):
                    last = mm(bank[:, 2 * j:2 * j + 2], rr[:, j * P:(j + 1) * P], sel2, True, True,
                              [tr_, ts_] + bw, inc=j == 3)
                rows.done(ri, last)
                b = bc(V("b_mod", 48 * L + 4 * i, 4), [P, 4, 2], 2)
                pb.done(bi, tt(mod[:, 4 * i:4 * i + 4, :], bank[:, 0:8].rearrange("p (c v) -> p c v", v=2), b, ADD,
                               [last]))

            info = {}

            def step(i):
                if i < 12:
                    load(i, info)
                    product(i, info)
                if i:
                    turn(i - 1, info)
            return [lambda i=i: step(i) for i in range(13)]

        def fox():
            phase(6)
            room("r", 2 * KC * T + 2 * KC * P + 10 * SLOT // 2)
            xh, xl, wfh, wfl = ra(KC, T), ra(KC, T), ra(KC, P), ra(KC, P)
            pairs(5)
            room("f")
            H, dh = 16, 64
            W = A["fox_w_in"][0]
            xt = ar(KC, T)
            tmp = ar(KC, T)
            rs = ar(T)
            qt = ar(KC, T)
            kt = ar(KC, T)
            gt = ar(KC, T)
            v = ar(2, DM)
            cum = ar(T)
            ncum = ar(T)
            wf = ar(KC, P)
            zf = fill(wf, 0.0)
            for q0 in (0, 64):
                tf = small(wf[:, :, q0:q0 + H], W[:, 4 * DM:4 * DM + H].rearrange("(a p) n -> p a n", p=P), [zf])
            g = V("norm_mix")
            xtok = rms_split(x, T, xh, xl, [(0, T, lambda c: g[:, c:c + 1], None)], tmp, xt, rs, ())
            xw = lambda k: xtok[k]
            X = lambda k: (xh[:, k, :], xl[:, k, :])
            def gates():
                fw = split(wf, wfh, wfl, [tf])
                bi, bank, bw = pb.next()
                for k in range(KC):
                    last = mm3(bank[:, 0:T], (wfh[:, k, :], wfl[:, k, :]), X(k), k == 0, k == KC - 1, xw(k) + bw + fw,
                               inc=k == KC - 1)
                z = ts(ncum[:, :], bank[:, 0:T], V("bf")[:, :], op0=ADD, w=[last])
                pb.done(bi, z)
                z = stt(cum[:, :], ncum[:, :], -1.0, ncum[:, :], MUL, MAX, [z])
                z = act(cum[:, :], cum[:, :], ACT.Exp, [z], scale=-1.0)
                z = act(cum[:, :], cum[:, :], ACT.Ln, [z], bias=ones[:, 0:1])
                z = stt(ncum[:, :], ncum[:, :], 0.0, cum[:, :], MIN, SUB, [z])
                z = scan(cum[:, :], bc(ones[:, 0:1], [P, T]), ncum[:, :], 0.0, MUL, ADD, [z])
                cw = ts(ncum[:, :], cum[:, :], -1.0, w=[z])
                gate_sum.append(cw)

            gate_sum = []
            gemm([gemm_t(W[:, 0:DM], KC, DM, X, T,
                         lambda j, n, ps, t: [act(qt[:, j:j + n, :], ps, ACT.Copy, [t], scale=dh ** -0.5)], xw, after=gates),
                  gemm_t(W[:, DM:2 * DM], KC, DM, X, T,
                         lambda j, n, ps, t: [cp(kt[:, j:j + n, :], ps, [t], k="a")], xw),
                  gemm_n(W[:, 2 * DM:3 * DM], KC, DM,
                         lambda k, a: (xh[:, k, a * P:(a + 1) * P], xl[:, k, a * P:(a + 1) * P]), (0, 1),
                         lambda a, o, n, ps, t: [cp(v[:, a, o:o + n], ps, [t], k="a")], xw),
                  gemm_t(W[:, 3 * DM:4 * DM], KC, DM, X, T,
                         lambda j, n, ps, t: [act(gt[:, j:j + n, :], ps, ACT.Sigmoid, [t])], xw)])
            ot = xt
            steps = modulation(0)
            s_b = Turns([tmp[:, 2 * i:2 * i + 2, :].rearrange("p a t -> p (a t)") for i in range(2)] + [ar(2 * T)])
            p_b = Turns([tmp[:, 4 + 2 * i:6 + 2 * i, :].rearrange("p a t -> p (a t)") for i in range(2)])
            qkv = E.barrier()
            mask = vec[:, VEC["mask_z"][0]:VEC["mask_z"][0] + 2 * P]
            cq = rs[:, 64:96].rearrange("p (a h) -> p a h", a=2)
            bi, bank, bw = pb.next()
            for a in range(2):
                last = mm(bank[:, H * a:H * a + H], cum[0:H, a * P:(a + 1) * P], ident[0:H, 0:H], True, True,
                          qkv + bw, inc=a == 1)
            cqw = cp(cq, bank[:, 0:2 * H].rearrange("p (a h) -> p a h", a=2), [last])
            pb.done(bi, cqw)
            mx_b = Turns([rs[:, 8 * i:8 * i + 8] for i in range(4)])
            batches = []
            for qb in range(2):
                nh = 4 if qb == 0 else 2
                for h0 in [2 * nh * i + j for i in range(H // nh // 2) for j in range(2)]:
                    batches.append((qb, nh, P * (qb + 1), h0))
            info = {}

            def scores(i):
                qb, nh, nk, h0 = batches[i]
                bi, bank, bw = pb.next()
                sv = bank[:, :].rearrange("p (h k) -> p h k", h=nh)
                for j in range(nh):
                    h = h0 + 2 * j
                    q0 = 64 * (h % 2)
                    mm(sv[:, j, :], qt[q0:q0 + 64, h // 2, qb * P:(qb + 1) * P],
                       kt[q0:q0 + 64, h // 2, 0:nk], True, False, qkv + bw + gate_sum)
                    sel = ident[q0:q0 + H, q0 + h:q0 + h + 1]
                    last = mm(sv[:, j, :], sel.to_broadcast([H, P]), ncum[q0:q0 + H, 0:nk], False, True,
                              inc=j == nh - 1)
                si, s_, sw = s_b.next()
                mi, m, mw = mx_b.next()
                s = s_.rearrange("p (h k) -> p h k", h=nh)
                for j in range(nh):
                    t = stt(s[:, j, :], sv[:, j, :], cq[:, qb, h0 + 2 * j:h0 + 2 * j + 1],
                            mask[:, P - (nk - P):2 * P], ADD, ADD, [last, cqw] + sw)
                pb.done(bi, t)
                t = red(m[:, 0:nh], s, MAX, [t] + mw)
                t = ts(m[:, 0:nh], m[:, 0:nh], -1.0, w=[t])
                for j in range(nh):
                    te = act(s[:, j, :], s[:, j, :], ACT.Exp, [t], bias=m[:, j:j + 1], accum=m[:, 4 + j:5 + j])
                info[i] = (si, s_, s, mi, m, te)

            def weights(i):
                qb, nh, nk, h0 = batches[i]
                si, s_, s, mi, m, t = info[i]
                t = rcp(m[:, 4:4 + nh], m[:, 4:4 + nh], [t])
                t = tt(s, s, bc(m[:, 4:4 + nh], [P, nh, nk], 2), MUL, [t])
                mx_b.done(mi, t)
                info[i] = (si, s_, t)

            def turned(i):
                si, s_, t = info[i]
                bi, bank, bw = pb.next()
                for j in range(4):
                    last = tr(bank[:, j * P:(j + 1) * P], s_[:, j * P:(j + 1) * P], [t] + bw, inc=j == 3)
                s_b.done(si, last)
                pi, pt, pw = p_b.next()
                t = cp(pt, bank[:, :], [last] + pw, k="a")
                pb.done(bi, t)
                info[i] = (pi, pt, t)

            def values(i):
                qb, nh, nk, h0 = batches[i]
                pi, pt, t = info.pop(i)
                bi, bank, bw = pb.next()
                q0 = 64 * (h0 % 2)
                for j in range(nh):
                    h = h0 + 2 * j
                    for kb in range(qb + 1):
                        last = mm(bank[q0:q0 + 64, j * P:(j + 1) * P], v[:, kb, h * dh:(h + 1) * dh],
                                  pt[:, (j * (qb + 1) + kb) * P:(j * (qb + 1) + kb + 1) * P],
                                  kb == 0, kb == qb, [t] + bw, inc=(j == nh - 1 and kb == qb),
                                  tile=(0, q0))
                p_b.done(pi, last)
                c0 = h0 // 2
                t = tt(ot[q0:q0 + 64, c0:c0 + nh, qb * P:(qb + 1) * P],
                       bank[q0:q0 + 64, 0:nh * P].rearrange("p (a t) -> p a t", a=nh),
                       gt[q0:q0 + 64, c0:c0 + nh, qb * P:(qb + 1) * P], MUL, [last])
                pb.done(bi, t)
                return t

            for i in range(len(batches) + 2):
                if 1 <= i <= len(batches):
                    weights(i - 1)
                if i < len(batches):
                    scores(i)
                if 1 <= i <= len(batches):
                    turned(i - 1)
                if i >= 2:
                    t = values(i - 2)
                if steps:
                    steps.pop(0)()
            otok = [split(ot[:, k, :], xh[:, k, :], xl[:, k, :], [t]) for k in range(KC)]
            gemm([gemm_t(A["fox_w_out"][0], KC, DM, X, T,
                         lambda j, n, ps, tk: [tt(x[:, j:j + n, :], ps, x[:, j:j + n, :], ADD, [tk])], lambda k: otok[k],
                         block=sum_early(x, T, [tmp[:, 6, :], tmp[:, 7, :]]))])

        def moe(L):
            phase(12)
            room("f")
            xt = ar(KC, T)
            tmp = ar(KC, T)
            rs = ar(T)
            xn = ar(2, DM)
            wr = ar(KC, 36)
            tw = small(wr, A["wr"][L])
            g = V("norm_ffn", 8 * L, 8)
            xw = rms_t(x, T, xt, lambda c: g[:, c:c + 1], tmp, rs, ())[-1]
            lg = ar(2, 36)
            bi, bank, bw = pb.next()
            rb, r1_ = R("br", 36 * L, 36)
            for a in range(2):
                for k in range(KC):
                    mm(bank[:, 36 * a:36 * a + 36], xt[:, k, a * P:(a + 1) * P], wr[:, k, :], k == 0, False,
                       xw + bw + [tw])
                last = mm(bank[:, 36 * a:36 * a + 36], r1_, rb, False, True, inc=a == 1)
            t = cp(lg, bank[:, 0:72].rearrange("p (a n) -> p a n", a=2), [last])
            pb.done(bi, t)

            def softmax(out, src, n, w):
                m = ar(2)
                t = red(m, src, MAX, w)
                t = tt(out, src, bc(m, [P, 2, n], 2), SUB, [t])
                t = act(out, out, ACT.Exp, [t])
                t = red(m, out, ADD, [t])
                t = rcp(m, m, [t])
                return tt(out, out, bc(m, [P, 2, n], 2), MUL, [t])

            def first_max(oh, val, src, n, w):
                c = ar(2, n)
                m = ar(2)
                t = red(val, src, MAX, w)
                t = tt(c, src, bc(val, [P, 2, n], 2), ALU.is_equal, [t])
                t = stt(c, c, -64.0, bc(V("iota", 0, n), [P, 2, n], 1), MUL, ADD, [t])
                t = red(m, c, MIN, [t])
                return tt(oh, c, bc(m, [P, 2, n], 2), ALU.is_equal, [t])

            pg, ohg, pgv = ar(2, 4), ar(2, 4), ar(2)
            t = softmax(pg, lg[:, :, 0:4], 4, [t])
            t = first_max(ohg, pgv, pg, 4, [t])
            big = ar(2, 4, 8)
            ein, oh1, oh2, m1, m2 = ar(2, 8), ar(2, 8), ar(2, 8), ar(2), ar(2)
            for a in range(2):
                t = tt(big[:, a], lg[:, a, 4:36].rearrange("p (g e) -> p g e", g=4),
                       bc(ohg[:, a], [P, 4, 8], 2), MUL, [t])
                t = red(ein[:, a, :], big[:, a].rearrange("p g e -> p e g"), ADD, [t])
            t = softmax(ein, ein, 8, [t])
            t = first_max(oh1, m1, ein, 8, [t])
            t = stt(ein, oh1, -2.0, ein, MUL, ADD, [t])
            t = first_max(oh2, m2, ein, 8, [t])
            for a in range(2):
                for c in range(0, KC, 4):
                    bi, bank, bw = pb.next()
                    for j in range(4):
                        last = tr(bank[:, j * P:(j + 1) * P], xt[:, c + j, a * P:(a + 1) * P], xw + bw, inc=j == 3)
                    xnw = cp(xn[:, a, c * P:(c + 4) * P], bank[:, :], [last], k="a")
                    pb.done(bi, xnw)
            r = ar(2)
            t = tt(r, m1, m2, ADD, [t])
            t = rcp(r, r, [t])
            t = tt(r, r, pgv, MUL, [t])
            t = tt(m1, m1, r, MUL, [t])
            t = tt(m2, m2, r, MUL, [t])
            sel8, gat8 = ar(2, 8), ar(2, 8)
            t = tt(sel8, oh1, oh2, ADD, [t])
            t = tt(oh1, oh1, bc(m1, [P, 2, 8], 2), MUL, [t])
            t = tt(oh2, oh2, bc(m2, [P, 2, 8], 2), MUL, [t])
            t = tt(gat8, oh1, oh2, ADD, [t])
            sel, px, gx = ar(2, NE), ar(2, NE + NX), ar(2, NE + NX)
            for a in range(2):
                t = tt(sel[:, a, :].rearrange("p (g e) -> p g e", g=4), bc(ohg[:, a], [P, 4, 8], 2),
                       bc(sel8[:, a], [P, 4, 8], 1), MUL, [t])
                t = tt(gx[:, a, 0:NE].rearrange("p (g e) -> p g e", g=4), bc(ohg[:, a], [P, 4, 8], 2),
                       bc(gat8[:, a], [P, 4, 8], 1), MUL, [t])
            bi, bank, bw = pb.next()
            mm(bank[:, 0:NE], V("tri"), sel[:, 0, :], True, True, [t] + bw)
            mm(bank[:, NE:2 * NE], ones, sel[:, 0, :], True, False)
            mm(bank[:, NE:2 * NE], V("tri"), sel[:, 1, :], False, True)
            mm(bank[:, 2 * NE:3 * NE], ones, sel[:, 0, :], True, False)
            last = mm(bank[:, 2 * NE:3 * NE], ones, sel[:, 1, :], False, True, inc=True)
            pos1, cnt, nb, pre = ar(2, NE), ar(NE), ar(NE), ar(NE)
            t = stt(pos1, bank[:, 0:2 * NE].rearrange("p (a n) -> p a n", a=2), 1.0, sel, ADD, MUL, [last])
            t = cp(cnt, bank[:, 2 * NE:3 * NE], [t])
            pb.done(bi, t)
            t = ts(px[:, :, 0:NE], pos1, -1.0, op0=ADD, w=[t])
            routed = t

            nx_ = dict(ohj=ar(NX, NE), ohk=ar(NX, NE), off=ar(NX), ids=ar(2, NX + 1))

            def further():
                t = routed
                t = ts(nb, cnt, SL + 0.5, op0=ALU.is_gt, w=[t])
                for i in range(2, T // SL):
                    t = stt(nb, cnt, i * SL + 0.5, nb, ALU.is_gt, ADD, [t])
                t = scan(pre, bc(ones[:, 0:1], [P, NE]), nb, 0.0, MUL, ADD, [t])
                ohj, ohk, off, ids = nx_["ohj"], nx_["ohk"], nx_["off"], nx_["ids"]
                jota = bc(V("jota"), [P, NX, NE], 2)
                t = tt(ohk, bc(pre, [P, NX, NE], 1), jota, ALU.is_gt, [t])
                t = tt(pre, pre, nb, SUB, [t])
                t = tt(ohj, bc(pre, [P, NX, NE], 1), jota, ALU.is_le, [t])
                t = tt(ohj, ohj, ohk, MUL, [t])
                t = tt(ohk, ohj, bc(pre, [P, NX, NE], 1), MUL, [t])
                t = red(off, ohk, ADD, [t])
                t = tt(off, V("jota"), off, SUB, [t])
                t = ts(off, off, float(SL), SL + 1.0, MUL, ADD, [t])
                t = tt(ohk, ohj, bc(V("iota", 0, NE), [P, NX, NE], 1), MUL, [t])
                t = red(ids[:, 0, 0:NX], ohk, ADD, [t])
                t = red(ids[:, 1, 0:NX], ohj, ADD, [t])
                t = red(ids[:, 0, NX:], nb, ADD, [t])
                t = red(ids[:, 1, NX:], nb, ADD, [t])
                for a in range(2):
                    t = tt(ohk, ohj, bc(pos1[:, a], [P, NX, NE], 1), MUL, [t])
                    t = red(px[:, a, NE:], ohk, ADD, [t])
                    t = tt(px[:, a, NE:], px[:, a, NE:], off, SUB, [t])
                    t = tt(ohk, ohj, bc(gx[:, a, 0:NE], [P, NX, NE], 1), MUL, [t])
                    t = red(gx[:, a, NE:], ohk, ADD, [t])
                tid = cp(eid[0:1, 0:2 * NX + 2], ids[0:1].rearrange("p a n -> p (a n)"), [t])
                return tid

            hold = back_to(0)
            xg_b = Turns([ar(KC, GB, SL) for _ in range(2)])
            back_to(hold)
            dt_b = Turns([ar(GB, T) for _ in range(2)])
            d_t = ar(2, GB, SL)
            dg_t = ar(2, GB, 4, SL)
            hs_b = Turns([ar(256) for _ in range(2)])
            ht_b = Turns([ar(2, 2, SL) for _ in range(2)])
            y_b = Turns([ar(256) for _ in range(2)])
            NB = NE + NX
            acc = banks[0:4]
            accw = [fill(acc[i][:, :], 0.0, pb.free[i]) for i in range(4)]
            pq = Turns(banks[4:8])
            pq.free = [list(pb.free[i]) for i in range(4, 8)]
            group = {}
            used = {"d": [], "g": []}

            def prepare(q):
                n = min(GB, NB - GB * q)
                dw, gw = [], []
                for a in range(2):
                    t = tt(d_t[:, a, 0:n, :], bc(V("iota", 0, SL), [P, n, SL], 1),
                           bc(px[:, a, GB * q:GB * q + n], [P, n, SL], 2), ALU.is_equal, [routed] + used["d"])
                    dw.append(t)
                for a in range(2):
                    gw.append(tt(dg_t[:, a, 0:n], bc(d_t[:, a, 0:n], [P, n, 4, SL], 2),
                                 bc(gx[:, a, GB * q:GB * q + n], [P, n, 4, SL], 2, 3), MUL, dw + used["g"]))
                xi, xg, xgw = xg_b.next()
                evs = []
                for c in range(0, KC, 2):
                    bi, bank, bw = pq.next()
                    for j in range(2):
                        for a in range(2):
                            last = mm(bank[:, j * T:j * T + n * SL], xn[:, a, (c + j) * P:(c + j + 1) * P],
                                      d_t[:, a, 0:n, :], a == 0, a == 1, dw + bw + [xnw], inc=(j == 1 and a == 1))
                    e = cp(xg[:, c:c + 2, 0:n, :],
                           bank[:, :].rearrange("p (a b s) -> p a b s", a=2, b=GB)[:, :, 0:n, :],
                           [last] + xgw, k="a" if c % 4 else "v")
                    evs.append(e)
                    pq.done(bi, e)
                used["d"] = [last]
                group[q] = [xi, xg, evs, gw]

            def prepare_back(q):
                n = min(GB, NB - GB * q)
                xi, xg, evs, gw = group[q]
                di, dt_, dtw = dt_b.next()
                dte = []
                for b in range(0, n, 2):
                    m = min(2, n - b)
                    bi, bank, bw = pq.next()
                    for j in range(m):
                        for a in range(2):
                            last = tr(bank[:, j * T + a * P:j * T + (a + 1) * P],
                                      dg_t[:, a, b + j].rearrange("p d s -> p (d s)"), gw + bw,
                                      inc=(j == m - 1 and a == 1))
                    e = cp(dt_[:, b:b + m, :], bank[:, 0:m * T].rearrange("p (a t) -> p a t", a=m), [last] + dtw,
                           k="v" if b % 4 else "a")
                    dte.append(e)
                    pq.done(bi, e)
                used["g"] = [last]
                group[q] = (xi, xg, evs, di, dt_, dte)

            info = {}

            def up(b):
                if b < NE:
                    gu = [wload(A["expert_w_gu"][L, b, k * 256:(k + 1) * 256, :], 2, DM) for k in range(4)]
                    dn = [wload(A["expert_w_down"][L, b, k * 256:(k + 1) * 256, :], 2, DM) for k in range(2)]
                xi, xg, evs, *_ = group[b // GB]
                bi, bank, bw = pq.next()
                for k in range(KC):
                    if b >= NE and k % 2 == 0:
                        sl = xload(A["expert_w_gu"][L], b - NE, k * P)
                    elif k % 2 == 0:
                        sl = gu[k // 2]
                    for h in range(4):
                        last = mm(bank[32 * h:32 * h + 32, 0:256], xg[:, k, b % GB, :],
                                  sl[1][:, k % 2, 256 * h:256 * h + 256], k == 0, k == KC - 1,
                                  evs + bw + [sl[2]], inc=(k % 2 == 1 and h == 3), tile=(0, 32 * h))
                    if k % 2 == 1:
                        (wfree if b < NE else xfree)([sl], last)
                xg_b.done(xi, last)
                hi, hs, hw = hs_b.next()
                t = act(hs[0:64, :], bank[0:64, 0:256], ACT.Silu, [last] + hw)
                t = tt(hs[0:64, :], hs[0:64, :], bank[64:128, 0:256], MUL, [t])
                pq.done(bi, t)
                info[b] = dict(dn=dn if b < NE else None, hs=hs, hi=hi, t=t)

            def across(b):
                f = info[b]
                bi, bank, bw = pq.next()
                for k in range(2):
                    last = tr(bank[:, k * 64:(k + 1) * 64], f["hs"][0:64, k * P:(k + 1) * P], [f["t"]] + bw, inc=k == 1)
                hs_b.done(f["hi"], last)
                hi, ht, hw = ht_b.next()
                t = cp(ht, bank[:, 0:128].rearrange("p (k h s) -> p k h s", k=2, h=2), [last] + hw, k="a")
                pq.done(bi, t)
                f.update(ht=ht, hti=hi, t=t)

            def down(b):
                f = info[b]
                bi, bank, bw = pq.next()
                for k in range(4):
                    if b >= NE and k % 2 == 0:
                        sl = xload(A["expert_w_down"][L], b - NE, k * P)
                    elif k % 2 == 0:
                        sl = f["dn"][k // 2]
                    for h in range(4):
                        last = mm(bank[32 * h:32 * h + 32, 0:256], f["ht"][:, k % 2, k // 2, :],
                                  sl[1][:, k % 2, 256 * h:256 * h + 256], k == 0, k == 3,
                                  [f["t"]] + bw + [sl[2]], inc=(k % 2 == 1 and h == 3), tile=(0, 32 * h))
                    if k % 2 == 1:
                        (wfree if b < NE else xfree)([sl], last)
                ht_b.done(f["hti"], last)
                yi, y, yw = y_b.next()
                t = cp(y, bank[:, 0:256], [last] + yw)
                pq.done(bi, t)
                f.update(y=y, yi=yi, t=t)

            def back(b):
                f = info.pop(b)
                _, _, _, di, dt_, dte = group[b // GB]
                for j in range(2):
                    for h in range(4):
                        last = mm(acc[h][:, j * T:(j + 1) * T], f["y"][32 * h:32 * h + 32, j * P:(j + 1) * P],
                                  dt_[32 * h:32 * h + 32, b % GB, :], False, True,
                                  [f["t"]] + dte + accw, inc=(j == 1 and h == 3), tile=(32 * h, 0), skip=True)
                y_b.done(f["yi"], last)
                dt_b.done(di, last)
                return last

            prepare(0)
            for b in range(NE + 2):
                if b < NE:
                    up(b)
                if b == 1:
                    tid = further()
                if b == 0:
                    prepare_back(0)
                if b % GB == 5 and b // GB + 1 < NE // GB:
                    prepare(b // GB + 1)
                    prepare_back(b // GB + 1)
                if 1 <= b <= NE:
                    across(b - 1)
                if b >= 2:
                    last = back(b - 2)
                if 1 <= b <= NE:
                    down(b - 1)
            before = last
            xr_ = {"n": 0, "slots": wt["order"][-3:]}
            xat = list(xcount)

            def xload(src, j, k0):
                c = xr_["n"] % 3
                i = xr_["slots"][c]
                xr_["n"] += 1
                xcount[c] += 1
                dst = slot_at(i, 2, DM)

                def go(e):
                    v, ok = idv[j]
                    s = src[bass.ds(v, 1), k0:k0 + 256, :].rearrange("o (a p) n -> p (o a) n", p=P)
                    return e.dma_start(dst, s, cond=ok)
                tok = E.dma("s", go, x_sem[c], 16 * xcount[c], wt["free"][i])
                wt["free"][i] = []
                return i, dst, tok

            xfree = wfree
            E.branch(eid[0:1, NX:NX + 1], tid)
            E.put("s", load_ids, inc=False)
            for b in range(NE, NB):
                if b % GB == 0:
                    prepare(b // GB)
                    prepare_back(b // GB)
                up(b)
                across(b)
                down(b)
                last = back(b)
            E.join([(x_sem[c], 16 * xat[c], 16 * (xcount[c] - xat[c])) for c in range(3)])
            ends = []
            for i in range(4):
                ends.append(tt(x[:, 2 * i:2 * i + 2, :], acc[i][:, :].rearrange("p (a t) -> p a t", a=2),
                               x[:, 2 * i:2 * i + 2, :], ADD, [before, last]))
            for i in range(4):
                pb.free[i] = [ends[i]]
                pb.free[4 + i] = pq.free[i]

        xcount = [0, 0, 0]
        idv = {}

        def load_ids(e):
            for j in range(NX):
                idv[j] = (e.value_load(eid[0:1, j:j + 1], min_val=0, max_val=NE - 1),
                          e.value_load(eid[0:1, NX + 1 + j:NX + 2 + j], min_val=0, max_val=1))
            return None

        def ret():
            phase(5)
            room("r", 2 * 16 * T + 4 * SLOT)
            gth, gtl = ra(16, T), ra(16, T)
            xh, xl = gth[:, 0:KC, :], gtl[:, 0:KC, :]
            pairs(4)
            room("f")
            W = A["ret_w_in"][0]
            tmp = ar(KC, T)
            rs = ar(T)
            qt, kt = ar(4, 2, T), ar(4, 2, T)
            v = ar(2, 2048)
            gt = ar(16, T)
            X = lambda k: (xh[:, k, :], xl[:, k, :])
            g = V("norm_mix", 8, 8)
            xtok = []
            xw = lambda k: xtok[k]

            def norm(mid):
                xtok.extend(rms_split(x, T, xh, xl, [(0, T, lambda c: g[:, c:c + 1], None)], tmp,
                                      gt[:, 0:KC, :], rs, (), mid))

            qf, kf = qt.rearrange("p h c t -> p (h c) t"), kt.rearrange("p h c t -> p (h c) t")
            t4 = tmp.rearrange("p (a h) t -> p a h t", a=2)
            cosb, sinb = bc(V("cos"), [P, 4, T], 1), bc(V("sin"), [P, 4, T], 1)

            def rotate(m):
                done = [(E.sem["a"], E.n["a"])]
                a, b = m[:, :, 0, :], m[:, :, 1, :]
                t = tt(t4[:, 0], a, sinb, MUL, done)
                t = tt(t4[:, 1], b, sinb, MUL, [t])
                t = tt(a, a, cosb, MUL, [t])
                t = tt(b, b, cosb, MUL, [t])
                t = tt(a, a, t4[:, 1], SUB, [t])
                tt(b, b, t4[:, 0], ADD, [t])

            gemm([gemm_t(W[:, 0:DM], KC, DM, X, T,
                         lambda j, n, ps, t: [cp(qf[:, j:j + n, :], ps, [t], k="a")], xw, after=lambda: rotate(qt)),
                  gemm_t(W[:, DM:2 * DM], KC, DM, X, T,
                         lambda j, n, ps, t: [act(kf[:, j:j + n, :], ps, ACT.Copy, [t], scale=1.0 / 16)], xw,
                         after=lambda: rotate(kt)),
                  gemm_n(W[:, 2 * DM:4 * DM], KC, 2048,
                         lambda k, a: (xh[:, k, a * P:(a + 1) * P], xl[:, k, a * P:(a + 1) * P]), (0, 1),
                         lambda a, o, n, ps, t: [cp(v[:, a, o:o + n], ps, [t], k="a")], xw),
                  gemm_t(W[:, 4 * DM:6 * DM], KC, 2048, X, T,
                         lambda j, n, ps, t: [act(gt[:, j:j + n, :], ps, ACT.Silu, [t])], xw)], norm)
            done = E.barrier()
            rot = None
            dec = V("dec").rearrange("p (h t) -> p h t", h=4)
            sts = Turns([ar(384) for _ in range(2)])
            steps = modulation(1)
            o_b = Turns([tmp[:, 0:4, :], ar(4, T)])
            sq = tmp[:, 4:8, :]
            gn = V("gn")
            info = {}

            def scores(h):
                bi, bank, bw = pb.next()
                for c in range(2):
                    mm(bank[:, 0:T], kt[:, h, c, 0:P], qt[:, h, c, :], c == 0, c == 1, done + bw)
                for c in range(2):
                    last = mm(bank[:, T:T + P], kt[:, h, c, P:T], qt[:, h, c, P:T], c == 0, c == 1, inc=c == 1)
                si, s, sw = sts.next()
                t = tt(s[:, 0:T], bank[:, 0:T], dec[:, h, :], MUL, [last] + sw)
                t = tt(s[:, T:T + P], bank[:, T:T + P], dec[:, h, 0:P], MUL, [t])
                pb.done(bi, t)
                info["s", h] = (si, s, t)

            def values(h):
                si, s, t = info.pop(("s", h))
                oi, o_, ow = o_b.next()
                to = []
                for e in range(0, 4, 2):
                    bi, bank, bw = pb.next()
                    for j in range(2):
                        o = h * 512 + (e + j) * P
                        mm(bank[:, j * T:j * T + P], v[:, 0, o:o + P], s[:, 0:P], True, True, [t] + bw)
                        mm(bank[:, j * T + P:(j + 1) * T], v[:, 0, o:o + P], s[:, P:T], True, False)
                        last = mm(bank[:, j * T + P:(j + 1) * T], v[:, 1, o:o + P], s[:, T:T + P], False, True,
                                  inc=j == 1)
                    to.append(cp(o_[:, e:e + 2, :], bank[:, :].rearrange("p (a t) -> p a t", a=2), [last] + ow, k="a"))
                    pb.done(bi, to[-1])
                sts.done(si, last)
                info["o", h] = (oi, o_, to)

            def centre(h):
                oi, o_, to = info["o", h]
                bi, ps, tok = colsum([o_[:, e, :] for e in range(4)], T, to)
                for e in range(4):
                    t = stt(o_[:, e, :], ps, -1.0 / 512, o_[:, e, :], MUL, ADD, [tok])
                pb.done(bi, t)
                info["q", h] = act(sq, o_, ACT.Square, [t, info.get("sq")])

            def norm(h):
                oi, o_, to = info.pop(("o", h))
                bi, ps, tok = colsum([sq[:, e, :] for e in range(4)], T, [info.pop(("q", h))])
                info["sq"] = tok
                r, ta = rstd_of(rs, ps, 1.0 / 512, [tok])
                pb.done(bi, ta)
                t = tt(o_, o_, bc(rs, [P, 4, T], 1), MUL, [r])
                for e in range(4):
                    j = 4 * h + e
                    t = stt(gt[:, j, :], o_[:, e, :], gn[:, j:j + 1], gt[:, j, :], MUL, MUL, [t])
                o_b.done(oi, t)
                hs = slice(4 * h, 4 * h + 4)
                return split(gt[:, hs, :], gth[:, hs, :], gtl[:, hs, :], [t])

            otok = []
            scores(0)
            values(0)
            for h in range(4):
                if h < 3:
                    scores(h + 1)
                centre(h)
                for _ in range(2):
                    steps.pop(0)()
                if h < 3:
                    values(h + 1)
                otok.append(norm(h))
                steps.pop(0)()
            while steps:
                steps.pop(0)()
            gemm([gemm_t(A["ret_w_out"][0], 16, DM, lambda k: (gth[:, k, :], gtl[:, k, :]), T,
                         lambda j, n, ps, tk: [tt(x[:, j:j + n, :], ps, x[:, j:j + n, :], ADD, [tk])],
                         lambda k: otok[k // 4], block=sum_early(x, T, [tmp[:, 0, :], tmp[:, 1, :]]))])

        def second(L):
            last_layer = L == 1
            lo = T if last_layer else 0
            mod = mods[:, 128 * L:128 * L + 96].rearrange("p (c v) -> p c v", v=2)
            gm = mods[:, 128 * L + 96:128 * L + 128].rearrange("p (i c v) -> p i c v", i=2, c=8)
            t = None
            for i, (nm, sc) in enumerate((("norm1", 8), ("norm2", 32))):
                t = stt(gm[:, i], mod[:, sc:sc + 8, :], 1.0, bc(V(nm, 8 * L, 8), [P, 8, 2], 2), ADD, MUL, [t])
            modw = t
            phase(3)
            room("r", 2 * KC * 2 * T)
            xh, xl = ra(KC, 2 * T), ra(KC, 2 * T)

            def parts(i, sh, lo_):
                out = []
                for v_, a, b in ((0, 0, T), (1, T, 2 * T)):
                    if a >= lo_:
                        out.append((a, b, lambda c, v_=v_: gm[:, i, c, v_:v_ + 1],
                                    lambda c, v_=v_: mod[:, sh + c, v_:v_ + 1]))
                return out

            def residual(g0, lo_):
                def ev(j, n, ps, tk):
                    for i in range(n):
                        for v_, a, b in ((0, 0, T), (1, T, 2 * T)):
                            if a >= lo_:
                                t = stt(xr[:, j + i, a:b], ps[:, i, a - lo_:b - lo_], mod[:, g0 + j + i, v_:v_ + 1],
                                        xr[:, j + i, a:b], MUL, ADD, [tk])
                    return [t]
                return ev

            room("f", F_LONG)
            yt = ar(KC, 2 * T)
            rs = ar(2 * T)
            sq_, tm_ = yt, ar(KC, 2 * T, at=KC * 2 * T + 2 * T)
            xtok = []
            xw = lambda k: xtok[k]

            def norm(mid):
                xtok.extend(rms_split(xr[:, :, :], 2 * T, xh, xl, parts(0, 0, 0), sq_, tm_, rs, [modw], mid))

            W = A["w_in_2"][L]
            X = lambda k: (xh[:, k, :], xl[:, k, :])
            XL = lambda k: (xh[:, k, lo:], xl[:, k, lo:])
            XN = lambda k, a: (xh[:, k, a * P:(a + 1) * P], xl[:, k, a * P:(a + 1) * P])
            nq = 2 * T - lo
            tiles = range(lo // P, 4)
            bcv = V("bc", 4 * L, 4)
            bu = V("bu", 2 * L, 2)
            early = KC * 2 * T + 2 * T
            cva, cvg, ut, sv = ar(2, 2 * T), ar(2, 2 * T), ar(2, 2 * T), ar(4, 256)
            lngb, wst = ar(2, 256), ar(4, P)
            st6, mv, sr = ar(4, 6), ar(4, 2), ar(4)
            qt, kt = ar(4, 2 * T), ar(4, 2 * T)
            vn = ar(4, 4, 129)
            on = ar(4, 512)
            graw = ar(2 * T)
            g_in, g_f = ar(2 * T), ar(2 * T)
            bks = ar(4)
            rows = [ar(2 * T) for _ in range(3)]
            nw = ar(4, 2, P)
            n_rooms = room("r")
            pairs(4)
            jobs = [
                gemm_t(W[:, 2576:2832], KC, 256, XL, nq,
                       lambda j, n, ps, tk: [act(cva[:, j + i, lo:], ps[:, i, :], ACT.Identity, [tk],
                                                 bias=bcv[:, j + i:j + i + 1]) for i in range(n)], xw, wide=256),
                gemm_t(W[:, 2832:3088], KC, 256, XL, nq,
                       lambda j, n, ps, tk: [act(cvg[:, j + i, lo:], ps[:, i, :], ACT.Sigmoid, [tk],
                                                 bias=bcv[:, 2 + j + i:3 + j + i]) for i in range(n)], xw, wide=256,
                       after=lambda: convolve())]
            conv_out = {}

            def convolve():
                after_conv_in = [(E.sem["a"], E.n["a"])]
                cw = V("conv_w", 62 * L, 62).rearrange("p (c k) -> p c k", c=2)
                cb = V("conv_b", 2 * L, 2)
                pads = yt.rearrange("p a t -> p (a t)")
                state = {"t": None}

                def later(f, *a, w=()):
                    def go():
                        state["t"] = f(*a, w=list(w) + [state["t"]])
                        conv_out["t"] = state["t"]
                    side[0].append(go)

                later(fill, pads[:, 0:286 * 2 + 376 + 640], 0.0, w=after_conv_in)
                later(tt, cva[:, :, lo:], cva[:, :, lo:], cvg[:, :, lo:], MUL)
                ct = cvg
                o1 = 572
                px0 = pads[:, o1:o1 + 376].rearrange("p (r c) -> p r c", r=4)
                px1 = pads[:, o1 + 376:o1 + 376 + 640]
                later(cp, px0[:, :, 15:79], cva[:, 0, T:].rearrange("p (r c) -> p r c", r=4))
                later(cp, px1[:, 192:448], cva[:, 1, T:])
                if not last_layer:
                    pc = pads[:, 0:572].rearrange("p (c t) -> p c t", c=2)
                    later(cp, pc[:, :, 15:271], cva[:, :, 0:T])
                    for c in range(2):
                        o = ct[:, c, 0:T]
                        later(ts, o, pc[:, c, 0:T], cw[:, c, 0:1], cb[:, c:c + 1], MUL, ADD)
                        for k in range(1, 31):
                            later(stt, o, pc[:, c, k:k + T], cw[:, c, k:k + 1], o, MUL, ADD)
                o = ct[:, 0, T:].rearrange("p (r c) -> p r c", r=4)
                later(ts, o, px0[:, :, 0:64], cw[:, 0, 0:1], cb[:, 0:1], MUL, ADD)
                for k in range(1, 31):
                    later(stt, o, px0[:, :, k:k + 64], cw[:, 0, k:k + 1], o, MUL, ADD)
                o = ct[:, 1, T:]
                later(ts, o, px1[:, 0:T], cw[:, 1, 12:13], cb[:, 1:2], MUL, ADD)
                for d in range(1, 7):
                    later(stt, o, px1[:, 64 * d:64 * d + T], cw[:, 1, 12 + d:13 + d], o, MUL, ADD)

                v = {}

                def ln1():
                    bi, v["ps"], v["tok"] = colsum([ct[:, c, lo:] for c in range(2)], nq, [conv_out["t"]])
                    for c in range(2):
                        t = stt(ct[:, c, lo:], v["ps"], -1.0 / 256, ct[:, c, lo:], MUL, ADD, [v["tok"]])
                    pb.done(bi, t)
                    v["q"] = act(cva[:, :, lo:], ct[:, :, lo:], ACT.Square, [t])

                def ln2():
                    bi, ps, tok = colsum([cva[:, c, lo:] for c in range(2)], nq, [v["q"]])
                    r, ta = rstd_of(rs[:, lo:], ps, 1.0 / 256, [tok])
                    pb.done(bi, ta)
                    t = tt(ct[:, :, lo:], ct[:, :, lo:], bc(rs[:, lo:], [P, 2, nq], 1), MUL, [r])
                    lg_, lb_ = V("cln_g", 2 * L, 2), V("cln_b", 2 * L, 2)
                    for c in range(2):
                        act(yt[:, 6 + c, lo:], ct[:, c, lo:], ACT.Silu, [t], bias=lb_[:, c:c + 1],
                            scale=lg_[:, c:c + 1])

                side[0].extend([None, None, ln1, None, None, ln2])

            def ln_vectors():
                w = [(E.sem["v"], E.n["v"])]
                return [small(lngb[:, 0, :], A["sgu_ln_g_2"][L:L + 1, :].to_broadcast([P, 256]), w),
                        small(lngb[:, 1, :], A["sgu_ln_b_2"][L:L + 1, :].to_broadcast([P, 256]), w),
                        small(wst, A["sgu_wt"][L])][-1:]

            r0, r1 = lo // P, 4

            def gating():
                v = {}

                def one():
                    for a in tiles:
                        t = put("v", lambda e, o=st6[:, a, :], i=sv[:, a, :]: e.bn_stats(o, i), [sv_done])
                        t = put("v", lambda e, o=mv[:, a, :], i=st6[:, a, :]: e.bn_aggr(o, i), [t])
                    v["r"], _ = rstd_of(sr[:, r0:r1], mv[:, r0:r1, 1], 1.0, [t])

                def two():
                    for a in tiles:
                        t = ts(sv[:, a, :], sv[:, a, :], mv[:, a, 0:1], sr[:, a:a + 1], SUB, MUL, [v["r"]])
                    n_ = r1 - r0
                    t = tt(sv[:, r0:r1, :], sv[:, r0:r1, :], bc(lngb[:, 0, :], [P, n_, 256], 1), MUL, [t] + lnw)
                    v["t"] = tt(sv[:, r0:r1, :], sv[:, r0:r1, :], bc(lngb[:, 1, :], [P, n_, 256], 1), ADD, [t])

                def three():
                    for c in range(2):
                        bi, bank, bw = pb.next()
                        for a in tiles:
                            for g in (2 * c, 2 * c + 1):
                                q0 = 64 * (g % 2)
                                o = bank[q0:q0 + 64, (a - r0) * P:(a - r0 + 1) * P]
                                mm(o, sv[:, a, g * 64:(g + 1) * 64], wst[:, g, :], True, False, [v["t"]] + bw,
                                   tile=(0, q0))
                                last = mm(o, R("sgub")[1][:, 0:64], R("sgub", 512 * L + g * P, P)[0], False, True,
                                          inc=(a == 3 and g % 2 == 1), tile=(96, q0))
                        pb.done(bi, tt(yt[:, 4 + c, lo:], ut[:, c, lo:], bank[:, 0:nq], MUL, [last]))

                sv_done = (E.sem["a"], E.n["a"])
                lnw = ln_vectors()
                side[0][0:0] = [one, None, two, None, None, three]

            tv = fill(vn[:, :, :, 128:129], 1.0, k="g")
            bq, bk = V("bq", 4 * L, 4), V("bk", 4 * L, 4)
            tbk = act(bks, bk, ACT.Copy, scale=128 ** -0.5)
            jobs += [
                gemm_t(W[:, 2064:2320], KC, 256, XL, nq,
                       lambda j, n, ps, tk: [act(ut[:, j + i, lo:], ps[:, i, :], ACT.Gelu_apprx_tanh, [tk],
                                                 bias=bu[:, j + i:j + i + 1]) for i in range(n)], xw, wide=256),
                gemm_n(W[:, 2320:2576], KC, 256, XN, tiles,
                       lambda a, o, n, ps, tk: [act(sv[:, a, :], ps, ACT.Gelu_apprx_tanh, [tk])],
                       xw, bias=R("bs", 256 * L, 256), wide=256, after=lambda: gating()),
                gemm_t(W[:, 0:512], KC, 512, XL, nq,
                       lambda j, n, ps, tk: [act(qt[:, j + i, lo:], ps[:, i, :], ACT.Identity, [tk],
                                                 bias=bq[:, j + i:j + i + 1]) for i in range(n)], xw),
                gemm_t(W[:, 512:1024], KC, 512, X, 512,
                       lambda j, n, ps, tk: [act(kt[:, j, :], ps[:, 0, :], ACT.Identity, [tk, tbk],
                                                 bias=bks[:, j:j + 1], scale=128 ** -0.5)], xw),
                gemm_n(W[:, 1024:1536], KC, 512, XN, range(4),
                       lambda a, o, n, ps, tk: [cp(vn[:, a, :, 0:P], ps.rearrange("p (h d) -> p h d", h=4), [tk, tv],
                                                   k="a")],
                       xw, bias=R("bv", 512 * L, 512)),
                gemm_n(W[:, 1536:2048], KC, 512, XN, tiles,
                       lambda a, o, n, ps, tk: [act(on[:, a, :], ps, ACT.Sigmoid, [tk])],
                       xw, bias=R("bo", 512 * L, 512)),
                ]
            jobs.insert(0, gemm_t(W[:, 2048:2064], KC, 16, X, 512,
                                  lambda j, n, ps, tk: [act(graw[0:16, :], ps[:, 0, :], ACT.Identity, [tk],
                                                            bias=V("bg", L, 1)[0:16, :])], xw, wide=256,
                                  after=lambda: gate_rows()))
            gates = {}
            zero = V("zero")

            def gate_rows():
                t = (E.sem["a"], E.n["a"])
                got = []
                for j in range(4):
                    q0 = 32 * (j // 2)
                    bi, bank, bw = pb.next()
                    last = mm(bank[q0:q0 + 4, :], ident[0:16, 4 * j:4 * j + 4], graw[0:16, :], True, True, [t] + bw,
                              inc=True, tile=(0, q0))
                    got.append(cp((g_f if j % 2 else g_in)[q0:q0 + 4, :], bank[q0:q0 + 4, :], [last], k="a"))
                    pb.done(bi, got[-1])
                chains = []
                for d in range(2):
                    q0 = 32 * d
                    fi, ii = g_f[q0:q0 + 4, :], g_in[q0:q0 + 4, :]
                    B, U, MT = (r_[q0:q0 + 4, :] for r_ in rows)
                    NW = nw[q0:q0 + 4]
                    on4 = ones[q0:q0 + 4, 0:1]
                    state = {"t": got[-1]}
                    chain = []

                    def later(f, *a, state=state, chain=chain, d=d, **kw):
                        def go():
                            state["t"] = f(*a, w=[state["t"]], **kw)
                            gates[d] = state["t"]
                        chain.append(go)

                    later(stt, B, fi, -1.0, fi, MUL, MAX)
                    later(act, B, B, ACT.Exp, scale=-1.0)
                    later(act, B, B, ACT.Ln, bias=on4)
                    later(stt, fi, fi, 0.0, B, MIN, SUB)
                    prev = zero[q0:q0 + 4, 0:1]
                    for a in ((0, 1, 2, 3) if d == 0 else (1, 0, 3, 2)):
                        s0, s1 = a * P, (a + 1) * P
                        if d == 0:
                            view = slice(s0, s1)
                        else:
                            view = slice(s1 - 1, s0 - 1 if s0 else None, -1)
                        le = s1 - 1 if d == 0 else s0
                        later(scan, B[:, view], bc(on4, [4, P]), fi[:, view], 0.0, MUL, ADD)
                        later(tt, U[:, s0:s1], ii[:, s0:s1], B[:, s0:s1], SUB)
                        later(scan, MT[:, view], U[:, view], U[:, view], prev, MAX, MAX)
                        later(ts, NW[:, a, 0, :], MT[:, s0:s1], -1.0)
                        later(ts, NW[:, a, 1, :], MT[:, s0:s1], -1.0, prev, MUL, ADD)
                        later(tt, MT[:, s0:s1], MT[:, s0:s1], B[:, s0:s1], ADD)
                        prev = MT[:, le:le + 1]
                    chains.append(chain)
                for pair in zip(*chains):
                    side[0].extend(pair)

            gemm(jobs, norm)
            ct = cvg
            drain()
            done = E.barrier()
            all_wait(done)
            shut(n_rooms - 1)
            hold = back_to(early)
            cn = ar(2, 4, 129)
            dts = Turns([ar(4, P) for _ in range(2)])
            back_to(hold)
            room("f")
            kn = ar(4, 4, P)
            hn = ar(4, 512)
            for a in range(4):
                bi, bank, bw = pb.next()
                for h in range(4):
                    last = tr(bank[:, h * P:(h + 1) * P], kt[:, h, a * P:(a + 1) * P], done + bw, inc=h == 3)
                knw = cp(kn[:, a], bank[:, :].rearrange("p (h d) -> p h d", h=4), [last], k="a")
                pb.done(bi, knw)

            all_wait(E.barrier())
            ytok = {k: split(yt[:, k, lo:], xh[:, k, lo:], xl[:, k, lo:], done) for k in range(4, KC)}
            emt, ut_ = rs[:, 0:32], rs[:, 32:64]
            U_, MT_ = rows[1], rows[2]
            for d in range(2):
                q0 = 32 * d
                pm, pmb, pmw = pb.next()
                for i, r_ in enumerate((MT_, U_)):
                    for a in range(4):
                        mtw = mm(pmb[:, 16 * i + 4 * a:16 * i + 4 * a + 4], r_[q0:q0 + 4, a * P:(a + 1) * P],
                                 ident[q0:q0 + 4, q0:q0 + 4], True, True, [gates[d]] + pmw, inc=True)
                te = act(emt[:, 16 * d:16 * d + 16], pmb[:, 0:16], ACT.Exp, [mtw], scale=-1.0)
                te = act(ut_[:, 16 * d:16 * d + 16], pmb[:, 16:32], ACT.Copy, [te])
                pb.done(pm, te)
            cnw = fill(cn, 0.0)
            wbs, qss, sts, kss = (Turns([ar(4, P) for _ in range(2)]) for _ in range(4))
            rd = ar(4)
            masks = (V("mask_le"), V("mask_ge"))
            order = []
            for f, b in zip((0, 1, 2, 3), (1, 0, 3, 2)):
                order += [(0, f), (1, b)]
            cnt_ = {"cn": [cnw]}
            written = set()
            pre = {}

            def prelude(i):
                d, a = order[i]
                q0 = 32 * d
                s0, s1 = a * P, (a + 1) * P
                le = P - 1 if d == 0 else 0
                with_out = not (last_layer and a < 2)
                final = a == (3 if d == 0 else 2)
                di, dt_, dw = dts.next()
                wi, wb, ww = wbs.next()
                tds, tws = [], []
                for hp in range(2):
                    bi, bank, bw = pb.next()
                    for j in range(2):
                        h = 2 * hp + j
                        sel = ident[q0:q0 + 4, q0 + h:q0 + h + 1].to_broadcast([4, P])
                        last = mm(bank[:, 256 * j:256 * j + 256], sel, nw[q0:q0 + 4, a].rearrange("p c t -> p (c t)"),
                                  True, True, [gates[d]] + bw, inc=j == 1)
                    bv = bank[:, :].rearrange("p (h c t) -> p h c t", h=2, c=2)
                    tw = act(wb[:, 2 * hp:2 * hp + 2, :], bv[:, :, 1, :], ACT.Exp, [last] + ww)
                    t = tt(dt_[:, 2 * hp:2 * hp + 2, :], bv[:, :, 0, :], bc(masks[d], [P, 2, P], 1), ADD, [last, tw] + dw)
                    pb.done(bi, t, tw)
                    tds.append(t)
                    tws.append(tw)
                for h in range(4):
                    c = 16 * d + 4 * a + h
                    dtw = act(dt_[:, h, :], dt_[:, h, :], ACT.Exp, [tds[h // 2], te], bias=ut_[:, c:c + 1])
                f = dict(di=di, dt=dt_, dtw=dtw, wi=wi, wb=wb, tws=tws, out=with_out, final=final, le=le, used=[])
                if with_out:
                    qi, qs, qw = qss.next()
                    si, st_, sw = sts.next()
                    tqs = tt(qs, qt[:, :, s0:s1], wb, MUL, tws + qw)
                    bi, bank, bw = pb.next()
                    bv = bank[:, :].rearrange("p (h t) -> p h t", h=4)
                    for h in range(4):
                        last = mm(bv[:, h, :], kt[:, h, s0:s1], qt[:, h, s0:s1], True, True, bw, inc=h == 3)
                    tst = tt(st_, bv, dt_, MUL, [last, dtw] + sw)
                    pb.done(bi, tst)
                    f.update(qi=qi, qs=qs, si=si, st=st_, tqs=tqs, tst=tst)
                if not final:
                    ki, ks, kw = kss.next()
                    tks = tt(ks, kn[:, a], bc(dt_[:, :, le], [P, 4, P], 2), MUL, [dtw, knw] + kw)
                    f.update(ki=ki, ks=ks, tks=tks)
                dts.done(di, (E.sem["v"], E.n["v"]))
                pre[i] = f

            def body(i):
                d, a = order[i]
                f = pre.pop(i)
                wb, le = f["wb"], f["le"]
                read = None
                tcn = f.get("tqs")
                if f["out"]:
                    for hp in range(2):
                        bi, bank, bw = pb.next()
                        pv = bank[:, 0:258].rearrange("p (h n) -> p h n", h=2)
                        for j in range(2):
                            h = 2 * hp + j
                            mm(pv[:, j, :], f["st"][:, h, :], vn[:, a, h, :], True, False,
                               [f["tst"], f["tqs"]] + bw + cnt_["cn"])
                            last = mm(pv[:, j, :], f["qs"][:, h, :], cn[:, d, h, :], False, True, inc=j == 1)
                        t = cp(rd[:, 2:4], pv[:, :, 128], [last, te])
                        em = emt[:, 16 * d + 4 * a + 2 * hp:16 * d + 4 * a + 2 * hp + 2]
                        t = stt(rd[:, 0:2], rd[:, 2:4], -1.0, em, MUL, MAX, [t])
                        t = tt(rd[:, 0:2], rd[:, 0:2], rd[:, 2:4], MAX, [t])
                        t = rcp(rd[:, 0:2], rd[:, 0:2], [t])
                        for j in range(2):
                            h = 2 * hp + j
                            o = hn[:, a, h * P:(h + 1) * P]
                            if a in written:
                                t = stt(o, pv[:, j, 0:P], rd[:, j:j + 1], o, MUL, ADD, [t])
                            else:
                                t = ts(o, pv[:, j, 0:P], rd[:, j:j + 1], w=[t])
                        pb.done(bi, t)
                    written.add(a)
                    qss.done(f["qi"], last)
                    sts.done(f["si"], last)
                    read = last
                if not f["final"]:
                    for hp in range(2):
                        bi, bank, bw = pb.next()
                        pv = bank[:, 0:258].rearrange("p (h n) -> p h n", h=2)
                        for j in range(2):
                            h = 2 * hp + j
                            last = mm(pv[:, j, :], f["ks"][:, h, :], vn[:, a, h, :], True, True, [f["tks"]] + bw, inc=j == 1)
                        for j in range(2):
                            h = 2 * hp + j
                            tcn = stt(cn[:, d, h, :], cn[:, d, h, :], wb[:, h, le:le + 1], pv[:, j, :], MUL, ADD,
                                      [last, read] + f["tws"])
                        pb.done(bi, tcn)
                    kss.done(f["ki"], last)
                    cnt_["cn"] = [tcn]
                wbs.done(f["wi"], tcn)

            for i in range(len(order) + 1):
                if i < len(order):
                    prelude(i)
                if i:
                    body(i - 1)
            mg = V("mlstm_g", 4 * L, 4)
            ss = emt[:, 0:4 * len(tiles)]
            t_hn = (E.sem["v"], E.n["v"])
            sq4 = {a: (qss.items + sts.items)[a] for a in tiles}
            for i, a in enumerate(tiles):
                h4 = hn[:, a, :].rearrange("p (h d) -> p h d", h=4)
                if i % 2:
                    t = tt(sq4[a], h4, h4, MUL, [t_hn])
                else:
                    t = act(sq4[a], h4, ACT.Square, [t_hn])
                t = red(ss[:, 4 * i:4 * i + 4], sq4[a], ADD, [t])
            r, _ = rstd_of(ss, ss, 1.0 / P, [t])
            for i, a in enumerate(tiles):
                h4 = hn[:, a, :].rearrange("p (h d) -> p h d", h=4)
                t = tt(h4, h4, bc(ss[:, 4 * i:4 * i + 4], [P, 4, P], 2), MUL, [r])
                t = tt(hn[:, a, :], hn[:, a, :], on[:, a, :], MUL, [t])
                bi, bank, bw = pb.next()
                for h in range(4):
                    last = tr(bank[:, h * P:(h + 1) * P], hn[:, a, h * P:(h + 1) * P], [t] + bw, inc=h == 3)
                for h in range(4):
                    t = act(yt[:, h, a * P:(a + 1) * P], bank[:, h * P:(h + 1) * P], ACT.Copy, [last],
                            scale=mg[:, h:h + 1])
                pb.done(bi, t)
            all_wait([t, last])
            shut(n_rooms - 1)
            room("r")
            pairs(4)
            ytok.update({k: split(yt[:, k, lo:], xh[:, k, lo:], xl[:, k, lo:], [t]) for k in range(4)})
            gemm([gemm_t(A["w_out_2"][L], KC, DM, XL, nq, residual(16, lo), lambda k: ytok[k],
                         block=sum_early(xr[:, :, lo:], nq, [cva[:, 0, lo:], cva[:, 1, lo:]]))])

            phase(5 if last_layer else 3)
            room("r", 2 * KC * nq + 3 * SLOT)
            xh, xl = ra(KC, nq), ra(KC, nq)
            pairs(3)
            room("f", 3 * nq)
            rs = ar(nq)
            sg = Turns([ar(nq) for _ in range(2)])
            n_rooms = room("f")
            sq_, tm_ = ar(KC, nq), ar(KC, nq)
            ps_ = [(a - lo, b - lo, m, s) for a, b, m, s in parts(1, 24, lo)]
            shut(n_rooms - 1)
            room("r")
            hh, hl = ra(22, nq), ra(22, nq)
            xtok = []
            xw = lambda k: xtok[k]

            def norm(mid):
                xtok.extend(rms_split(xr[:, :, lo:], nq, xh, xl, ps_, sq_, tm_, rs, [], mid))

            XF = lambda k: (xh[:, k, :], xl[:, k, :])
            jobs = []
            pend = {}

            def ev_gate(j, n, ps, tk):
                si, s, sw = sg.next()
                t = act(s, ps[:, 0, :], ACT.Silu, [tk] + sw)
                pend[j] = (si, s, t)
                return [t]

            def ev_up(j, n, ps, tk):
                si, s, t = pend.pop(j)
                t = tt(s, s, ps[:, 0, :], MUL, [t, tk])
                done = split(s, hh[:, j, :], hl[:, j, :], [t])
                sg.done(si, *done)
                return [t]

            for o in range(0, FF2, 256):
                jobs += [gemm_t(A["w_gu_2"][L][:, o:o + 256], KC, 256, XF, nq,
                                lambda j, n, ps, tk, o=o: ev_gate(o // P + j, n, ps, tk), xw, wide=256),
                         gemm_t(A["w_gu_2"][L][:, FF2 + o:FF2 + o + 256], KC, 256, XF, nq,
                                lambda j, n, ps, tk, o=o: ev_up(o // P + j, n, ps, tk), xw, wide=256)]
            gemm(jobs, norm)
            gemm([gemm_t(A["w_down_2"][L], 22, DM, lambda k: (hh[:, k, :], hl[:, k, :]), nq, residual(40, lo),
                         [(E.sem["v"], E.n["v"])], block=sum_early(xr[:, :, lo:], nq, sg.items))])

        def final_():
            phase(9)
            room("f")
            xt = ar(KC, T)
            tmp = ar(KC, T)
            rs = ar(T)
            res = ar(2, DM)
            g = V("final")
            xw = rms_t(x, T, xt, lambda c: g[:, c:c + 1], tmp, rs, ())[-1]
            put_out(xt, res, xw)

        def put_out(xt, res, xw):
            for a in range(2):
                for c in range(0, KC, 4):
                    bi, bank, bw = pb.next()
                    for j in range(4):
                        last = tr(bank[:, j * P:(j + 1) * P], xt[:, c + j, a * P:(a + 1) * P], list(xw) + bw, inc=j == 3)
                    t = cp(res[:, a, c * P:(c + 4) * P], bank[:, :], [last], k="v")
                    pb.done(bi, t)
            E.dma("s", lambda e: e.dma_start(A["out"][0].rearrange("(a p) d -> p a d", p=P), res), s_out, 16, [t])
            E.q["s"].append(([(s_out, 16)], lambda e: None, None))

        def norm_x():
            phase(9)
            room("f")
            tmp = ar(KC, T)
            rs = ar(T)
            g = V("norm_final")
            rms_t(x, T, x, lambda c: g[:, c:c + 1], tmp, rs, ())

        steps = [("fox", fox), ("moe0", lambda: moe(0)), ("ret", ret), ("moe1", lambda: moe(1)),
                 ("norm", norm_x), ("sec0", lambda: second(0)), ("sec1", lambda: second(1))]
        for name, f in steps:
            f()
            if stop == name:
                break
        if stop is None:
            final_()
        else:
            phase(9)
            room("f")
            put_out(x, ar(2, DM), E.barrier())
        tail = [(ring_sem[i], 16 * wt["count"][i]) for i in range(NSLOT) if wt["count"][i]]
        tail += [(s_small, nsm[0]), (s_x, 32)]
        E.q["s"].append((tail, lambda e: None, None))
        shut()
        block = ctx.enter_context(nc.Block())
        E.run(block)


def consts():
    f = np.float32
    p = np.arange(P)
    inv = (f(1.0) / (f(10000.0) ** np.linspace(0.0, 1.0, 128, dtype=f))).astype(f)
    ang = (np.arange(T, dtype=f)[:, None] * inv[None, :]).astype(f)
    lg = np.log(1.0 - 2.0 ** (-5.0 - np.arange(4, dtype=np.float64)))
    rel = np.arange(T)[None, :] - p[:, None]
    dec = np.where(rel[:, None, :] >= 0, np.exp(lg[None, :, None] * np.maximum(rel, 0)[:, None, :]), 0.0)
    d = {
        "cos": np.cos(ang).T, "sin": np.sin(ang).T, "dec": dec.reshape(P, 1024), "ident": np.eye(P),
        "mask_z": np.zeros((P, P)), "mask_ge": np.where(p[None, :] > p[:, None], NEG, 0.0), "mask_le": np.where(p[None, :] < p[:, None], NEG, 0.0),
        "tri": (p[:, None] < p[None, :]), "ones": np.ones((P, P)), "iota": np.tile(np.arange(64), (P, 1)),
        "zero": np.zeros((P, 64)), "eps": np.full((P, 1), EPS), "jota": np.tile(np.arange(NX), (P, 1)),
    }
    return {k: np.asarray(v, f) for k, v in d.items()}


def layout(a):
    f = np.float32
    v = np.zeros((P, NVEC), f)

    def cols(name, x):
        o, w = VEC[name]
        v[:, o:o + w] = x.reshape(w, P).T

    cols("norm_mix", a["norm_mix"])
    cols("norm_ffn", a["norm_ffn"])
    cols("norm_final", a["norm_final"])
    cols("gn", a["ret_gn_gain"])
    cols("norm1", a["norm1_g_2"])
    cols("norm2", a["norm2_g_2"])
    cols("final", a["final_g_2"])
    cols("b_mod", a["b_mod_2"])
    cols("mlstm_g", a["mlstm_g_2"])
    cols("cln_g", a["conv_ln_g_2"])
    cols("cln_b", a["conv_ln_b_2"])
    cols("conv_b", a["conv_b_2"])
    cols("c", a["c_2"])
    cols("cc", a["c_ctx_2"])
    b = a["b_in_2"]
    cols("bq", b[:, 0:512])
    cols("bk", b[:, 512:1024])
    cols("bu", b[:, 2064:2320])
    cols("bc", b[:, 2576:3088])
    o, w = VEC["conv_w"]
    v[:, o:o + w] = a["conv_w_2"].reshape(2, 31, 2, P).transpose(3, 0, 2, 1).reshape(P, 124)
    o, _ = VEC["bg"]
    v[0:16, o:o + 2] = b[:, 2048:2064].T
    o, _ = VEC["bf"]
    v[0:16, o] = v[64:80, o] = a["fox_b_f"][0]
    for k, x in consts().items():
        o, w = VEC[k]
        v[:, o:o + w] = x
    r = np.zeros((P, NROW), f)

    def put(name, x):
        q, o, w = ROW[name]
        r[q, o:o + w] = x.reshape(-1)

    put("br", np.concatenate([a["router_group_b"], a["router_expert_b"]], 1))
    put("bv", b[:, 1024:1536])
    put("bo", b[:, 1536:2048])
    put("bs", b[:, 2320:2576])
    put("sgub", a["sgu_b_2"])
    wr = np.concatenate([a["router_group_w"], a["router_expert_w"]], 2)
    out = {k: a[k] for k in BIG}
    out["vec"], out["row"] = v, r
    out["wr"] = np.ascontiguousarray(wr.reshape(2, KC, P, 36).transpose(0, 2, 1, 3))
    out["sgu_wt"] = np.ascontiguousarray(a["sgu_w_2"].transpose(0, 3, 1, 2))
    return out


BIG = ["x", "ctx_2", "fox_w_in", "fox_w_out", "ret_w_in", "ret_w_out", "expert_w_gu", "expert_w_down",
       "w_mod_2", "w_in_2", "w_out_2", "w_gu_2", "w_down_2", "sgu_ln_g_2", "sgu_ln_b_2"]


def kernel(**inputs):
    import numpy as _np
    import concourse.bacc as _bacc
    from concourse import mybir as _mybir
    from concourse.bass_utils import run_bass_kernel_spmd as _run

    arrays = {k: _np.ascontiguousarray(v) for k, v in layout({k: _np.asarray(v) for k, v in inputs.items()}).items()}
    nc = _bacc.Bacc("TRN2", target_bir_lowering=False, num_devices=1)
    aps = {k: nc.dram_tensor(f"in_{k}", v.shape, _mybir.dt.from_np(v.dtype), kind="ExternalInput").ap()
           for k, v in arrays.items()}
    aps["out"] = nc.dram_tensor("out_0", (1, T, DM), _mybir.dt.float32, kind="ExternalOutput").ap()
    build(nc, aps)
    r = _run(nc, [{f"in_{k}": v for k, v in arrays.items()}], core_ids=[0])
    return r.results[0]["out_0"]
```
